# Optimizing a Trainium2 kernel written in Bass

```python
import math
import jax, jax.numpy as jnp
from jax import lax
import numpy as np

D_MODEL = 1024
BATCH = 1
SEQ = 256
DEPTH = 1

N_MIXERS = 2
N_ATTN_LAYERS = (DEPTH + N_MIXERS - 1) // N_MIXERS
N_FOURIER_LAYERS = DEPTH // N_MIXERS
N_DIFF_HEADS = 8
DIFF_HEAD_DIM = D_MODEL // N_DIFF_HEADS // 2
DIFF_V_DIM = 2 * DIFF_HEAD_DIM
Q_BLOCK = 128
N_FOURIER_GROUPS = 4
FOURIER_GROUP_DIM = D_MODEL // N_FOURIER_GROUPS
N_EXPERT_GROUPS = 4
EXPERTS_PER_GROUP = 4
N_EXPERTS = N_EXPERT_GROUPS * EXPERTS_PER_GROUP
EXPERT_TOP_K = 2
D_EXPERT = D_MODEL // 2
N_ADA = 6
ADA_INIT_SCALE = 0.5
EPS = 1e-6


def rmsnorm(x, g):
    xf = x.astype(jnp.float32)
    y = xf * lax.rsqrt(jnp.mean(xf * xf, axis=-1, keepdims=True) + EPS)
    return (y * g.astype(jnp.float32)).astype(x.dtype)

def modulate(h, shift, scale):
    return h * (1.0 + scale[:, None, :]) + shift[:, None, :]

def alibi_slopes(n_heads):
    return 2.0 ** (-8.0 * jnp.arange(1, n_heads + 1, dtype=jnp.float32) / n_heads)

def diff_attention(h, w_in, lam_q1, lam_k1, lam_q2, lam_k2, subln_g, w_out, layer_idx):
    B, S, D = h.shape
    H, dh, dv = N_DIFF_HEADS, DIFF_HEAD_DIM, DIFF_V_DIM
    qkv = h @ w_in
    q, k, v = jnp.split(qkv, 3, axis=-1)
    q = q.reshape(B, S, H, 2, dh) * (dh ** -0.5)
    k = k.reshape(B, S, H, 2, dh)
    v = v.reshape(B, S, H, dv)
    q1, q2 = q[..., 0, :], q[..., 1, :]
    k1, k2 = k[..., 0, :], k[..., 1, :]
    lam_init = 0.8 - 0.6 * math.exp(-0.3 * layer_idx)
    lam = (jnp.exp(jnp.sum(lam_q1.astype(jnp.float32) * lam_k1.astype(jnp.float32)))
           - jnp.exp(jnp.sum(lam_q2.astype(jnp.float32) * lam_k2.astype(jnp.float32)))
           + lam_init)
    slopes = alibi_slopes(H)
    pos = jnp.arange(S, dtype=jnp.float32)
    nb = S // Q_BLOCK
    q1b = q1.reshape(B, nb, Q_BLOCK, H, dh).transpose(1, 0, 3, 2, 4)
    q2b = q2.reshape(B, nb, Q_BLOCK, H, dh).transpose(1, 0, 3, 2, 4)
    posb = pos.reshape(nb, Q_BLOCK)

    def block(args):
        qa, qb, pq = args
        bias = -slopes[:, None, None] * jnp.abs(pq[:, None] - pos[None, :])
        s1 = jnp.einsum('bhqd,bkhd->bhqk', qa, k1, preferred_element_type=jnp.float32) + bias
        s2 = jnp.einsum('bhqd,bkhd->bhqk', qb, k2, preferred_element_type=jnp.float32) + bias
        a = jax.nn.softmax(s1, axis=-1) - lam * jax.nn.softmax(s2, axis=-1)
        return jnp.einsum('bhqk,bkhd->bqhd', a.astype(v.dtype), v)

    o = lax.map(block, (q1b, q2b, posb))
    o = o.transpose(1, 0, 2, 3, 4).reshape(B, S, H, dv)
    o = rmsnorm(o, subln_g) * (1.0 - lam_init)
    return o.reshape(B, S, H * dv) @ w_out

def fourier_mix(h, w_in, w_out):
    B, S, D = h.shape
    u = (h @ w_in).reshape(B, S, N_FOURIER_GROUPS, FOURIER_GROUP_DIM).astype(jnp.float32)
    f = jnp.fft.fft2(u, axes=(1, 3), norm="ortho").real
    return f.reshape(B, S, D).astype(h.dtype) @ w_out

def hier_moe(h, w_rg, b_rg, w_re, b_re, w_gate, w_up, w_down):
    B, S, D = h.shape
    t = h.reshape(B * S, D)
    T = t.shape[0]
    g_logits = (t @ w_rg).astype(jnp.float32) + b_rg.astype(jnp.float32)
    g_prob = jax.nn.softmax(g_logits, axis=-1)
    g_idx = jnp.argmax(g_logits, axis=-1)
    g_w = jnp.take_along_axis(g_prob, g_idx[:, None], axis=-1)
    e_logits = jnp.einsum('td,dge->tge', t, w_re).astype(jnp.float32) + b_re.astype(jnp.float32)
    e_sel = jnp.take_along_axis(e_logits, g_idx[:, None, None], axis=1)[:, 0]
    top_v, top_i = lax.top_k(e_sel, EXPERT_TOP_K)
    top_w = jax.nn.softmax(top_v, axis=-1)
    e_w = jnp.sum(jax.nn.one_hot(top_i, EXPERTS_PER_GROUP, dtype=jnp.float32) * top_w[..., None], axis=1)
    gates = (jax.nn.one_hot(g_idx, N_EXPERT_GROUPS, dtype=jnp.float32)[:, :, None]
             * (g_w[:, :, None] * e_w[:, None, :])).reshape(T, N_EXPERTS)
    hid = jax.nn.silu(jnp.einsum('td,edf->tef', t, w_gate)) * jnp.einsum('td,edf->tef', t, w_up)
    hid = hid * gates.astype(hid.dtype)[:, :, None]
    y = jnp.einsum('tef,efd->td', hid, w_down)
    return y.reshape(B, S, D)

def first_inputs(seed: int = 0) -> dict:
    key = jax.random.key(seed)
    ks = jax.random.split(key, 24)
    D = D_MODEL

    def nrm(k, shape, scale):
        return jax.random.normal(k, shape, jnp.float32) * scale

    return {
        "x": nrm(ks[0], (BATCH, SEQ, D), 1.0),
        "c": nrm(ks[1], (BATCH, D), 1.0),
        "ada_w": nrm(ks[2], (DEPTH, D, N_ADA * D), ADA_INIT_SCALE * D ** -0.5),
        "ada_b": nrm(ks[3], (DEPTH, N_ADA * D), 0.02),
        "norm_mix": 1.0 + nrm(ks[4], (DEPTH, D), 0.02),
        "norm_ffn": 1.0 + nrm(ks[5], (DEPTH, D), 0.02),
        "attn_w_in": nrm(ks[6], (N_ATTN_LAYERS, D, 3 * D), D ** -0.5),
        "attn_lam_q1": nrm(ks[7], (N_ATTN_LAYERS, DIFF_HEAD_DIM), 0.1),
        "attn_lam_k1": nrm(ks[8], (N_ATTN_LAYERS, DIFF_HEAD_DIM), 0.1),
        "attn_lam_q2": nrm(ks[9], (N_ATTN_LAYERS, DIFF_HEAD_DIM), 0.1),
        "attn_lam_k2": nrm(ks[10], (N_ATTN_LAYERS, DIFF_HEAD_DIM), 0.1),
        "attn_subln": 1.0 + nrm(ks[11], (N_ATTN_LAYERS, DIFF_V_DIM), 0.02),
        "attn_w_out": nrm(ks[12], (N_ATTN_LAYERS, N_DIFF_HEADS * DIFF_V_DIM, D), (N_DIFF_HEADS * DIFF_V_DIM) ** -0.5),
        "fourier_w_in": nrm(ks[13], (N_FOURIER_LAYERS, D, D), D ** -0.5),
        "fourier_w_out": nrm(ks[14], (N_FOURIER_LAYERS, D, D), D ** -0.5),
        "router_group_w": nrm(ks[15], (DEPTH, D, N_EXPERT_GROUPS), D ** -0.5),
        "router_group_b": nrm(ks[16], (DEPTH, N_EXPERT_GROUPS), 0.01),
        "router_expert_w": nrm(ks[17], (DEPTH, D, N_EXPERT_GROUPS, EXPERTS_PER_GROUP), D ** -0.5),
        "router_expert_b": nrm(ks[18], (DEPTH, N_EXPERT_GROUPS, EXPERTS_PER_GROUP), 0.01),
        "expert_w_gate": nrm(ks[19], (DEPTH, N_EXPERTS, D, D_EXPERT), D ** -0.5),
        "expert_w_up": nrm(ks[20], (DEPTH, N_EXPERTS, D, D_EXPERT), D ** -0.5),
        "expert_w_down": nrm(ks[21], (DEPTH, N_EXPERTS, D_EXPERT, D), D_EXPERT ** -0.5),
        "norm_final": 1.0 + nrm(ks[22], (D,), 0.02),
    }

def first_block(x, c, ada_w, ada_b, norm_mix, norm_ffn, attn_w_in, attn_lam_q1, attn_lam_k1,
              attn_lam_q2, attn_lam_k2, attn_subln, attn_w_out, fourier_w_in, fourier_w_out,
              router_group_w, router_group_b, router_expert_w, router_expert_b,
              expert_w_gate, expert_w_up, expert_w_down, norm_final):
    cond = jax.nn.silu(c)
    for i in range(DEPTH):
        mod = cond @ ada_w[i] + ada_b[i]
        sh1, sc1, g1, sh2, sc2, g2 = jnp.split(mod, N_ADA, axis=-1)
        h = modulate(rmsnorm(x, norm_mix[i]), sh1, sc1)
        j = i // N_MIXERS
        if i % N_MIXERS == 0:
            y = diff_attention(h, attn_w_in[j], attn_lam_q1[j], attn_lam_k1[j], attn_lam_q2[j],
                               attn_lam_k2[j], attn_subln[j], attn_w_out[j], i)
        else:
            y = fourier_mix(h, fourier_w_in[j], fourier_w_out[j])
        x = x + g1[:, None, :] * y
        h = modulate(rmsnorm(x, norm_ffn[i]), sh2, sc2)
        y = hier_moe(h, router_group_w[i], router_group_b[i], router_expert_w[i], router_expert_b[i],
                     expert_w_gate[i], expert_w_up[i], expert_w_down[i])
        x = x + g2[:, None, :] * y
    return rmsnorm(x, norm_final)


N_ATTN_HEADS = 8
ATTN_HEAD_DIM = 64
KV_LATENT = 256
N_IDX_HEADS = 8
IDX_HEAD_DIM = 32
TOPK_MAX = 256
N_RWKV_HEADS = 8
RWKV_HEAD_DIM = 64
DECAY_LORA = 64
AAA_LORA = 64
GATE_LORA = 160
N_GROUPS = 4
EXPERTS_PER_GROUP_2 = 8
N_EXPERTS_2 = N_GROUPS * EXPERTS_PER_GROUP_2
D_EXPERT_2 = 512
TOP_K_EXPERTS = 2
NORM_EPS = 1e-6
GN_EPS = 64e-5
ATTN_W = N_ATTN_HEADS * ATTN_HEAD_DIM
RWKV_W = N_RWKV_HEADS * RWKV_HEAD_DIM
IDX_Q_W = N_IDX_HEADS * IDX_HEAD_DIM
SHIFT_W = 3 * RWKV_W + DECAY_LORA + AAA_LORA + GATE_LORA
IN_SPLITS = (ATTN_W, KV_LATENT, IDX_Q_W, IDX_HEAD_DIM, N_IDX_HEADS, SHIFT_W, D_MODEL, D_MODEL)
IN_W = ATTN_W + KV_LATENT + IDX_Q_W + IDX_HEAD_DIM + N_IDX_HEADS + SHIFT_W + 2 * D_MODEL


def _split(x, sizes):
    idx = np.cumsum(sizes)[:-1].tolist()
    return jnp.split(x, idx, axis=-1)

def _rmsnorm(x, g):
    xf = x.astype(jnp.float32)
    y = xf * lax.rsqrt(jnp.mean(xf * xf, axis=-1, keepdims=True) + NORM_EPS)
    return (y * g.astype(jnp.float32)).astype(x.dtype)

def _dsa_attention(q, k, v, q_idx, k_idx, w_idx):
    B, S = q.shape[0], q.shape[1]
    top_k = min(TOPK_MAX, S // 4)
    nb = S // Q_BLOCK
    f32 = jnp.float32
    slopes = 2.0 ** (-8.0 * jnp.arange(1, N_ATTN_HEADS + 1, dtype=f32) / N_ATTN_HEADS)
    key_pos = jnp.arange(S)
    k_idx_f = k_idx.astype(f32)
    idx_scale = (IDX_HEAD_DIM ** -0.5) * (N_IDX_HEADS ** -0.5)

    def blocks(a):
        return jnp.moveaxis(a.reshape((B, nb, Q_BLOCK) + a.shape[2:]), 1, 0)

    def one_block(args):
        qb, qib, wib, start = args
        t = start + jnp.arange(Q_BLOCK)
        dots = jnp.einsum('bthd,bsd->bths', qib.astype(f32), k_idx_f)
        score = jnp.einsum('bths,bth->bts', jax.nn.relu(dots), wib.astype(f32)) * idx_scale
        causal = key_pos[None, :] <= t[:, None]
        score = jnp.where(causal[None], score, -jnp.inf)
        _, sel = lax.top_k(score, top_k)
        k_sel = jax.vmap(lambda kb, ib: kb[ib])(k, sel)
        v_sel = jax.vmap(lambda vb, ib: vb[ib])(v, sel)
        logits = jnp.einsum('bthd,btkhd->bthk', qb.astype(f32), k_sel.astype(f32)) * (ATTN_HEAD_DIM ** -0.5)
        dist = (t[None, :, None] - sel).astype(f32)
        logits = logits - slopes[None, None, :, None] * dist[:, :, None, :]
        valid = sel <= t[None, :, None]
        logits = jnp.where(valid[:, :, None, :], logits, -jnp.inf)
        p = jax.nn.softmax(logits, axis=-1)
        o = jnp.einsum('bthk,btkhd->bthd', p, v_sel.astype(f32))
        return o.astype(q.dtype)

    starts = jnp.arange(nb) * Q_BLOCK
    out = lax.map(one_block, (blocks(q), blocks(q_idx), blocks(w_idx), starts))
    return jnp.moveaxis(out, 0, 1).reshape(B, S, ATTN_W)

def _rwkv7_time_mix(p_shift, mu, w0, w2, a0, a2, g2, k_k, k_a, r_k, ln_w, ln_b):
    B, S = p_shift.shape[0], p_shift.shape[1]
    H, N = N_RWKV_HEADS, RWKV_HEAD_DIM
    f32 = jnp.float32
    prev = jnp.pad(p_shift[:, :-1], ((0, 0), (1, 0), (0, 0)))
    mixed = p_shift + (prev - p_shift) * mu
    r, k, v, wl, al, gl = _split(mixed, (RWKV_W, RWKV_W, RWKV_W, DECAY_LORA, AAA_LORA, GATE_LORA))
    w = -jax.nn.softplus(-(w0 + jnp.tanh(wl) @ w2)) - 0.5
    decay = jnp.exp(-jnp.exp(w.astype(f32)))
    a = jax.nn.sigmoid(a0 + al @ a2)
    g = jax.nn.sigmoid(gl) @ g2
    heads = lambda z: z.reshape(B, S, H, N).astype(f32)
    kk = heads(k * k_k)
    kk = kk / jnp.maximum(jnp.sqrt(jnp.sum(kk * kk, axis=-1, keepdims=True)), 1e-12)
    k = k * (1.0 + (a - 1.0) * k_a)
    r_h, k_h, v_h, a_h, d_h = heads(r), heads(k), heads(v), heads(a), heads(decay)

    def step(state, inp):
        r_t, d_t, k_t, v_t, kk_t, b_t = inp
        sa = jnp.einsum('bhij,bhj->bhi', state, -kk_t)
        state = state * d_t[:, :, None, :] + sa[..., None] * b_t[:, :, None, :] + v_t[..., None] * k_t[:, :, None, :]
        y = jnp.einsum('bhij,bhj->bhi', state, r_t)
        return state, y

    xs = tuple(jnp.moveaxis(z, 1, 0) for z in (r_h, d_h, k_h, v_h, kk, kk * a_h))
    _, y = lax.scan(step, jnp.zeros((B, H, N, N), f32), xs)
    y = jnp.moveaxis(y, 0, 1)
    mean = jnp.mean(y, axis=-1, keepdims=True)
    var = jnp.mean(jnp.square(y - mean), axis=-1, keepdims=True)
    y = ((y - mean) * lax.rsqrt(var + GN_EPS)).reshape(B, S, RWKV_W) * ln_w + ln_b
    bonus = (jnp.sum(r_h * k_h * r_k, axis=-1, keepdims=True) * v_h).reshape(B, S, RWKV_W)
    return ((y + bonus) * g).astype(p_shift.dtype)

def _hier_moe(xt, wg_router, we_router, e_bias, w_gate, w_up, w_down):
    T, D = xt.shape
    f32 = jnp.float32
    p_group = jax.nn.softmax((xt @ wg_router).astype(f32), axis=-1)
    g_sel = jnp.argmax(p_group, axis=-1)
    p_gsel = jnp.max(p_group, axis=-1)
    e_logits = (xt @ we_router).astype(f32).reshape(T, N_GROUPS, EXPERTS_PER_GROUP_2) + e_bias.astype(f32).reshape(N_GROUPS, EXPERTS_PER_GROUP_2)
    e_in = jnp.take_along_axis(e_logits, g_sel[:, None, None], axis=1)[:, 0]
    top_v, top_i = lax.top_k(e_in, TOP_K_EXPERTS)
    w_top = jax.nn.softmax(top_v, axis=-1) * p_gsel[:, None]
    expert_id = g_sel[:, None] * EXPERTS_PER_GROUP_2 + top_i
    combine = jnp.sum(jax.nn.one_hot(expert_id, N_EXPERTS_2, dtype=f32) * w_top[..., None], axis=1)

    def body(acc, ew):
        wg, wu, wd, cw = ew
        hdn = jax.nn.silu(xt @ wg) * (xt @ wu)
        return acc + cw[:, None] * (hdn @ wd).astype(f32), None

    acc, _ = lax.scan(body, jnp.zeros((T, D), f32), (w_gate, w_up, w_down, combine.T))
    return acc.astype(xt.dtype)

def second_inputs(seed: int = 0) -> dict:
    key = jax.random.key(seed)
    ks = iter(jax.random.split(key, 40))
    nrm = lambda shape, scale: jax.random.normal(next(ks), shape, jnp.float32) * scale
    L = DEPTH
    return {
        "x": nrm((BATCH, SEQ, D_MODEL), 1.0),
        "c": nrm((BATCH, D_MODEL), 1.0),
        "ada_w": nrm((L, D_MODEL, 6 * D_MODEL), 0.5 * D_MODEL ** -0.5),
        "ada_b": nrm((L, 6 * D_MODEL), 0.02),
        "mix_norm_g": 1.0 + nrm((L, D_MODEL), 0.02),
        "w_in": nrm((L, D_MODEL, IN_W), D_MODEL ** -0.5),
        "kv_norm_g": 1.0 + nrm((L, KV_LATENT), 0.02),
        "w_kv_up": nrm((L, KV_LATENT, 2 * ATTN_W), KV_LATENT ** -0.5),
        "q_norm_g": 1.0 + nrm((L, ATTN_HEAD_DIM), 0.02),
        "k_norm_g": 1.0 + nrm((L, ATTN_HEAD_DIM), 0.02),
        "rwkv_mu": jax.random.uniform(next(ks), (L, SHIFT_W), jnp.float32, 0.2, 0.8),
        "rwkv_w0": -1.0 + nrm((L, RWKV_W), 0.5),
        "rwkv_w2": nrm((L, DECAY_LORA, RWKV_W), 0.5 * DECAY_LORA ** -0.5),
        "rwkv_a0": nrm((L, RWKV_W), 0.1),
        "rwkv_a2": nrm((L, AAA_LORA, RWKV_W), 0.5 * AAA_LORA ** -0.5),
        "rwkv_g2": nrm((L, GATE_LORA, RWKV_W), GATE_LORA ** -0.5),
        "rwkv_k_k": 0.85 + nrm((L, RWKV_W), 0.02),
        "rwkv_k_a": 1.0 + nrm((L, RWKV_W), 0.02),
        "rwkv_r_k": nrm((L, N_RWKV_HEADS, RWKV_HEAD_DIM), 0.1),
        "rwkv_ln_w": 1.0 + nrm((L, RWKV_W), 0.02),
        "rwkv_ln_b": nrm((L, RWKV_W), 0.02),
        "w_branch_attn": nrm((L, ATTN_W, D_MODEL), ATTN_W ** -0.5),
        "w_branch_rwkv": nrm((L, RWKV_W, D_MODEL), RWKV_W ** -0.5),
        "w_out": nrm((L, D_MODEL, D_MODEL), D_MODEL ** -0.5),
        "moe_norm_g": 1.0 + nrm((L, D_MODEL), 0.02),
        "router_group_w": nrm((L, D_MODEL, N_GROUPS), D_MODEL ** -0.5),
        "router_expert_w": nrm((L, D_MODEL, N_EXPERTS_2), D_MODEL ** -0.5),
        "router_expert_bias": nrm((L, N_EXPERTS_2), 0.01),
        "expert_w_gate": nrm((L, N_EXPERTS_2, D_MODEL, D_EXPERT_2), D_MODEL ** -0.5),
        "expert_w_up": nrm((L, N_EXPERTS_2, D_MODEL, D_EXPERT_2), D_MODEL ** -0.5),
        "expert_w_down": nrm((L, N_EXPERTS_2, D_EXPERT_2, D_MODEL), D_EXPERT_2 ** -0.5),
    }

def second_block(x, c, ada_w, ada_b, mix_norm_g, w_in, kv_norm_g, w_kv_up, q_norm_g, k_norm_g,
              rwkv_mu, rwkv_w0, rwkv_w2, rwkv_a0, rwkv_a2, rwkv_g2, rwkv_k_k, rwkv_k_a, rwkv_r_k,
              rwkv_ln_w, rwkv_ln_b, w_branch_attn, w_branch_rwkv, w_out, moe_norm_g,
              router_group_w, router_expert_w, router_expert_bias, expert_w_gate, expert_w_up,
              expert_w_down):
    B, S, D = x.shape
    h = x
    for l in range(DEPTH):
        mod = jax.nn.silu(c) @ ada_w[l] + ada_b[l]
        sh1, sc1, gt1, sh2, sc2, gt2 = jnp.split(mod[:, None, :], 6, axis=-1)

        xn = _rmsnorm(h, mix_norm_g[l]) * (1.0 + sc1) + sh1
        proj = xn @ w_in[l]
        q_a, kv_lat, q_i, k_i, w_i, p_shift, gate_a, gate_r = _split(proj, IN_SPLITS)
        q = _rmsnorm(q_a.reshape(B, S, N_ATTN_HEADS, ATTN_HEAD_DIM), q_norm_g[l])
        kv = _rmsnorm(kv_lat, kv_norm_g[l]) @ w_kv_up[l]
        k_lin, v_lin = jnp.split(kv, 2, axis=-1)
        k = _rmsnorm(k_lin.reshape(B, S, N_ATTN_HEADS, ATTN_HEAD_DIM), k_norm_g[l])
        v = v_lin.reshape(B, S, N_ATTN_HEADS, ATTN_HEAD_DIM)
        o_attn = _dsa_attention(q, k, v, q_i.reshape(B, S, N_IDX_HEADS, IDX_HEAD_DIM), k_i, w_i)
        o_rwkv = _rwkv7_time_mix(p_shift, rwkv_mu[l], rwkv_w0[l], rwkv_w2[l], rwkv_a0[l], rwkv_a2[l],
                                 rwkv_g2[l], rwkv_k_k[l], rwkv_k_a[l], rwkv_r_k[l], rwkv_ln_w[l], rwkv_ln_b[l])
        merged = jax.nn.sigmoid(gate_a) * (o_attn @ w_branch_attn[l]) + jax.nn.sigmoid(gate_r) * (o_rwkv @ w_branch_rwkv[l])
        h = h + gt1 * (merged @ w_out[l])

        xn2 = _rmsnorm(h, moe_norm_g[l]) * (1.0 + sc2) + sh2
        moe = _hier_moe(xn2.reshape(B * S, D), router_group_w[l], router_expert_w[l], router_expert_bias[l],
                        expert_w_gate[l], expert_w_up[l], expert_w_down[l])
        h = h + gt2 * moe.reshape(B, S, D)
    return h


def setup_inputs(seed=0):
    out = dict(first_inputs(seed))
    for name, value in second_inputs(seed + 1).items():
        if name != "x":
            out[name + "_2"] = value
    return out


def reference(
    x, c, ada_w, ada_b, norm_mix, norm_ffn, attn_w_in, attn_lam_q1, attn_lam_k1, attn_lam_q2,
    attn_lam_k2, attn_subln, attn_w_out, fourier_w_in, fourier_w_out, router_group_w,
    router_group_b, router_expert_w, router_expert_b, expert_w_gate, expert_w_up, expert_w_down,
    norm_final, c_2, ada_w_2, ada_b_2, mix_norm_g_2, w_in_2, kv_norm_g_2, w_kv_up_2, q_norm_g_2,
    k_norm_g_2, rwkv_mu_2, rwkv_w0_2, rwkv_w2_2, rwkv_a0_2, rwkv_a2_2, rwkv_g2_2, rwkv_k_k_2,
    rwkv_k_a_2, rwkv_r_k_2, rwkv_ln_w_2, rwkv_ln_b_2, w_branch_attn_2, w_branch_rwkv_2, w_out_2,
    moe_norm_g_2, router_group_w_2, router_expert_w_2, router_expert_bias_2, expert_w_gate_2,
    expert_w_up_2, expert_w_down_2,
):
    x = first_block(
        x, c, ada_w, ada_b, norm_mix, norm_ffn, attn_w_in, attn_lam_q1, attn_lam_k1,
        attn_lam_q2, attn_lam_k2, attn_subln, attn_w_out, fourier_w_in, fourier_w_out,
        router_group_w, router_group_b, router_expert_w, router_expert_b, expert_w_gate,
        expert_w_up, expert_w_down, norm_final,
    )
    return second_block(
        x, c_2, ada_w_2, ada_b_2, mix_norm_g_2, w_in_2, kv_norm_g_2, w_kv_up_2, q_norm_g_2,
        k_norm_g_2, rwkv_mu_2, rwkv_w0_2, rwkv_w2_2, rwkv_a0_2, rwkv_a2_2, rwkv_g2_2,
        rwkv_k_k_2, rwkv_k_a_2, rwkv_r_k_2, rwkv_ln_w_2, rwkv_ln_b_2, w_branch_attn_2,
        w_branch_rwkv_2, w_out_2, moe_norm_g_2, router_group_w_2, router_expert_w_2,
        router_expert_bias_2, expert_w_gate_2, expert_w_up_2, expert_w_down_2,
    )


_drawn_inputs = setup_inputs


def setup_inputs(seed=0):
    import zlib

    import numpy as np

    out = dict(_drawn_inputs(seed))
    spreads = {}
    factors = {'norm_mix': 6.666,
     'norm_ffn': 4.158,
     'attn_lam_q1': 3.155,
     'attn_lam_k1': 102.712,
     'attn_lam_q2': 6.639,
     'attn_lam_k2': 8.0,
     'attn_subln': 4.716,
     'router_group_b': 8.0,
     'router_expert_b': 7.964,
     'mix_norm_g_2': 4.313,
     'kv_norm_g_2': 28.621,
     'q_norm_g_2': 30.375,
     'k_norm_g_2': 32.938,
     'rwkv_w2_2': 5.41,
     'rwkv_a0_2': 7.459,
     'rwkv_k_k_2': 200.0,
     'rwkv_k_a_2': 8.0,
     'rwkv_ln_w_2': 200.0,
     'rwkv_ln_b_2': 197.439,
     'moe_norm_g_2': 14.388,
     'router_expert_bias_2': 32.474,
     'rwkv_w0_2': 2.686}
    for name, (base, spread) in spreads.items():
        noise = np.random.default_rng([zlib.crc32(name.encode()), seed]).standard_normal(out[name].shape)
        drawn = base * np.exp(spread * noise) if base else spread * noise
        out[name] = __import__('jax').numpy.asarray(drawn.astype(out[name].dtype))
    for name, factor in factors.items():
        out[name] = (out[name] * factor).astype(out[name].dtype)
    return out
```

```python
import math
from contextlib import ExitStack

import numpy as np

import concourse.bass as bass
from concourse import mybir

F32 = mybir.dt.float32
I32 = mybir.dt.int32
ALU = mybir.AluOpType
ACT = mybir.ActivationFunctionType
X = mybir.AxisListType.X

P = 128
S = 256
D = 1024
NT = S // P
KC = D // P
EPS = 1e-6
CELL = 4096
SLOTS = 64
ROUNDS = S // SLOTS
FE = 512
FC = FE // P
BIG = 3.0e38

ROWS_A = [("c", 8), ("c_2", 8), ("norm_mix", 8), ("norm_ffn", 8), ("mix_norm_g_2", 8), ("moe_norm_g_2", 8),
          ("ada_b", 48)]
ROWS_B = [("ada_b_2", 48), ("rwkv_w0_2", 4), ("rwkv_a0_2", 4), ("rwkv_k_k_2", 4), ("rwkv_k_a_2", 4),
          ("rwkv_r_k_2", 4), ("rwkv_ln_w_2", 4), ("rwkv_ln_b_2", 4), ("kv_norm_g_2", 2), ("attn_subln", 1)]


def row_starts(rows):
    at, out = 0, {}
    for name, n in rows:
        out[name] = at
        at += n
    return out, at


def build(nc, inp, out, debug=None, until=99):
    ctx = ExitStack()
    with ctx:
        def sb(name, cols, dt=F32, parts=P):
            return ctx.enter_context(nc.sbuf_tensor(name, [parts, cols], dt))

        sems = {}

        def sem(name):
            if name not in sems:
                sems[name] = nc.alloc_semaphore(name)
            return sems[name]

        KEPT = {"v_chain", "p_chain", "ssq", "ms_done", "root", "x_ready", "xn_ready", "hT_psum", "hT_done", "mod_done",
                "modc_psum", "g_psum", "g_out", "prio", "logits", "masked", "places", "g_shifted", "g_exp", "d12",
                "d12_exp", "nf_loaded", "ada2_used0", "ada2_used1", "ada2_used2", "p2_used", "p2_loaded0",
                "p2_loaded1", "p2_loaded2", "p2_loaded3"}

        def give_back():
            old = sorted(n for n in sems if n not in KEPT)
            nc.clear_and_free_semaphores([sems.pop(n) for n in old])
            nc.all_engine_barrier()

        def chain(eng, name):
            count = [0]

            def step(ins):
                count[0] += 1
                ins.then_inc(sem(name), 1)
                eng.wait_ge(sem(name), count[0])
            return step

        v_step = chain(nc.vector, "v_chain")
        p_step = chain(nc.gpsimd, "p_chain")

        ring = sb("ring", 6 * CELL)
        side = sb("side", 2 * CELL)
        acc = sb("acc", 6 * D)
        tmp = sb("tmp", CELL)
        x_sb = sb("x_sb", NT * D)
        xn_sb = sb("xn_sb", NT * D)
        hT_sb = sb("hT_sb", KC * S)
        gate_rows = sb("gate_rows", 2 * D)
        ident = sb("ident", P)
        ones = sb("ones", P)
        before = sb("before", P)
        headones = sb("headones", P)
        slot_ids = sb("slot_ids", SLOTS)
        colsA = sb("colsA", P)
        colsB = sb("colsB", P)
        cond = sb("cond", 2 * KC)
        modc = sb("modc", 4 * KC)
        small = sb("small", 64)
        NE_MAX = 32
        TAB = ROUNDS * NE_MAX + 2
        pos_t = sb("pos_t", NT * TAB)
        mask_t = sb("mask_t", NT * TAB)
        gate_t = sb("gate_t", NT * TAB)
        rounds_i = sb("rounds_i", 1, I32)
        qk_cols = sb("qk_cols", 2)

        ps = [ctx.enter_context(nc.psum_tensor(f"ps{i}", [P, 512], F32)) for i in range(8)]

        x3 = x_sb[:, :].rearrange("p (t d) -> p t d", t=NT)
        xn3 = xn_sb[:, :].rearrange("p (t d) -> p t d", t=NT)
        hT = hT_sb[:, :].rearrange("p (c s) -> p c s", c=KC)
        g_b = gate_rows[:, :].rearrange("p (g d) -> p g d", g=2)

        def cell(i, kc=8, w=512):
            return ring[:, i * CELL:i * CELL + kc * w].rearrange("p (c n) -> p c n", c=kc)

        def w_cols(ap, a, b):
            return ap[:, a:b].rearrange("(c p) n -> p c n", p=P)

        stA, nA = row_starts(ROWS_A)
        stB, nB = row_starts(ROWS_B)
        MU0 = nB + 2
        NB_ALL = MU0 + 15
        rowsA = tmp[:, 0:P]
        rowsB = tmp[:, P:2 * P]

        def colA(name, i=0, n=1):
            return colsA[:, stA[name] + i:stA[name] + i + n]

        def colB(name, i=0, n=1):
            return colsB[:, stB[name] + i:stB[name] + i + n]

        lam_in = tmp[:, 512:768].rearrange("p (v d) -> p v d", v=4)
        lam = small[:, 0:8]

        AW = 256
        N_ADA_P = 6 * D // AW
        SIDE_SLOTS = 4

        def side_slot(n):
            a = (n % SIDE_SLOTS) * 2048
            return side[:, a:a + 2048].rearrange("p (c n) -> p c n", c=8)

        def load_ada(sp, w, first, n, base):
            for i in range(first, first + n):
                g = base + i
                if g >= SIDE_SLOTS:
                    sp.wait_ge(sem("ada_used"), g - SIDE_SLOTS + 1)
                sp.dma_start(side_slot(g), w_cols(w, i * AW, (i + 1) * AW)).then_inc(
                    sem(f"ada_loaded{g % SIDE_SLOTS}"), 16)

        def sum_ada(v, first, n, base, blk, then=None):
            for i in range(first, first + n):
                g = base + i
                v.wait_ge(sem(f"ada_loaded{g % SIDE_SLOTS}"), 16 * (g // SIDE_SLOTS + 1))
                a = acc[:, i * AW:(i + 1) * AW]
                w = side_slot(g)
                for k in range(KC):
                    s = cond[:, blk * KC + k:blk * KC + k + 1]
                    if k == 0:
                        ins = v.tensor_scalar(a, w[:, k, :], s, None, ALU.mult)
                    else:
                        ins = v.scalar_tensor_tensor(a, w[:, k, :], s, a, ALU.mult, ALU.add)
                    if k < KC - 1:
                        v_step(ins)
                ins.then_inc(sem("ada_used"), 1)

        def ada_columns(pe, vecs, bank, name, wait):
            pe.wait_ge(sem(wait[0]), wait[1])
            for n, m in enumerate(vecs):
                for j in range(KC):
                    last = pe.matmul(ps[bank][:, n * KC + j:n * KC + j + 1], acc[:, m * D + j * P:m * D + (j + 1) * P],
                                     ones[:, 0:1], start=True, stop=True)
            last.then_inc(sem(name), 1)

        def ada_rows(pe, m, bank0, name, wait):
            pe.wait_ge(sem(wait[0]), wait[1])
            for n in range(2):
                last = pe.matmul(ps[bank0 + n][:, :], ones[:, :], acc[:, m * D + n * 512:m * D + (n + 1) * 512],
                                 start=True, stop=True)
            last.then_inc(sem(name), 1)

        NORMS = ["norm1", "norm2", "final1", "norm3", "norm4"]

        def rms_scalar(act, n, scr):
            if n:
                act.wait_ge(sem("x_ready"), n)
            for t in range(NT):
                act.activation(scr[:, t * D:(t + 1) * D], x3[:, t, :], ACT.Square,
                               accum_out=small[:, 8 + t:9 + t]).then_inc(sem("ssq"), 1)
            act.wait_ge(sem("ms_done"), n + 1)
            act.activation(small[:, 12:14], small[:, 10:12], ACT.Sqrt).then_inc(sem("root"), 1)

        def rms_vector(v, n, out3, weight=None, name="xn_ready"):
            v.wait_ge(sem("ssq"), NT * (n + 1))
            v.tensor_scalar(small[:, 10:12], small[:, 8:10], 1.0 / D, EPS, ALU.mult, ALU.add).then_inc(
                sem("ms_done"), 1)
            v.wait_ge(sem("root"), n + 1)
            v_step(v.reciprocal(small[:, 14:16], small[:, 12:14]))
            for t in range(NT):
                if weight is None:
                    ins = v.tensor_scalar(out3[:, t, :], x3[:, t, :], small[:, 14 + t:15 + t], None, ALU.mult)
                else:
                    ins = v.scalar_tensor_tensor(out3[:, t, :], x3[:, t, :], small[:, 14 + t:15 + t], weight,
                                                 ALU.mult, ALU.mult)
            ins.then_inc(sem(name), 1)

        def hT_tensor(pe, n):
            pe.wait_ge(sem("xn_ready"), n + 1)
            for c in range(KC):
                b = ps[4 + c // 2]
                for t in range(NT):
                    o = (c % 2) * S + t * P
                    last = pe.transpose(b[:, o:o + P], xn3[:, t, c * P:(c + 1) * P], ident[:, :])
                if c % 2:
                    last.then_inc(sem("hT_psum"), 1)

        def hT_vector(v, n):
            v.wait_ge(sem("mod_done"), n + 1)
            for c in range(KC):
                if c % 2 == 0:
                    v.wait_ge(sem("hT_psum"), 4 * n + c // 2 + 1)
                o = (c % 2) * S
                v.tensor_scalar(hT[:, c, :], ps[4 + c // 2][:, o:o + S], modc[:, (2 * (n % 2)) * KC + c:(2 * (n % 2)) * KC + c + 1],
                                modc[:, (2 * (n % 2) + 1) * KC + c:(2 * (n % 2) + 1) * KC + c + 1],
                                ALU.mult, ALU.add).then_inc(sem("hT_done"), 1)

        with nc.Block() as block:
            @block.sync
            def _(sp):
                sp.dma_start(x3, inp["x"][0].rearrange("(t p) d -> p t d", p=P)).then_inc(sem("x_loaded"), 16)
                sp.wait_ge(sem("rows_zero"), 1)
                for rows, st, spec in ((rowsA, stA, ROWS_A), (rowsB, stB, ROWS_B)):
                    for name, n in spec:
                        src = inp[name]
                        src = src.rearrange("a h d -> (a h d)") if name == "rwkv_r_k_2" else src.rearrange("a n -> (a n)")
                        sp.dma_start(rows[st[name]:st[name] + n, :], src.rearrange("(r n) -> r n", n=P)).then_inc(
                            sem("rows_loaded"), 16)
                for i, name in enumerate(("q_norm_g_2", "k_norm_g_2")):
                    for h in range(2):
                        sp.dma_start(rowsB[nB + i:nB + i + 1, h * 64:(h + 1) * 64], inp[name]).then_inc(
                            sem("rows_loaded"), 16)
                mu = inp["rwkv_mu_2"].rearrange("a n -> (a n)")
                sp.dma_start(rowsB[MU0:MU0 + 14, :], mu[0:14 * P].rearrange("(r n) -> r n", n=P)).then_inc(
                    sem("rows_loaded"), 16)
                sp.dma_start(rowsB[MU0 + 14:MU0 + 15, 0:32], mu[14 * P:14 * P + 32].rearrange("(a n) -> a n", a=1)).then_inc(
                    sem("rows_loaded"), 16)
                load_ada(sp, inp["ada_w"][0], 0, 8, 0)
                for i in range(6):
                    sp.dma_start(cell(i), w_cols(inp["attn_w_in"][0], i * 512, (i + 1) * 512)).then_inc(
                        sem(f"m1_loaded{i}"), 16)
                for i, name in enumerate(("attn_lam_q1", "attn_lam_k1", "attn_lam_q2", "attn_lam_k2")):
                    sp.dma_start(lam_in[:, i, :], inp[name][0:1, :].broadcast_to((P, 64))).then_inc(
                        sem("lam_loaded"), 16)
                for i, m in enumerate((2, 5)):
                    sp.dma_start(g_b[:, i, :], inp["ada_b"][0:1, m * D:(m + 1) * D].broadcast_to((P, D))).then_inc(
                        sem("gb_loaded"), 16)
            N_ROW_DMAS = len(ROWS_A) + len(ROWS_B) + 6

            @block.gpsimd
            def _(pool):
                pool.memset(tmp[:, 0:2 * P], 0.0).then_inc(sem("rows_zero"), 1)
                pool.wait_ge(sem("rows_zero"), 1)
                p_step(pool.memset(ident[:, :], 0.0))
                p_step(pool.memset(ones[:, :], 1.0))
                p_step(pool.memset(headones[:, :], 1.0))
                p_step(pool.affine_select(out=ident[:, :], in_=ident[:, :], compare_op=ALU.not_equal, fill=1.0, base=0,
                                          pattern=[[-1, P]], channel_multiplier=1))
                p_step(pool.affine_select(out=before[:, :], in_=ones[:, :], compare_op=ALU.is_gt, fill=0.0, base=0,
                                          pattern=[[1, P]], channel_multiplier=-1))
                p_step(pool.memset(headones[0:64, 64:128], 0.0))
                p_step(pool.memset(headones[64:128, 0:64], 0.0))
                pool.iota(slot_ids[:, :], pattern=[[1, SLOTS]], base=0, channel_multiplier=0,
                          allow_small_or_imprecise_dtypes=True).then_inc(sem("const"), 1)

            @block.tensor
            def _(pe):
                pe.wait_ge(sem("const"), 1)
                pe.wait_ge(sem("rows_loaded"), 16 * N_ROW_DMAS)
                pe.transpose(ps[0][:, 0:P], rowsA, ident[:, :])
                pe.transpose(ps[0][:, P:2 * P], rowsB, ident[:, :]).then_inc(sem("cols_psum"), 1)
                ada_columns(pe, (0, 1), 1, "modc_psum", ("ada_used", 8))
                hT_tensor(pe, 0)

            @block.scalar
            def _(act):
                act.wait_ge(sem("x_loaded"), 16)
                rms_scalar(act, 0, xn_sb)
                act.wait_ge(sem("cols_done"), 2)
                act.activation(cond[:, :], colsA[:, 0:16], ACT.Sigmoid).then_inc(sem("sig_c"), 1)

            @block.vector
            def _(v):
                v.wait_ge(sem("cols_psum"), 1)
                v.tensor_copy(colsA[:, :], ps[0][:, 0:P]).then_inc(sem("cols_done"), 1)
                v.tensor_copy(colsB[:, :], ps[0][:, P:2 * P]).then_inc(sem("cols_done"), 1)
                rms_vector(v, 0, xn3)
                v.wait_ge(sem("sig_c"), 1)
                v_step(v.tensor_tensor(cond[:, :], cond[:, :], colsA[:, 0:16], ALU.mult))
                sum_ada(v, 0, 8, 0, 0)

        H = 8
        qkT = tmp[:, :].rearrange("p (c s) -> p c s", c=2 * H)
        v3 = xn3
        sub08 = qk_cols[:, 0:1]
        LAM_INIT = 0.8 - 0.6 * math.exp(0.0)

        def fill_modc(v, vec_scale, vec_shift, psc, shift_at, scale_at, norm_col, ada_shift, ada_scale):
            v_step(v.tensor_tensor(modc[:, vec_shift:vec_shift + KC], psc[:, shift_at:shift_at + KC], ada_shift, ALU.add))
            v_step(v.tensor_tensor(modc[:, vec_scale:vec_scale + KC], psc[:, scale_at:scale_at + KC], ada_scale, ALU.add))
            v_step(v.scalar_tensor_tensor(modc[:, vec_scale:vec_scale + KC], modc[:, vec_scale:vec_scale + KC], 1.0,
                                          norm_col, ALU.add, ALU.mult))

        def copy_lam(v):
            v.wait_ge(sem("lam_loaded"), 64)
            for i in range(2):
                v_step(v.tensor_tensor(lam_in[:, 2 * i, :], lam_in[:, 2 * i, :], lam_in[:, 2 * i + 1, :], ALU.mult))
                v_step(v.tensor_reduce(lam[:, i:i + 1], lam_in[:, 2 * i, :], X, ALU.add))
            v.sem_inc(sem("lam_sums"), 1) if False else v.tensor_scalar(sub08, colB("attn_subln"), 1.0 - LAM_INIT, None, ALU.mult).then_inc(sem("lam_sums"), 1)

        with nc.Block() as block:
            @block.sync
            def _(sp):
                load_ada(sp, inp["ada_w"][0], 8, 16, 0)

            @block.tensor
            def _(pe):
                for m in range(16):
                    if m % 4 == 0:
                        pe.wait_ge(sem(f"m1_loaded{m // 4}"), 16)
                    if m == 0:
                        pe.wait_ge(sem("hT_done"), KC)
                    if m >= 4:
                        pe.wait_ge(sem("qk_out"), m - 3)
                    w = cell(m // 4)
                    for c in range(KC):
                        last = pe.matmul(ps[m % 4][:, 0:S], w[:, c, (m % 4) * P:(m % 4 + 1) * P], hT[:, c, :],
                                         start=(c == 0), stop=(c == KC - 1))
                    last.then_inc(sem("qk_psum"), 1)
                for g in range(4):
                    t, n = g // 2, g % 2
                    if t == 0:
                        pe.wait_ge(sem(f"m1_loaded{4 + n}"), 16)
                    for c in range(KC):
                        last = pe.matmul(ps[4 + g][:, :], hT[:, c, t * P:(t + 1) * P], cell(4 + n)[:, c, :],
                                         start=(c == 0), stop=(c == KC - 1))
                    last.then_inc(sem("v_psum"), 1)
                pe.wait_ge(sem("qk_out"), 16)
                ada_rows(pe, 2, 0, "g_psum", ("ada_used", 24))
                ada_columns(pe, (3, 4), 2, "modc_psum", ("ada_used", 24))
                pe.wait_ge(sem("g_out"), 1)
                ada_rows(pe, 5, 0, "g_psum", ("ada_used", 24))

            @block.scalar
            def _(act):
                act.wait_ge(sem("lam_sums"), 1)
                act.activation(lam[:, 2:4], lam[:, 0:2], ACT.Exp).then_inc(sem("lam_exp"), 1)
                for m in range(16):
                    act.wait_ge(sem("qk_psum"), m + 1)
                    act.activation(qkT[:, m, :], ps[m % 4][:, 0:S], ACT.Copy).then_inc(sem("qk_out"), 1)
                for g in range(4):
                    t, n = g // 2, g % 2
                    act.wait_ge(sem("v_psum"), g + 1)
                    act.activation(v3[:, t, n * 512:(n + 1) * 512], ps[4 + g][:, :], ACT.Copy).then_inc(sem("v_out"), 1)

            @block.vector
            def _(v):
                v.wait_ge(sem("modc_psum"), 1)
                fill_modc(v, 0, KC, ps[1], 0, KC, colA("norm_mix", 0, KC), colA("ada_b", 0, KC), colA("ada_b", KC, KC))
                v.sem_inc(sem("mod_done"), 1) if False else v.tensor_copy(small[:, 20:21], small[:, 14:15]).then_inc(sem("mod_done"), 1)
                hT_vector(v, 0)
                copy_lam(v)
                v.wait_ge(sem("lam_exp"), 1)
                v_step(v.tensor_tensor(lam[:, 4:5], lam[:, 2:3], lam[:, 3:4], ALU.subtract))
                v_step(v.tensor_scalar(lam[:, 5:6], lam[:, 4:5], -1.0, -LAM_INIT, ALU.mult, ALU.add))
                sum_ada(v, 8, 16, 0, 0)
                v.wait_ge(sem("gb_loaded"), 32)
                for i in range(2):
                    v.wait_ge(sem("g_psum"), i + 1)
                    for n in range(2):
                        a = g_b[:, i, n * 512:(n + 1) * 512]
                        ins = v.tensor_tensor(a, ps[n][:, :], a, ALU.add)
                    ins.then_inc(sem("g_out"), 1)
                v.wait_ge(sem("modc_psum"), 2)
                fill_modc(v, 2 * KC, 3 * KC, ps[2], 0, KC, colA("norm_ffn", 0, KC), colA("ada_b", 3 * KC, KC), colA("ada_b", 4 * KC, KC))

        sS = acc[:, 0:1024].rearrange("p (b n) -> p b n", b=2)
        e_a = acc[:, 1024:2048].rearrange("p (b n) -> p b n", b=2)
        a_a = acc[:, 2048:2560].rearrange("p (b n) -> p b n", b=2)
        aT = acc[:, 2560:3072].rearrange("p (b n) -> p b n", b=2)
        o3 = acc[:, 3072:5120].rearrange("p (t d) -> p t d", t=NT)
        dist = acc[:, 5120:5632].rearrange("p (t s) -> p t s", t=NT)
        st_a = acc[:, 5632:5888]
        U = H * NT

        with nc.Block() as block:
            @block.sync
            def _(sp):
                for i in range(2):
                    sp.dma_start(cell(4 + i), w_cols(inp["attn_w_out"][0], i * 512, (i + 1) * 512)).then_inc(
                        sem(f"wo1_loaded{i}"), 16)

            @block.gpsimd
            def _(pool):
                pool.iota(dist, pattern=[[P, NT], [-1, S]], base=0, channel_multiplier=1,
                          allow_small_or_imprecise_dtypes=True).then_inc(sem("dist"), 1)

            @block.tensor
            def _(pe):
                def scores(u):
                    h, t = u // NT, u % NT
                    if u >= 2:
                        pe.wait_ge(sem("att_biased"), u - 1)
                    for w in range(2):
                        last = pe.matmul(ps[2 * (u % 2) + w][:, 0:S], qkT[w * 64:(w + 1) * 64, h, t * P:(t + 1) * P],
                                         qkT[w * 64:(w + 1) * 64, H + h, :], start=True, stop=True)
                    last.then_inc(sem("att_scores"), 1)

                def turn(u):
                    pe.wait_ge(sem("att_a"), u + 1)
                    if u >= 2:
                        pe.wait_ge(sem("att_aT"), u - 1)
                    for k in range(2):
                        last = pe.transpose(ps[4 + u % 2][:, k * P:(k + 1) * P], a_a[:, u % 2, k * P:(k + 1) * P], ident[:, :])
                    last.then_inc(sem("att_aT_psum"), 1)

                def av(u):
                    h = u // NT
                    pe.wait_ge(sem("att_aT"), u + 1)
                    if u >= 2:
                        pe.wait_ge(sem("att_o"), u - 1)
                    for k in range(2):
                        last = pe.matmul(ps[6 + u % 2][:, 0:P], aT[:, u % 2, k * P:(k + 1) * P],
                                         v3[:, k, h * P:(h + 1) * P], start=(k == 0), stop=(k == 1))
                    last.then_inc(sem("att_av"), 1)

                scores(0)
                for u in range(U + 1):
                    if u + 1 < U:
                        scores(u + 1)
                    if u < U:
                        turn(u)
                    if u >= 1:
                        av(u - 1)

            @block.scalar
            def _(act):
                for u in range(U + 1):
                    if u < U:
                        act.wait_ge(sem("att_max"), u + 1)
                        for w in range(2):
                            act.activation(e_a[:, u % 2, w * S:(w + 1) * S], sS[:, u % 2, w * S:(w + 1) * S], ACT.Exp,
                                           bias=st_a[:, 4 * u + w:4 * u + w + 1], scale=0.125,
                                           accum_out=st_a[:, 4 * u + 2 + w:4 * u + 3 + w]).then_inc(sem("att_exp"), 1)
                    if u >= 1:
                        act.wait_ge(sem("att_aT_psum"), u)
                        act.activation(aT[:, (u - 1) % 2, :], ps[4 + (u - 1) % 2][:, 0:S], ACT.Copy).then_inc(sem("att_aT"), 1)

            @block.vector
            def _(v):
                v.wait_ge(sem("dist"), 1)
                v_step(v.scalar_tensor_tensor(dist, dist, -1.0, dist, ALU.mult, ALU.max))

                def first(u):
                    h, t = u // NT, u % NT
                    v.wait_ge(sem("att_scores"), u + 1)
                    for w in range(2):
                        ins = v.scalar_tensor_tensor(sS[:, u % 2, w * S:(w + 1) * S], dist[:, t, :], -8.0 * 2.0 ** -(h + 1),
                                                     ps[2 * (u % 2) + w][:, 0:S], ALU.mult, ALU.add)
                    ins.then_inc(sem("att_biased"), 1)
                    v.wait_ge(sem("att_biased"), u + 1)
                    v_step(v.tensor_reduce(st_a[:, 192 + 2 * (u % 2):194 + 2 * (u % 2)],
                                           sS[:, u % 2, :].rearrange("p (w s) -> p w s", w=2), X, ALU.max))
                    v.tensor_scalar(st_a[:, 4 * u:4 * u + 2], st_a[:, 192 + 2 * (u % 2):194 + 2 * (u % 2)], -0.125, None,
                                    ALU.mult).then_inc(sem("att_max"), 1)

                def second(u):
                    v.wait_ge(sem("att_exp"), 2 * u + 2)
                    r = st_a[:, 64 + 4 * u:64 + 4 * u + 2]
                    v_step(v.reciprocal(r, st_a[:, 4 * u + 2:4 * u + 4]))
                    v_step(v.tensor_scalar(r[:, 1:2], r[:, 1:2], lam[:, 5:6], None, ALU.mult))
                    if u >= 2:
                        v.wait_ge(sem("att_aT_psum"), u - 1)
                    v_step(v.tensor_scalar(a_a[:, u % 2, :], e_a[:, u % 2, 0:S], r[:, 0:1], None, ALU.mult))
                    v.scalar_tensor_tensor(a_a[:, u % 2, :], e_a[:, u % 2, S:2 * S], r[:, 1:2], a_a[:, u % 2, :],
                                           ALU.mult, ALU.add).then_inc(sem("att_a"), 1)

                def third(u):
                    h, t = u // NT, u % NT
                    v.wait_ge(sem("att_av"), u + 1)
                    v.tensor_copy(o3[:, t, h * P:(h + 1) * P], ps[6 + u % 2][:, 0:P]).then_inc(sem("att_o"), 1)

                first(0)
                for u in range(U + 1):
                    if u + 1 < U:
                        first(u + 1)
                    if u < U:
                        second(u)
                    if u >= 1:
                        third(u - 1)

        NG = 4

        def load_router(sp, k, wg, we, bg, be):
            ne = be.shape[1]
            rw = tmp[:, 2048:2048 + KC * (NG + ne)].rearrange("p (c n) -> p c n", c=KC)
            sp.dma_start(rw[:, :, 0:NG], wg.rearrange("(c p) g -> p c g", p=P)).then_inc(sem(f"router{k}"), 16)
            sp.dma_start(rw[:, :, NG:], we.rearrange("(c p) g -> p c g", p=P)).then_inc(sem(f"router{k}"), 16)
            if bg is not None:
                sp.dma_start(tmp[:, 2400:2400 + NG], bg.broadcast_to((P, NG))).then_inc(sem(f"router{k}"), 16)
            sp.dma_start(tmp[:, 2400 + NG:2400 + NG + ne], be.broadcast_to((P, ne))).then_inc(sem(f"router{k}"), 16)

        oT = hT

        def residual(v, i, banks, first_bank, name):
            for g in range(4):
                t, n = g // 2, g % 2
                v.wait_ge(sem(name), g + 1)
                y = tmp[:, g * 512:(g + 1) * 512]
                v_step(v.tensor_tensor(y, ps[first_bank + g][:, :], g_b[:, i, n * 512:(n + 1) * 512], ALU.mult))
                xs = x3[:, t, n * 512:(n + 1) * 512]
                ins = v.tensor_tensor(xs, xs, y, ALU.add)
                ins.then_inc(sem(name + "_x"), 1)
            v.wait_ge(sem(name + "_x"), 4)
            v.tensor_copy(small[:, 21:22], small[:, 14:15]).then_inc(sem("x_ready"), 1)

        with nc.Block() as block:
            @block.sync
            def _(sp):
                load_router(sp, 0, inp["router_group_w"][0], inp["router_expert_w"][0].rearrange("d g e -> d (g e)"),
                            inp["router_group_b"], inp["router_expert_b"].rearrange("a g e -> a (g e)"))

            @block.tensor
            def _(pe):
                pe.wait_ge(sem("o_normed"), 1)
                for c in range(H):
                    b = ps[4 + c // 2]
                    for t in range(NT):
                        o = (c % 2) * S + t * P
                        last = pe.transpose(b[:, o:o + P], o3[:, t, c * P:(c + 1) * P], ident[:, :])
                    last.then_inc(sem("oT_psum"), 1)
                for g in range(4):
                    t, n = g // 2, g % 2
                    if t == 0:
                        pe.wait_ge(sem(f"wo1_loaded{n}"), 16)
                    pe.wait_ge(sem("oT_done"), H)
                    for c in range(KC):
                        last = pe.matmul(ps[g][:, :], oT[:, c, t * P:(t + 1) * P], cell(4 + n)[:, c, :],
                                         start=(c == 0), stop=(c == KC - 1))
                    last.then_inc(sem("y1"), 1)
                hT_tensor(pe, 1)

            @block.scalar
            def _(act):
                for t in range(NT):
                    act.activation(tmp[:, t * D:(t + 1) * D], o3[:, t, :], ACT.Square).then_inc(sem("o_sq"), 1)
                act.wait_ge(sem("o_ms"), 1)
                act.activation(st_a[:, 16:32], st_a[:, 0:16], ACT.Sqrt).then_inc(sem("o_root"), 1)
                rms_scalar(act, 1, xn_sb)

            @block.vector
            def _(v):
                v.wait_ge(sem("o_sq"), 2)
                v_step(v.tensor_reduce(st_a[:, 32:48], tmp[:, 0:2 * D].rearrange("p (g d) -> p g d", d=P), X, ALU.add))
                v.tensor_scalar(st_a[:, 0:16], st_a[:, 32:48], 1.0 / P, EPS, ALU.mult, ALU.add).then_inc(sem("o_ms"), 1)
                v.wait_ge(sem("o_root"), 1)
                v_step(v.reciprocal(st_a[:, 48:64], st_a[:, 16:32]))
                og = acc[:, 3072:5120].rearrange("p (g d) -> p g d", d=P)
                v.tensor_tensor(og, og, st_a[:, 48:64].unsqueeze(2).broadcast_to((P, 16, P)), ALU.mult).then_inc(sem("o_normed"), 1)
                for c in range(H):
                    v.wait_ge(sem("oT_psum"), 2 * (c // 2) + 2)
                    o = (c % 2) * S
                    v.tensor_scalar(oT[:, c, :], ps[4 + c // 2][:, o:o + S], sub08, None, ALU.mult).then_inc(sem("oT_done"), 1)
                residual(v, 0, None, 0, "y1")
                rms_vector(v, 1, xn3)
                v.tensor_copy(small[:, 20:21], small[:, 14:15]).then_inc(sem("mod_done"), 1)
                hT_vector(v, 1)


        def route(k, ne, has_bg):
            EP = ne // NG
            NR = NG + ne
            W_TAB = ROUNDS * ne + 2
            rw = tmp[:, 2048:2048 + KC * NR].rearrange("p (c n) -> p c n", c=KC)
            bias = tmp[:, 2400:2400 + NR]
            pos = pos_t[:, 0:NT * W_TAB].rearrange("p (t n) -> p t n", t=NT)
            mask = mask_t[:, 0:NT * W_TAB].rearrange("p (t n) -> p t n", t=NT)
            gate = gate_t[:, 0:NT * W_TAB].rearrange("p (t n) -> p t n", t=NT)
            at = [2500]

            def t2(*dims):
                n = int(np.prod(dims))
                a = tmp[:, at[0]:at[0] + n]
                at[0] += n
                if len(dims) == 2:
                    return a.rearrange("p (t n) -> p t n", t=dims[0])
                if len(dims) == 3:
                    return a.rearrange("p (t g n) -> p t g n", t=dims[0], g=dims[1])
                return a
            L = t2(NT, NR)
            prio = t2(8)
            gm, em, zs, v1, m1, v2, m2, d12, w1, w2, gw = [t2(NT) for _ in range(11)]
            ohg, gs = t2(NT, NG), t2(NT, NG)
            prod = t2(NT, NG, EP)
            esel, e2, oh1, oh2, ew, em_ = [t2(NT, EP) for _ in range(6)]
            cnt, thr, rf = t2(ne), t2(4), t2(4)

            def per(a, n):
                return a.unsqueeze(2).broadcast_to((P, NT, n))

            with nc.Block() as block:
                @block.gpsimd
                def _(pool):
                    pool.iota(prio, pattern=[[-1, 8]], base=8, channel_multiplier=0,
                              allow_small_or_imprecise_dtypes=True).then_inc(sem("prio"), 1)

                @block.tensor
                def _(pe):
                    pe.wait_ge(sem(f"router{k}"), 64 if has_bg else 48)
                    for t in range(NT):
                        for c in range(KC):
                            last = pe.matmul(ps[0][:, t * NR:(t + 1) * NR], hT[:, c, t * P:(t + 1) * P], rw[:, c, :],
                                             start=(c == 0), stop=(c == KC - 1))
                    last.then_inc(sem("logits"), 1)
                    pe.wait_ge(sem("masked"), k + 1)
                    pe.matmul(ps[1][:, 0:ne], before[:, :], mask[:, 0, 0:ne], start=True, stop=True)
                    pe.matmul(ps[1][:, ne:2 * ne], ones[:, :], mask[:, 0, 0:ne], start=True, stop=False)
                    pe.matmul(ps[1][:, ne:2 * ne], before[:, :], mask[:, 1, 0:ne], start=False, stop=True)
                    pe.matmul(ps[1][:, 2 * ne:3 * ne], ones[:, :], mask[:, 0, 0:ne], start=True, stop=False)
                    pe.matmul(ps[1][:, 2 * ne:3 * ne], ones[:, :], mask[:, 1, 0:ne], start=False, stop=True).then_inc(
                        sem("places"), 1)

                @block.scalar
                def _(act):
                    act.wait_ge(sem("g_shifted"), k + 1)
                    act.activation(gs, gs, ACT.Exp).then_inc(sem("g_exp"), 1)
                    act.wait_ge(sem("d12"), k + 1)
                    act.activation(d12, d12, ACT.Exp).then_inc(sem("d12_exp"), 1)

                @block.vector
                def _(v):
                    v_step(v.memset(pos, 0.0))
                    v_step(v.memset(mask, 0.0))
                    v_step(v.memset(gate, 0.0))
                    v.wait_ge(sem("prio"), k + 1)
                    v.wait_ge(sem("logits"), k + 1)
                    if has_bg:
                        v_step(v.tensor_tensor(L, ps[0][:, 0:NT * NR].rearrange("p (t n) -> p t n", t=NT),
                                               bias.unsqueeze(1).broadcast_to((P, NT, NR)), ALU.add))
                    else:
                        v_step(v.tensor_copy(L, ps[0][:, 0:NT * NR].rearrange("p (t n) -> p t n", t=NT)))
                        v_step(v.tensor_tensor(L[:, :, NG:], L[:, :, NG:],
                                               bias[:, NG:].unsqueeze(1).broadcast_to((P, NT, ne)), ALU.add))
                    G = L[:, :, 0:NG]
                    E4 = L[:, :, NG:].rearrange("p t (g e) -> p t g e", g=NG)

                    def first_max(src, n, top, best, oh):
                        v_step(v.tensor_reduce(top, src, X, ALU.max))
                        v_step(v.tensor_tensor(oh, src, per(top, n), ALU.is_equal))
                        v_step(v.tensor_tensor(oh, oh, prio[:, 0:n].unsqueeze(1).broadcast_to((P, NT, n)), ALU.mult))
                        v_step(v.tensor_reduce(best, oh, X, ALU.max))
                        v_step(v.tensor_tensor(oh, oh, per(best, n), ALU.is_equal))
                    first_max(G, NG, gm, em, ohg)
                    v.tensor_tensor(gs, G, per(gm, NG), ALU.subtract).then_inc(sem("g_shifted"), 1)
                    v_step(v.tensor_tensor(prod, E4, ohg.unsqueeze(3).broadcast_to((P, NT, NG, EP)), ALU.mult))
                    v_step(v.tensor_reduce(esel, prod.rearrange("p t g e -> p t e g"), X, ALU.add))
                    first_max(esel, EP, v1, m1, oh1)
                    v_step(v.scalar_tensor_tensor(e2, oh1, -BIG, esel, ALU.mult, ALU.add))
                    first_max(e2, EP, v2, m2, oh2)
                    v.tensor_tensor(d12, v2, v1, ALU.subtract).then_inc(sem("d12"), 1)
                    v.wait_ge(sem("g_exp"), k + 1)
                    v_step(v.tensor_reduce(zs, gs, X, ALU.add))
                    v_step(v.reciprocal(gw, zs))
                    v.wait_ge(sem("d12_exp"), k + 1)
                    v_step(v.tensor_scalar(w1, d12, 1.0, None, ALU.add))
                    v_step(v.reciprocal(w1, w1))
                    v_step(v.tensor_tensor(w1, w1, gw, ALU.mult))
                    v_step(v.tensor_tensor(w2, w1, d12, ALU.mult))
                    v_step(v.tensor_tensor(em_, oh1, oh2, ALU.add))
                    v_step(v.tensor_tensor(oh1, oh1, per(w1, EP), ALU.mult))
                    v_step(v.tensor_tensor(oh2, oh2, per(w2, EP), ALU.mult))
                    v_step(v.tensor_tensor(ew, oh1, oh2, ALU.add))
                    for dst, src in ((mask, em_), (gate, ew)):
                        ins = v.tensor_tensor(dst[:, :, 0:ne].rearrange("p t (g e) -> p t g e", g=NG),
                                              ohg.unsqueeze(3).broadcast_to((P, NT, NG, EP)),
                                              src.unsqueeze(2).broadcast_to((P, NT, NG, EP)), ALU.mult)
                        if dst is mask:
                            ins.then_inc(sem("masked"), 1)
                        else:
                            v_step(ins)
                    v.wait_ge(sem("masked"), k + 1)
                    for q in range(1, ROUNDS):
                        v.tensor_copy(mask[:, :, q * ne:(q + 1) * ne], mask[:, :, 0:ne])
                        v.tensor_copy(gate[:, :, q * ne:(q + 1) * ne], gate[:, :, 0:ne])
                    v.wait_ge(sem("places"), k + 1)
                    pp = ps[1][:, 0:NT * ne].rearrange("p (t n) -> p t n", t=NT)
                    for q in range(ROUNDS):
                        v.tensor_scalar(pos[:, :, q * ne:(q + 1) * ne], pp, -float(q * SLOTS), None, ALU.add)
                    v_step(v.tensor_reduce(cnt[:, 0:1], ps[1][:, 2 * ne:3 * ne], X, ALU.max))
                    for q in range(1, ROUNDS):
                        v_step(v.tensor_scalar(thr[:, q:q + 1], cnt[:, 0:1], float(q * SLOTS), None, ALU.is_gt))
                    v_step(v.tensor_tensor(rf[:, 0:1], thr[:, 1:2], thr[:, 2:3], ALU.add))
                    v_step(v.tensor_tensor(rf[:, 0:1], rf[:, 0:1], thr[:, 3:4], ALU.add))
                    v_step(v.tensor_scalar(rounds_i[:, :], rf[:, 0:1], 1.0, None, ALU.add))

        def experts(k, ne, wg, wu, wd, sides=None, more_loads=None):
            NP = ne // 2
            W_TAB = ROUNDS * ne + 2
            pos = pos_t[:, 0:NT * W_TAB].rearrange("p (t n) -> p t n", t=NT)
            mask = mask_t[:, 0:NT * W_TAB].rearrange("p (t n) -> p t n", t=NT)
            gate = gate_t[:, 0:NT * W_TAB].rearrange("p (t n) -> p t n", t=NT)
            xg = hT_sb[:, 0:1024].rearrange("p (c n) -> p c n", c=KC)
            outb = hT_sb[:, 1024:2048]
            hid = tmp[:, 0:FE]
            hidT = tmp[:, FE:2 * FE].rearrange("p (f n) -> p f n", f=FC)
            oh = tmp[:, 1024:1280].rearrange("p (t n) -> p t n", t=NT)
            ohw = tmp[:, 1280:1536].rearrange("p (t n) -> p t n", t=NT)
            pT = tmp[:, 1536:1792]
            zero = tmp[:, 1792:1792 + 512]
            y_ps, gate_ps, up_ps, out_ps = ps[0:4], ps[4], ps[5], ps[6:8]
            n = f"{k}"

            def dst(e, j):
                i = 3 * e + j
                return cell(i) if j < 2 else cell(i, 4, 1024)

            def src(j, e):
                w = (wg, wu, wd)[j][bass.ds(e, 1), :, :] if not isinstance(e, int) else (wg, wu, wd)[j][e:e + 1, :, :]
                return w.rearrange("o (c p) n -> p (o c) n", p=P)

            def load_pair(sp, pair, it, wait):
                for j in range(3):
                    if wait:
                        sp.wait_ge(sem(("gate_used", "up_used", "down_used")[j] + n), it)
                    for e in range(2):
                        sp.dma_start(dst(e, j), src(j, 2 * pair + e)).then_inc(sem(f"moe{n}_loaded{3 * e + j}"), 16)

            with nc.Block() as block:
                @block.sync
                def _(sp):
                    load_pair(sp, 0, 0, False)
                    if sides is not None:
                        sides(sp, 0)
                    with sp.Fori(1, NP) as pair:
                        load_pair(sp, pair, pair, True)
                        if sides is not None:
                            sides(sp, pair)
                    rounds = sp.value_load(rounds_i[0:1, 0:1], min_val=1, max_val=ROUNDS)
                    with sp.If(rounds > 1):
                        with sp.Fori(1, rounds) as q:
                            with sp.Fori(0, NP) as pair:
                                load_pair(sp, pair, q * NP + pair, True)
                    sp.nop()
                    if more_loads is not None:
                        more_loads(sp)

                @block.tensor
                def _(pe):
                    rounds = pe.value_load(rounds_i[0:1, 0:1], min_val=1, max_val=ROUNDS)

                    def gather(half):
                        for c in range(4 * half, 4 * half + 4):
                            for t in range(NT):
                                last = pe.matmul((gate_ps, up_ps)[half][:, (c % 4) * P:(c % 4 + 1) * P],
                                                 xn3[:, t, c * P:(c + 1) * P], oh[:, t, :],
                                                 start=(t == 0), stop=(t == NT - 1))
                        last.then_inc(sem("gat_psum" + n), 1)

                    def project(j, bank):
                        for c in range(KC):
                            for e in range(2):
                                last = pe.matmul(bank[e * SLOTS:(e + 1) * SLOTS, :], xg[:, c, e * SLOTS:(e + 1) * SLOTS],
                                                 dst(e, j)[:, c, :], start=(c == 0), stop=(c == KC - 1))
                        return last

                    def down():
                        for h in range(2):
                            for f in range(FC):
                                for e in range(2):
                                    last = pe.matmul(out_ps[h][e * SLOTS:(e + 1) * SLOTS, :],
                                                     hidT[:, f, e * SLOTS:(e + 1) * SLOTS],
                                                     dst(e, 2)[:, f, h * 512:(h + 1) * 512],
                                                     start=(f == 0), stop=(f == FC - 1))
                        last.then_inc(sem("down_used" + n), 1)

                    def scatter(stop):
                        for t in range(NT):
                            for h in range(2):
                                last = pe.matmul(y_ps[2 * t + h][:, :], pT[:, t * P:(t + 1) * P], outb[:, h * 512:(h + 1) * 512],
                                                 start=False, stop=stop, skip_group_check=True)
                        return last

                    pe.wait_ge(sem("moe_zero" + n), 1)
                    for b in range(4):
                        pe.matmul(y_ps[b][:, :], zero[:, 0:P], zero, start=True, stop=False, skip_group_check=True)
                    pe.wait_ge(sem("oh_done" + n), 1)
                    gather(0)
                    gather(1)
                    with pe.Fori(0, rounds * NP) as it:
                        pe.wait_ge(sem("gat_done" + n), 2 * it + 2)
                        for e in range(2):
                            pe.wait_ge(sem(f"moe{n}_loaded{3 * e}"), 16 * it + 16)
                        project(0, gate_ps).then_inc(sem("gate_used" + n), 1)
                        pe.wait_ge(sem("out0_done" + n), it + 1)
                        pe.wait_ge(sem("out1_done" + n), it + 1)
                        pe.wait_ge(sem("pT_done" + n), it + 1)
                        scatter(False)
                        pe.wait_ge(sem("oh_done" + n), it + 1)
                        for t in range(NT):
                            last = pe.transpose(out_ps[1][:, t * P:(t + 1) * P], ohw[:, t, :], ident[:, :])
                        last.then_inc(sem("pT_psum" + n), 1)
                        for e in range(2):
                            pe.wait_ge(sem(f"moe{n}_loaded{3 * e + 1}"), 16 * it + 16)
                        project(1, up_ps).then_inc(sem("up_used" + n), 1)
                        pe.wait_ge(sem("hid_done" + n), it + 1)
                        for f in range(FC):
                            last = pe.transpose(out_ps[0][:, f * P:(f + 1) * P], hid[:, f * P:(f + 1) * P], ident[:, :])
                        last.then_inc(sem("hidT_psum" + n), 1)
                        pe.wait_ge(sem("oh_done" + n), it + 2)
                        gather(0)
                        gather(1)
                        pe.wait_ge(sem("pT_done" + n), it + 2)
                        pe.wait_ge(sem("hidT_done" + n), it + 1)
                        for e in range(2):
                            pe.wait_ge(sem(f"moe{n}_loaded{3 * e + 2}"), 16 * it + 16)
                        down()
                    pe.wait_ge(sem("out0_done" + n), rounds * NP + 1)
                    pe.wait_ge(sem("out1_done" + n), rounds * NP + 1)
                    scatter(True).then_inc(sem("y_done" + n), 1)

                @block.scalar
                def _(act):
                    rounds = act.value_load(rounds_i[0:1, 0:1], min_val=1, max_val=ROUNDS)

                    def take(half, count):
                        act.wait_ge(sem("gat_psum" + n), count)
                        for c in range(4 * half, 4 * half + 4):
                            last = act.activation(xg[:, c, :], (gate_ps, up_ps)[half][:, (c % 4) * P:(c % 4 + 1) * P],
                                                  ACT.Identity, scale=modc[:, 2 * KC + c:2 * KC + c + 1],
                                                  bias=modc[:, 3 * KC + c:3 * KC + c + 1])
                        last.then_inc(sem("gat_done" + n), 1)
                    take(0, 1)
                    take(1, 2)
                    with act.Fori(0, rounds * NP) as it:
                        act.wait_ge(sem("gate_used" + n), it + 1)
                        act.activation(hid, gate_ps[:, :], ACT.Sigmoid).then_inc(sem("sig_done" + n), 1)
                        take(0, 2 * it + 3)
                        take(1, 2 * it + 4)
                        act.wait_ge(sem("down_used" + n), it + 1)
                        act.activation(outb[:, 512:1024], out_ps[1][:, :], ACT.Copy).then_inc(sem("out1_done" + n), 1)

                @block.vector
                def _(v):
                    rounds = v.value_load(rounds_i[0:1, 0:1], min_val=1, max_val=ROUNDS)

                    def slots_of(col):
                        for e in range(2):
                            for t in range(NT):
                                if isinstance(col, int):
                                    p1, m1, g1 = [a[:, t, col + e:col + e + 1] for a in (pos, mask, gate)]
                                else:
                                    p1, m1, g1 = [a[:, t, bass.ds(col + e, 1)] for a in (pos, mask, gate)]
                                v.tensor_scalar(oh[:, t, e * SLOTS:(e + 1) * SLOTS], slot_ids[:, :], p1, m1,
                                                ALU.is_equal, ALU.mult)
                                last = v.tensor_scalar(ohw[:, t, e * SLOTS:(e + 1) * SLOTS], slot_ids[:, :], p1, g1,
                                                       ALU.is_equal, ALU.mult)
                        last.then_inc(sem("oh_done" + n), 1)

                    def body(it, side):
                        v.wait_ge(sem("sig_done" + n), it + 1)
                        v.tensor_tensor(hid, gate_ps[:, :], hid, ALU.mult).then_inc(sem("silu" + n), 1)
                        v.wait_ge(sem("pT_psum" + n), it + 1)
                        v.tensor_copy(pT, out_ps[1][:, 0:256]).then_inc(sem("pT_done" + n), 1)
                        slots_of(2 * it + 2)
                        v.wait_ge(sem("silu" + n), it + 1)
                        v.wait_ge(sem("up_used" + n), it + 1)
                        v.tensor_tensor(hid, up_ps[:, :], hid, ALU.mult).then_inc(sem("hid_done" + n), 1)
                        v.wait_ge(sem("hidT_psum" + n), it + 1)
                        v.tensor_copy(hidT, out_ps[0][:, :].rearrange("p (f n) -> p f n", f=FC)).then_inc(
                            sem("hidT_done" + n), 1)
                        if side is not None:
                            side(v, it)
                        v.wait_ge(sem("down_used" + n), it + 1)
                        v.tensor_copy(outb[:, 0:512], out_ps[0][:, :]).then_inc(sem("out0_done" + n), 1)

                    v.memset(zero, 0.0).then_inc(sem("moe_zero" + n), 1)
                    v.memset(pT, 0.0).then_inc(sem("pT_done" + n), 1)
                    v.memset(outb[:, 0:512], 0.0).then_inc(sem("out0_done" + n), 1)
                    v.memset(outb[:, 512:1024], 0.0).then_inc(sem("out1_done" + n), 1)
                    slots_of(0)
                    if sides is None:
                        with v.Fori(0, rounds * NP) as it:
                            body(it, None)
                    else:
                        with v.Fori(0, NP) as it:
                            body(it, sides)
                        with v.If(rounds > 1):
                            with v.Fori(NP, rounds * NP) as it:
                                body(it, None)
                        v.nop()
                    v.wait_ge(sem("y_done" + n), 1)
                    for g in range(4):
                        t, h = g // 2, g % 2
                        y = tmp[:, 2304 + (g % 2) * 512:2304 + (g % 2 + 1) * 512]
                        v_step(v.tensor_tensor(y, y_ps[g][:, :], g_b[:, 1, h * 512:(h + 1) * 512], ALU.mult))
                        xs = x3[:, t, h * 512:(h + 1) * 512]
                        ins = v.tensor_tensor(xs, xs, y, ALU.add)
                        if g < 3:
                            v_step(ins)
                        else:
                            ins.then_inc(sem("x_ready"), 1)

        ADA_PER_PAIR = N_ADA_P // 8

        def ada2_side(eng, it):
            sync = eng is nc.sync
            for j in range(ADA_PER_PAIR):
                ws = side[:, j * 2048:(j + 1) * 2048].rearrange("p (c n) -> p c n", c=8)
                if isinstance(it, int):
                    wsrc = inp["ada_w_2"][0][:, (ADA_PER_PAIR * it + j) * AW:(ADA_PER_PAIR * it + j + 1) * AW]
                    a = acc[:, (ADA_PER_PAIR * it + j) * AW:(ADA_PER_PAIR * it + j + 1) * AW]
                elif sync:
                    wsrc = inp["ada_w_2"][0][:, bass.ds(it * (ADA_PER_PAIR * AW) + j * AW, AW)]
                else:
                    a = acc[:, bass.ds(it * (ADA_PER_PAIR * AW) + j * AW, AW)]
                if sync:
                    if not isinstance(it, int):
                        eng.wait_ge(sem(f"ada2_used{j}"), it)
                    eng.dma_start(ws, wsrc.rearrange("(c p) n -> p c n", p=P)).then_inc(sem(f"ada2_loaded{j}"), 16)
                else:
                    eng.wait_ge(sem(f"ada2_loaded{j}"), 16 * it + 16)
                    for c in range(KC):
                        s = cond[:, KC + c:KC + c + 1]
                        if c == 0:
                            ins = eng.tensor_scalar(a, ws[:, c, :], s, None, ALU.mult)
                        else:
                            ins = eng.scalar_tensor_tensor(a, ws[:, c, :], s, a, ALU.mult, ALU.add)
                        if c < KC - 1:
                            ins.then_inc(sem("ada2_chain"), 1)
                            eng.wait_ge(sem("ada2_chain"), it * (ADA_PER_PAIR * (KC - 1)) + j * (KC - 1) + c + 1)
                        else:
                            ins.then_inc(sem(f"ada2_used{j}"), 1)

        route(0, 16, True)
        if until > 4:
            experts(0, 16, inp["expert_w_gate"][0], inp["expert_w_up"][0], inp["expert_w_down"][0], sides=ada2_side,
                    more_loads=lambda sp: sp.dma_start(
                        g_b[:, 0, :], inp["norm_final"].rearrange("(a n) -> a n", a=1).broadcast_to((P, D))).then_inc(
                            sem("nf_loaded"), 16))
        if debug and until <= 5:
            debug(nc, sem, locals())
            return

        give_back()
        w_in = inp["w_in_2"][0]
        MIX_CELLS = 4
        SH0 = 1064
        GA0 = SH0 + 1824
        pieces = [(0, 512), (512, 1024), (SH0, SH0 + 512), (SH0 + 512, SH0 + 1024), (SH0 + 1024, SH0 + 1536),
                  (SH0 + 1536, GA0)]
        LORA, GATE0, BRA, BRR, OUT0 = 6, 7, 11, 12, 13

        def p2_wait(sp, i):
            if i >= MIX_CELLS:
                sp.wait_ge(sem("p2_used"), i - MIX_CELLS + 1)

        def p2_load(sp, i, dst, src):
            sp.dma_start(dst, src).then_inc(sem(f"p2_loaded{i % MIX_CELLS}"), 16)

        p2_loads = {}
        count = [0] * MIX_CELLS
        for i in range(15):
            count[i % MIX_CELLS] += 5 if i == LORA else 1
            p2_loads[i] = 16 * count[i % MIX_CELLS]

        def p2_ready(pe, i):
            pe.wait_ge(sem(f"p2_loaded{i % MIX_CELLS}"), p2_loads[i])

        def p2(i, kc=8, w=512):
            return cell(i % MIX_CELLS, kc, w)

        q_tok = tmp[:, 0:1024].rearrange("p (t d) -> p t d", t=NT)
        kvl = tmp[:, 1024:1536].rearrange("p (t d) -> p t d", t=NT)
        qiT = tmp[:, 1536:2048].rearrange("p (c s) -> p c s", c=2)
        kiT = tmp[:, 2048:2304]
        wi_w = tmp[:, 3008:3072].rearrange("p (c n) -> p c n", c=KC)
        krep = tmp[:, 3072:4096].rearrange("p (c n) -> p c n", c=KC)
        w_idx = small[:, 24:40]
        omm = small[:, 40:55]
        mixed = ring[:, 4 * CELL:4 * CELL + 15 * S].rearrange("p (c s) -> p c s", c=15)
        lora = p2(LORA, 1, 4096)[:, 0, :]
        M_STRICT, M_INCL = pos_t[:, 0:P], pos_t[:, P:2 * P]
        M_16, M_OFF = mask_t[:, 0:P], mask_t[:, P:2 * P]
        M_16L = gate_t[:, 0:P]
        chunk_of = gate_t[:, P:P + 4]

        with nc.Block() as block:
            @block.sync
            def _(sp):
                for i in range(4):
                    p2_load(sp, i, p2(i), w_cols(w_in, *pieces[i]))
                for i, m in enumerate((2, 5)):
                    sp.dma_start(side[:, i * D:(i + 1) * D], inp["ada_b_2"][0:1, m * D:(m + 1) * D].broadcast_to((P, D))).then_inc(
                        sem("gb2_loaded"), 16)
                for r in range(4):
                    sp.dma_start(krep[:, :, r * 32:(r + 1) * 32], w_cols(w_in, 1024, 1056)).then_inc(sem("ki_loaded"), 16)
                sp.dma_start(wi_w, w_cols(w_in, 1056, 1064)).then_inc(sem("ki_loaded"), 16)
                p2_wait(sp, 4)
                p2_load(sp, 4, p2(4), w_cols(w_in, *pieces[4]))
                p2_wait(sp, 5)
                p2_load(sp, 5, p2(5)[:, :, 0:288], w_cols(w_in, *pieces[5]))
                p2_wait(sp, LORA)
                sp.wait_ge(sem("lora_zero"), 1)
                p2_load(sp, LORA, lora[0:64, 0:512], inp["rwkv_w2_2"][0])
                p2_load(sp, LORA, lora[64:128, 0:512], inp["rwkv_a2_2"][0])
                p2_load(sp, LORA, lora[:, 512:1024], inp["rwkv_g2_2"][0][0:128, :])
                p2_load(sp, LORA, lora[0:32, 1024:1536], inp["rwkv_g2_2"][0][128:160, :])
                p2_load(sp, LORA, lora[:, 1536:3584].rearrange("p (c n) -> p c n", c=2),
                        inp["w_kv_up_2"][0].rearrange("(c p) n -> p c n", p=P))
                p2_wait(sp, GATE0)
                p2_load(sp, GATE0, p2(GATE0), w_cols(w_in, GA0, GA0 + 512))

            @block.gpsimd
            def _(pool):
                pool.memset(mixed[:, 14, :], 0.0).then_inc(sem("mixed_zero"), 1)
                pool.wait_ge(sem("mixed_zero"), 1)
                for m in (M_STRICT, M_INCL, M_16, M_OFF, M_16L, chunk_of):
                    p_step(pool.memset(m, 0.0 if m is M_OFF else 1.0))

                def block_mask(m, size, upper, strict):
                    v3_ = m.rearrange("p (b n) -> p b n", n=size)
                    s_ = 1 if upper else -1
                    p_step(pool.affine_select(out=v3_, in_=v3_, compare_op=ALU.is_gt if strict else ALU.is_ge, fill=0.0,
                                              base=0, pattern=[[s_ * size, P // size], [s_, size]], channel_multiplier=-s_))
                    p_step(pool.affine_select(out=v3_, in_=v3_, compare_op=ALU.is_ge, fill=0.0, base=0,
                                              pattern=[[-size, P // size], [0, size]], channel_multiplier=1))
                    p_step(pool.affine_select(out=v3_, in_=v3_, compare_op=ALU.is_gt, fill=0.0, base=size,
                                              pattern=[[size, P // size], [0, size]], channel_multiplier=-1))
                block_mask(M_STRICT, 32, True, True)
                block_mask(M_INCL, 32, True, False)
                block_mask(M_16, 16, True, True)
                block_mask(M_16L, 16, False, True)
                p_step(pool.tensor_tensor(M_OFF, M_STRICT, M_16, ALU.subtract))
                p_step(pool.affine_select(out=chunk_of, in_=chunk_of, compare_op=ALU.is_ge, fill=0.0, base=0,
                                          pattern=[[-32, 4]], channel_multiplier=1))
                p_step(pool.affine_select(out=chunk_of, in_=chunk_of, compare_op=ALU.is_gt, fill=0.0, base=32,
                                          pattern=[[32, 4]], channel_multiplier=-1))
                pool.wait_ge(sem("p2_used"), LORA - MIX_CELLS + 1)
                pool.memset(lora[:, 1024:1536], 0.0).then_inc(sem("lora_zero"), 1)

            @block.tensor
            def _(pe):
                done = ("ada2_used0", 8)
                pe.wait_ge(sem("ada2_used1"), 8)
                pe.wait_ge(sem("ada2_used2"), 8)
                ada_columns(pe, (0, 1), 1, "modc_psum", done)
                ada_columns(pe, (3, 4), 2, "modc_psum", done)
                hT_tensor(pe, 2)
                pe.wait_ge(sem("hT_done"), 3 * KC)
                for t in range(NT):
                    if t == 0:
                        p2_ready(pe, 0)
                    for c in range(KC):
                        last = pe.matmul(ps[t][:, :], hT[:, c, t * P:(t + 1) * P], p2(0)[:, c, :], start=(c == 0), stop=(c == KC - 1))
                    last.then_inc(sem("pj_q"), 1)
                last_q = last
                p2_ready(pe, 1)
                for t in range(NT):
                    for c in range(KC):
                        last = pe.matmul(ps[2][:, t * S:(t + 1) * S], hT[:, c, t * P:(t + 1) * P], p2(1)[:, c, 0:S],
                                         start=(c == 0), stop=(c == KC - 1))
                last.then_inc(sem("pj_kv"), 1)
                for j in range(2):
                    for c in range(KC):
                        last = pe.matmul(ps[3][:, j * S:(j + 1) * S], p2(1)[:, c, S + j * P:S + (j + 1) * P], hT[:, c, :],
                                         start=(c == 0), stop=(c == KC - 1))
                last.then_inc(sem("pj_qi"), 1)
                pe.wait_ge(sem("ki_loaded"), 80)
                pe.wait_ge(sem("hT_done"), 3 * KC)
                for c in range(KC):
                    last = pe.matmul(ps[4][:, 0:S], krep[:, c, :], hT[:, c, :], start=(c == 0), stop=(c == KC - 1))
                for t in range(NT):
                    for c in range(KC):
                        last = pe.matmul(ps[4][:, S + t * 8:S + (t + 1) * 8], hT[:, c, t * P:(t + 1) * P], wi_w[:, c, :],
                                         start=(c == 0), stop=(c == KC - 1))
                last.then_inc(sem("pj_ki"), 1)
                pe.wait_ge(sem("pj_q_out"), 2)
                ada_rows(pe, 2, 0, "g_psum", done)
                pe.wait_ge(sem("g_out"), 3)
                ada_rows(pe, 5, 0, "g_psum", done)
                pe.wait_ge(sem("g_out"), 4)
                pe.wait_ge(sem("pj_kv_out"), 1)
                pe.wait_ge(sem("pj_qi_out"), 1)
                for i in range(2):
                    pe.matmul(ps[5][:, 0:1], ident[:, :], ones[:, 0:1], start=True, stop=True).then_inc(sem("p2_used"), 1)
                for m in range(15):
                    i = 2 + m // 4 if m < 12 else 5
                    o = (m % 4) * P if m < 12 else (m - 12) * P
                    n = 32 if m == 14 else P
                    if o == 0:
                        p2_ready(pe, i)
                    if m >= 4:
                        pe.wait_ge(sem("mixed_done"), m - 3)
                    for c in range(KC):
                        last = pe.matmul(ps[m % 4][0:n, 0:S], p2(i)[:, c, o:o + n], hT[:, c, :], start=(c == 0), stop=(c == KC - 1))
                    last.then_inc(sem("pj_shift"), 1)
                    if m in (3, 7, 11, 14):
                        pe.matmul(ps[5][:, 0:1], ident[:, :], ones[:, 0:1], start=True, stop=True).then_inc(sem("p2_used"), 1)

            @block.scalar
            def _(act):
                rms_scalar(act, 2, xn_sb)
                rms_scalar(act, 3, xn_sb)
                for t in range(NT):
                    act.wait_ge(sem("pj_q"), t + 1)
                    act.activation(q_tok[:, t, :], ps[t][:, :], ACT.Copy).then_inc(sem("pj_q_out"), 1)
                act.wait_ge(sem("pj_kv"), 1)
                act.activation(tmp[:, 1024:1536], ps[2][:, :], ACT.Copy).then_inc(sem("pj_kv_out"), 1)
                act.wait_ge(sem("pj_qi"), 1)
                act.activation(tmp[:, 1536:2048], ps[3][:, :], ACT.Copy).then_inc(sem("pj_qi_out"), 1)
                act.wait_ge(sem("pj_ki"), 1)
                act.activation(kiT, ps[4][:, 0:S], ACT.Copy).then_inc(sem("pj_ki_out"), 1)
                act.activation(w_idx, ps[4][:, S:S + 16], ACT.Copy, scale=1.0 / 16.0).then_inc(sem("pj_ki_out"), 1)
                act.wait_ge(sem("omm"), 1)
                act.wait_ge(sem("mixed_zero"), 1)
                for m in range(15):
                    n = 32 if m == 14 else P
                    act.wait_ge(sem("pj_shift"), m + 1)
                    act.activation(mixed[0:n, m, :], ps[m % 4][0:n, 0:S], ACT.Copy, scale=omm[0:n, m:m + 1]).then_inc(
                        sem("mixed_own"), 1)

            @block.vector
            def _(v):
                v.wait_ge(sem("nf_loaded"), 16)
                rms_vector(v, 2, x3, weight=g_b[:, 0, :], name="x_ready")
                rms_vector(v, 3, xn3)
                v.wait_ge(sem("modc_psum"), 3)
                fill_modc(v, 0, KC, ps[1], 0, KC, colA("mix_norm_g_2", 0, KC), colB("ada_b_2", 0, KC), colB("ada_b_2", KC, KC))
                v.wait_ge(sem("modc_psum"), 4)
                fill_modc(v, 2 * KC, 3 * KC, ps[2], 0, KC, colA("moe_norm_g_2", 0, KC), colB("ada_b_2", 3 * KC, KC),
                          colB("ada_b_2", 4 * KC, KC))
                v.tensor_copy(small[:, 20:21], small[:, 14:15]).then_inc(sem("mod_done"), 1)
                hT_vector(v, 2)
                v.tensor_scalar(omm, colsB[:, MU0:MU0 + 15], -1.0, 1.0, ALU.mult, ALU.add).then_inc(sem("omm"), 1)
                v.wait_ge(sem("gb2_loaded"), 32)
                for i in range(2):
                    v.wait_ge(sem("g_psum"), i + 3)
                    for n in range(2):
                        a = g_b[:, i, n * 512:(n + 1) * 512]
                        ins = v.tensor_tensor(a, ps[n][:, :], side[:, i * D + n * 512:i * D + (n + 1) * 512], ALU.add)
                    ins.then_inc(sem("g_out"), 1)
                for m in range(15):
                    n = 32 if m == 14 else P
                    v.wait_ge(sem("mixed_own"), m + 1)
                    a = mixed[0:n, m, 1:S]
                    v.scalar_tensor_tensor(a, ps[m % 4][0:n, 0:S - 1], colsB[0:n, MU0 + m:MU0 + m + 1], a, ALU.mult, ALU.add).then_inc(
                        sem("mixed_done"), 1)

        if debug and until <= 6:
            debug(nc, sem, locals())
            return

        give_back()
        k_tok = side[:, 0:1024].rearrange("p (t d) -> p t d", t=NT)
        vv_tok = side[:, 1024:2048].rearrange("p (t d) -> p t d", t=NT)
        qT2 = side[:, 2048:3072].rearrange("p (c s) -> p c s", c=4)
        kT2 = side[:, 3072:4096].rearrange("p (c s) -> p c s", c=4)
        latT = side[:, 4096:4608].rearrange("p (c s) -> p c s", c=2)
        work = side[:, 4608:5120].rearrange("p (t s) -> p t s", t=NT)
        drop = side[:, 5120:5632].rearrange("p (t s) -> p t s", t=NT)
        dst2 = side[:, 5632:6144].rearrange("p (t s) -> p t s", t=NT)
        o_tok = side[:, 6144:7168].rearrange("p (t d) -> p t d", t=NT)
        oaT = side[:, 7168:8192].rearrange("p (c s) -> p c s", c=4)
        sq6 = acc[:, 0:1024]
        rl = acc[:, 1024:2048].rearrange("p (b s) -> p b s", b=4)
        lg = acc[:, 2048:2560].rearrange("p (b s) -> p b s", b=2)
        ee = acc[:, 2560:3072].rearrange("p (b s) -> p b s", b=2)
        eT = acc[:, 3072:3584].rearrange("p (b s) -> p b s", b=2)
        st6 = acc[:, 3584:3840]
        TAKEN = -3.3e38
        TOPK = 64
        kv_up = lora[:, 1536:3584].rearrange("p (c n) -> p c n", c=2)

        with nc.Block() as block:
            @block.gpsimd
            def _(pool):
                pool.iota(dst2, pattern=[[P, NT], [-1, S]], base=0, channel_multiplier=1,
                          allow_small_or_imprecise_dtypes=True).then_inc(sem("dst2"), 1)
                for t in range(NT):
                    pool.wait_ge(sem("idx_score"), t + 1)
                    pool.affine_select(out=work[:, t, :], in_=work[:, t, :], compare_op=ALU.is_ge, fill=-BIG, base=t * P,
                                       pattern=[[-1, S]], channel_multiplier=1).then_inc(sem("idx_causal"), 1)
                pool.wait_ge(sem("drop_raw"), 1)
                for t in range(NT):
                    pool.affine_select(out=drop[:, t, :], in_=drop[:, t, :], compare_op=ALU.is_ge, fill=-1.0, base=t * P,
                                       pattern=[[-1, S]], channel_multiplier=1).then_inc(sem("drop"), 1)

            @block.tensor
            def _(pe):
                def dots(u):
                    t, h = u // 8, u % 8
                    r = 32 * (h % 4)
                    if u >= 4:
                        pe.wait_ge(sem("idx_relu"), u - 3)
                    pe.matmul(ps[h % 4][:, 0:S], qiT[r:r + 32, h // 4, t * P:(t + 1) * P], kiT[r:r + 32, :],
                              start=True, stop=True).then_inc(sem("idx_dots"), 1)
                for u in range(4):
                    dots(u)
                pe.wait_ge(sem("lat_normed"), 1)
                for c in range(2):
                    for t in range(NT):
                        last = pe.transpose(ps[4][:, c * S + t * P:c * S + (t + 1) * P], kvl[:, t, c * P:(c + 1) * P], ident[:, :])
                last.then_inc(sem("lat_psum"), 1)
                pe.wait_ge(sem("q_normed"), 1)
                for c in range(4):
                    for t in range(NT):
                        last = pe.transpose(ps[5 + c // 2][:, (c % 2) * S + t * P:(c % 2) * S + (t + 1) * P],
                                            q_tok[:, t, c * P:(c + 1) * P], ident[:, :])
                last.then_inc(sem("q_psum"), 1)
                for u in range(4, 8):
                    dots(u)
                p2_ready(pe, LORA)
                pe.wait_ge(sem("latT_done"), 2)
                for n in range(2):
                    for t in range(NT):
                        if n == 0 and t == 1:
                            pe.wait_ge(sem("latT_done"), 2)
                        if n == 1:
                            pe.wait_ge(sem("kv_out"), t + 1)
                            if t == 0:
                                pe.wait_ge(sem("qT_done"), 4)
                        b = ps[7] if (t == 0) else ps[4]
                        for c in range(2):
                            last = pe.matmul(b[:, :], latT[:, c, t * P:(t + 1) * P], kv_up[:, c, n * 512:(n + 1) * 512],
                                             start=(c == 0), stop=(c == 1))
                        last.then_inc(sem("kv_psum"), 1)
                for u in range(8, 16):
                    dots(u)
                pe.wait_ge(sem("k_normed"), 1)
                for c in range(4):
                    for t in range(NT):
                        last = pe.transpose(ps[5 + c // 2][:, (c % 2) * S + t * P:(c % 2) * S + (t + 1) * P],
                                            k_tok[:, t, c * P:(c + 1) * P], ident[:, :])
                last.then_inc(sem("k_psum"), 1)

                def scores(u):
                    h, t = u // NT, u % NT
                    jo = (h % 2) * 64
                    if u == 0:
                        pe.wait_ge(sem("kT_done"), 4)
                        pe.wait_ge(sem("idx_relu"), 16)
                    if u >= 4:
                        pe.wait_ge(sem("sa_biased"), u - 3)
                    pe.matmul(ps[u % 4][:, 0:S], qT2[jo:jo + 64, h // 2, t * P:(t + 1) * P], kT2[jo:jo + 64, h // 2, :],
                              start=True, stop=True).then_inc(sem("sa_scores"), 1)

                def turn(u):
                    pe.wait_ge(sem("sa_exp"), u + 1)
                    if u >= 2:
                        pe.wait_ge(sem("sa_eT"), u - 1)
                    if u == 0:
                        pe.wait_ge(sem("kv_out"), 4)
                    for k in range(2):
                        last = pe.transpose(ps[4 + u % 2][:, k * P:(k + 1) * P], ee[:, u % 2, k * P:(k + 1) * P], ident[:, :])
                    last.then_inc(sem("sa_eT_psum"), 1)

                def av(u):
                    h = u // NT
                    pe.wait_ge(sem("sa_eT"), u + 1)
                    if u >= 2:
                        pe.wait_ge(sem("sa_o"), u - 1)
                    for k in range(2):
                        last = pe.matmul(ps[6 + u % 2][:, 0:64], eT[:, u % 2, k * P:(k + 1) * P],
                                         vv_tok[:, k, h * 64:(h + 1) * 64], start=(k == 0), stop=(k == 1))
                    last.then_inc(sem("sa_av"), 1)
                scores(0)
                scores(1)
                for u in range(17):
                    if u + 2 < 16:
                        scores(u + 2)
                    if u < 16:
                        turn(u)
                    if u >= 1:
                        av(u - 1)
                pe.wait_ge(sem("sa_o"), 16)
                pe.wait_ge(sem("sa_eT"), 16)
                for c in range(4):
                    for t in range(NT):
                        last = pe.transpose(ps[4 + c // 2][:, (c % 2) * S + t * P:(c % 2) * S + (t + 1) * P],
                                            o_tok[:, t, c * P:(c + 1) * P], ident[:, :])
                last.then_inc(sem("oa_psum"), 1)

            @block.scalar
            def _(act):
                for t in range(NT):
                    act.activation(sq6[:, t * S:(t + 1) * S], kvl[:, t, :], ACT.Square,
                                   accum_out=st6[:, t:t + 1]).then_inc(sem("lat_sq"), 1)
                act.wait_ge(sem("lat_ms"), 1)
                act.activation(st6[:, 4:6], st6[:, 2:4], ACT.Sqrt).then_inc(sem("lat_root"), 1)
                act.activation(acc[:, 4096:5120], tmp[:, 0:1024], ACT.Square).then_inc(sem("q_sq"), 1)
                act.wait_ge(sem("q_ms"), 1)
                act.activation(st6[:, 32:48], st6[:, 16:32], ACT.Sqrt).then_inc(sem("q_root"), 1)

                def relu(u):
                    act.wait_ge(sem("idx_dots"), u + 1)
                    if u >= 4:
                        act.wait_ge(sem("idx_added"), u - 3)
                    act.activation(rl[:, u % 4, :], ps[u % 4][:, 0:S], ACT.Relu).then_inc(sem("idx_relu"), 1)
                for u in range(8):
                    relu(u)
                for i in range(4):
                    n, t = i // 2, i % 2
                    act.wait_ge(sem("kv_psum"), i + 1)
                    act.activation((k_tok, vv_tok)[n][:, t, :], (ps[7] if t == 0 else ps[4])[:, :], ACT.Copy).then_inc(
                        sem("kv_out"), 1)
                act.wait_ge(sem("kv_out"), 2)
                act.activation(sq6, side[:, 0:1024], ACT.Square).then_inc(sem("k_sq"), 1)
                act.wait_ge(sem("k_ms"), 1)
                act.activation(st6[:, 64:80], st6[:, 48:64], ACT.Sqrt).then_inc(sem("k_root"), 1)
                for u in range(8, 16):
                    relu(u)
                for u in range(17):
                    if u < 16:
                        act.wait_ge(sem("sa_max"), u + 1)
                        if u >= 2:
                            act.wait_ge(sem("sa_eT_psum"), u - 1)
                        act.activation(ee[:, u % 2, :], lg[:, u % 2, :], ACT.Exp, bias=st6[:, 96 + u:97 + u],
                                       accum_out=st6[:, 112 + u:113 + u]).then_inc(sem("sa_exp"), 1)
                    if u >= 1:
                        act.wait_ge(sem("sa_eT_psum"), u)
                        if u >= 3:
                            act.wait_ge(sem("sa_av"), u - 2)
                        act.activation(eT[:, (u - 1) % 2, :], ps[4 + (u - 1) % 2][:, 0:S], ACT.Copy).then_inc(sem("sa_eT"), 1)

            @block.vector
            def _(v):
                v_step(v.tensor_scalar(qk_cols[:, 1:2], colsB[:, nB:nB + 1], 0.125, None, ALU.mult))
                v.wait_ge(sem("lat_sq"), 2)
                v.tensor_scalar(st6[:, 2:4], st6[:, 0:2], 1.0 / S, EPS, ALU.mult, ALU.add).then_inc(sem("lat_ms"), 1)
                v.wait_ge(sem("lat_root"), 1)
                v_step(v.reciprocal(st6[:, 6:8], st6[:, 4:6]))
                v.tensor_tensor(kvl, kvl, st6[:, 6:8].unsqueeze(2).broadcast_to((P, NT, S)), ALU.mult).then_inc(sem("lat_normed"), 1)

                def head_norm(sq, st, sq_sem, ms_sem, root_sem, a, done):
                    v.wait_ge(sem(sq_sem), 1)
                    v_step(v.tensor_reduce(st6[:, st:st + 16], sq.rearrange("p (g d) -> p g d", d=64), X, ALU.add))
                    v.tensor_scalar(st6[:, st:st + 16], st6[:, st:st + 16], 1.0 / 64, EPS, ALU.mult, ALU.add).then_inc(sem(ms_sem), 1)
                    v.wait_ge(sem(root_sem), 1)
                    v_step(v.reciprocal(st6[:, st:st + 16], st6[:, st + 16:st + 32]))
                    g = a.rearrange("p (g d) -> p g d", d=64)
                    v.tensor_tensor(g, g, st6[:, st:st + 16].unsqueeze(2).broadcast_to((P, 16, 64)), ALU.mult).then_inc(sem(done), 1)
                head_norm(acc[:, 4096:5120], 16, "q_sq", "q_ms", "q_root", tmp[:, 0:1024], "q_normed")
                v.wait_ge(sem("lat_psum"), 1)
                for c in range(2):
                    v.tensor_scalar(latT[:, c, :], ps[4][:, c * S:(c + 1) * S], colB("kv_norm_g_2", c), None, ALU.mult).then_inc(
                        sem("latT_done"), 1)
                v.wait_ge(sem("q_psum"), 1)
                for c in range(4):
                    v.tensor_scalar(qT2[:, c, :], ps[5 + c // 2][:, (c % 2) * S:(c % 2 + 1) * S], qk_cols[:, 1:2], None,
                                    ALU.mult).then_inc(sem("qT_done"), 1)

                def add_head(u):
                    t, h = u // 8, u % 8
                    v.wait_ge(sem("idx_relu"), u + 1)
                    w = w_idx[:, t * 8 + h:t * 8 + h + 1]
                    if h == 0:
                        ins = v.tensor_scalar(work[:, t, :], rl[:, u % 4, :], w, None, ALU.mult)
                    else:
                        ins = v.scalar_tensor_tensor(work[:, t, :], rl[:, u % 4, :], w, work[:, t, :], ALU.mult, ALU.add)
                    ins.then_inc(sem("idx_added"), 1)
                    v.wait_ge(sem("idx_added"), u + 1)
                    if h == 7:
                        v.tensor_copy(st6[:, 200 + t:201 + t], work[:, t, 0:1]).then_inc(sem("idx_score"), 1)
                for u in range(8):
                    add_head(u)
                head_norm(sq6, 48, "k_sq", "k_ms", "k_root", side[:, 0:1024], "k_normed")
                for u in range(8, 16):
                    add_head(u)
                v.wait_ge(sem("k_psum"), 1)
                for c in range(4):
                    v.tensor_scalar(kT2[:, c, :], ps[5 + c // 2][:, (c % 2) * S:(c % 2 + 1) * S], colsB[:, nB + 1:nB + 2], None,
                                    ALU.mult).then_inc(sem("kT_done"), 1)
                for r in range(TOPK // 8):
                    for t in range(NT):
                        if r == 0:
                            v.wait_ge(sem("idx_causal"), t + 1)
                        top = st6[:, 160 + 8 * t:168 + 8 * t]
                        v_step(v.max(top, work[:, t, :]))
                        v_step(v.match_replace(work[:, t, :], top, work[:, t, :], TAKEN))
                v.tensor_scalar(drop, work, TAKEN, 1.0, ALU.is_equal, ALU.subtract).then_inc(sem("drop_raw"), 1)
                v.wait_ge(sem("dst2"), 1)
                v.wait_ge(sem("drop"), 2)

                def first(u):
                    h, t = u // NT, u % NT
                    b = lg[:, u % 2, :]
                    v.wait_ge(sem("sa_scores"), u + 1)
                    v.scalar_tensor_tensor(b, dst2[:, t, :], -2.0 ** -(h + 1), ps[u % 4][:, 0:S], ALU.mult, ALU.add).then_inc(
                        sem("sa_biased"), 1)
                    v.wait_ge(sem("sa_biased"), u + 1)
                    v_step(v.scalar_tensor_tensor(b, drop[:, t, :], 1.0e30, b, ALU.mult, ALU.add))
                    v_step(v.tensor_reduce(st6[:, 208 + u % 2:209 + u % 2], b, X, ALU.max))
                    v.tensor_scalar(st6[:, 96 + u:97 + u], st6[:, 208 + u % 2:209 + u % 2], -1.0, None, ALU.mult).then_inc(
                        sem("sa_max"), 1)

                def last_(u):
                    h, t = u // NT, u % NT
                    v.wait_ge(sem("sa_av"), u + 1)
                    v_step(v.reciprocal(st6[:, 128 + u:129 + u], st6[:, 112 + u:113 + u]))
                    v.tensor_scalar(o_tok[:, t, h * 64:(h + 1) * 64], ps[6 + u % 2][:, 0:64], st6[:, 128 + u:129 + u], None,
                                    ALU.mult).then_inc(sem("sa_o"), 1)
                first(0)
                for u in range(17):
                    if u + 1 < 16:
                        if u >= 1:
                            v.wait_ge(sem("sa_exp"), u)
                        first(u + 1)
                    if u >= 1:
                        last_(u - 1)
                v.wait_ge(sem("oa_psum"), 1)
                for c in range(4):
                    v.tensor_copy(oaT[:, c, :], ps[4 + c // 2][:, (c % 2) * S:(c % 2 + 1) * S])

        if debug and until <= 7:
            debug(nc, sem, locals())
            return

        C = 32
        NC = S // C
        r_, k_, v_ = [mixed[:, 4 * i:4 * i + 4, :] for i in range(3)]
        c5 = 5 * CELL

        def ch4(a):
            return a.rearrange("p (c s) -> p c s", c=4)
        aa, LL, kk, gg = [ring[:, c5 + i * 1024:c5 + (i + 1) * 1024] for i in range(4)]
        eP, ePrev, eN, bonus, t1, t2_ = [acc[:, i * 1024:(i + 1) * 1024] for i in range(6)]
        tl = tmp[:, :].rearrange("p (w c s) -> p w c s", w=4, c=4)
        rT_, aT_, kT_, bT_ = [tmp[:, i * 1024:(i + 1) * 1024] for i in range(4)]
        toks = side[:, 0:4096].rearrange("p (w t d) -> p w t d", w=4, t=NT)
        v_tk, k_tk, b_tk, a_tk = [toks[:, i, :, :] for i in range(4)]
        tw = side[:, 4096:4352]
        sgl = side[:, 4352:4864].rearrange("p (c s) -> p c s", c=2)
        omka = small[:, 56:60]
        wC = colsB[:, NB_ALL:NB_ALL + 32].rearrange("p (c n) -> p c n", c=4)
        assert NB_ALL + 32 <= P
        EXPM = math.exp(-0.5)

        with nc.Block() as block:
            @block.gpsimd
            def _(pool):
                p_step(pool.memset(t1, 1.0))
                pool.memset(t1.rearrange("p (n c) -> p n c", c=C)[:, :, 0:1], 0.0).then_inc(sem("scan_mask"), 1)

            @block.tensor
            def _(pe):
                pe.wait_ge(sem("tanh"), 1)
                for c in range(4):
                    last = pe.matmul(ps[c // 2][:, (c % 2) * S:(c % 2 + 1) * S], lora[0:64, c * P:(c + 1) * P], tw[0:64, :],
                                     start=True, stop=True)
                last.then_inc(sem("w_psum"), 1)
                for c in range(4):
                    last = pe.matmul(ps[2 + c // 2][:, (c % 2) * S:(c % 2 + 1) * S], lora[64:128, c * P:(c + 1) * P],
                                     mixed[64:128, 12, :], start=True, stop=True)
                last.then_inc(sem("a_psum"), 1)
                pe.wait_ge(sem("sgl"), 1)
                for c in range(4):
                    for k in range(2):
                        last = pe.matmul(ps[4 + c // 2][:, (c % 2) * S:(c % 2 + 1) * S],
                                         lora[:, 512 * (k + 1) + c * P:512 * (k + 1) + (c + 1) * P], sgl[:, k, :],
                                         start=(k == 0), stop=(k == 1))
                last.then_inc(sem("gate_psum"), 1)
                pe.wait_ge(sem("kk_sq"), 1)
                for n in range(2):
                    last = pe.matmul(ps[6 + n][:, :], headones[:, :], t2_[:, n * 512:(n + 1) * 512], start=True, stop=True)
                last.then_inc(sem("kk_psum"), 1)
                pe.wait_ge(sem("wa_out"), 8)

                def turn(w, src, banks, name):
                    for c in range(4):
                        for t in range(NT):
                            last = pe.transpose(ps[banks + t][:, c * P:(c + 1) * P], ch4(src)[:, c, t * P:(t + 1) * P], ident[:, :])
                    last.then_inc(sem("tok_psum"), 1)
                turn(0, ring[:, 4 * CELL + 2048:4 * CELL + 3072], 0, "v")
                pe.wait_ge(sem("rk_done"), 1)
                pe.wait_ge(sem("kk_root"), 1)
                for n in range(2):
                    last = pe.matmul(ps[6 + n][:, :], headones[:, :], t2_[:, n * 512:(n + 1) * 512], start=True, stop=True)
                last.then_inc(sem("bonus_psum"), 1)
                pe.wait_ge(sem("tilde"), 1)
                turn(1, kT_, 2, "k")
                pe.wait_ge(sem("tilde"), 2)
                pe.wait_ge(sem("gate_out"), 1)
                turn(2, bT_, 4, "b")
                pe.wait_ge(sem("tilde"), 3)
                pe.wait_ge(sem("tok_out"), 1)
                turn(3, aT_, 0, "a")

            @block.scalar
            def _(act):
                act.activation(tw[0:64, :], mixed[0:64, 12, :], ACT.Tanh).then_inc(sem("tanh"), 1)
                act.activation(sgl, mixed[:, 13:15, :], ACT.Sigmoid).then_inc(sem("sgl"), 1)
                act.wait_ge(sem("w_psum"), 1)
                for c in range(4):
                    act.activation(ch4(ePrev)[:, c, :], ps[c // 2][:, (c % 2) * S:(c % 2 + 1) * S], ACT.Sigmoid,
                                   bias=colB("rwkv_w0_2", c)).then_inc(sem("wa_out"), 1)
                act.wait_ge(sem("a_psum"), 1)
                for c in range(4):
                    act.activation(ch4(aa)[:, c, :], ps[2 + c // 2][:, (c % 2) * S:(c % 2 + 1) * S], ACT.Sigmoid,
                                   bias=colB("rwkv_a0_2", c)).then_inc(sem("wa_out"), 1)
                act.wait_ge(sem("gate_psum"), 1)
                for n in range(2):
                    last = act.activation(gg[:, n * 512:(n + 1) * 512], ps[4 + n][:, :], ACT.Copy)
                last.then_inc(sem("gate_out"), 1)
                act.wait_ge(sem("kk_psum"), 1)
                for n in range(2):
                    last = act.activation(bonus[:, n * 512:(n + 1) * 512], ps[6 + n][:, :], ACT.Sqrt)
                last.then_inc(sem("kk_root"), 1)
                act.wait_ge(sem("tok_psum"), 1)

                def tok(w, banks):
                    act.wait_ge(sem("tok_psum"), w + 1)
                    for t in range(NT):
                        last = act.activation(toks[:, w, t, :], ps[banks + t][:, :], ACT.Copy)
                    last.then_inc(sem("tok_out"), 1)
                tok(0, 0)
                act.wait_ge(sem("logdecay"), 1)
                act.activation(eP, LL, ACT.Exp).then_inc(sem("eP"), 1)
                act.activation(eN, LL, ACT.Exp, scale=-1.0).then_inc(sem("eN"), 1)
                act.wait_ge(sem("logprev"), 1)
                act.activation(ePrev, ePrev, ACT.Exp).then_inc(sem("ePrev"), 1)
                tok(1, 2)
                tok(2, 4)
                tok(3, 0)

            @block.vector
            def _(v):
                v_step(v.tensor_scalar(omka, colB("rwkv_k_a_2", 0, 4), -1.0, 1.0, ALU.mult, ALU.add))
                for c in range(4):
                    ins = v.tensor_scalar(ch4(kk)[:, c, :], k_[:, c, :], colB("rwkv_k_k_2", c), None, ALU.mult)
                v_step(ins)
                v.tensor_tensor(t2_, kk, kk, ALU.mult).then_inc(sem("kk_sq"), 1)
                v.wait_ge(sem("wa_out"), 4)
                v_step(v.tensor_scalar(ePrev, ePrev, -EXPM, None, ALU.mult))
                v.wait_ge(sem("scan_mask"), 1)
                v.tensor_tensor_scan(LL, t1, ePrev, 0.0, ALU.mult, ALU.add).then_inc(sem("logdecay"), 1)
                v.wait_ge(sem("logdecay"), 1)
                v.tensor_tensor(ePrev, LL, ePrev, ALU.subtract).then_inc(sem("logprev"), 1)
                v.wait_ge(sem("wa_out"), 8)
                for c in range(4):
                    ins = v.tensor_scalar(ch4(t1)[:, c, :], ch4(aa)[:, c, :], colB("rwkv_k_a_2", c), omka[:, c:c + 1],
                                          ALU.mult, ALU.add)
                v_step(ins)
                v_step(v.tensor_tensor(k_, k_, ch4(t1), ALU.mult))
                v.wait_ge(sem("kk_root"), 1)
                v_step(v.tensor_scalar(bonus, bonus, 1e-12, None, ALU.max))
                v_step(v.reciprocal(bonus, bonus))
                v_step(v.tensor_tensor(kk, kk, bonus, ALU.mult))
                for c in range(4):
                    ins = v.scalar_tensor_tensor(ch4(t2_)[:, c, :], k_[:, c, :], colB("rwkv_r_k_2", c), r_[:, c, :],
                                                 ALU.mult, ALU.mult)
                ins.then_inc(sem("rk_done"), 1)
                v.wait_ge(sem("eN"), 1)
                v.tensor_tensor(ch4(kT_), k_, ch4(eN), ALU.mult).then_inc(sem("tilde"), 1)
                v_step(v.tensor_tensor(t1, kk, aa, ALU.mult))
                v.tensor_tensor(bT_, t1, eN, ALU.mult).then_inc(sem("tilde"), 1)
                v.wait_ge(sem("ePrev"), 1)
                v.scalar_tensor_tensor(aT_, kk, -1.0, ePrev, ALU.mult, ALU.mult).then_inc(sem("tilde"), 1)
                v.wait_ge(sem("eP"), 1)
                v_step(v.tensor_tensor(ch4(rT_), r_, ch4(eP), ALU.mult))
                v_step(v.tensor_copy(wC, ch4(eP).rearrange("p c (n i) -> p c n i", i=C)[:, :, :, C - 1]))
                v.wait_ge(sem("bonus_psum"), 1)
                for n in range(2):
                    v_step(v.tensor_tensor(bonus[:, n * 512:(n + 1) * 512].rearrange("p (c s) -> p c s", c=2),
                                           ps[6 + n][:, :].rearrange("p (c s) -> p c s", c=2), v_[:, 2 * n:2 * n + 2, :], ALU.mult))

        if debug and until <= 7.1:
            debug(nc, sem, locals())
            return

        rbT = ring[:, 4 * CELL:4 * CELL + 2048].rearrange("p (u n) -> p u n", u=16)
        HT = ring[:, 4 * CELL + 2048:4 * CELL + 3072].rearrange("p (u n) -> p u n", u=8)
        Gs = acc[:, 0:1024].rearrange("p (t h d) -> p t h d", t=NT, h=8)
        Yv = acc[:, 1024:2048].rearrange("p (t h d) -> p t h d", t=NT, h=8)
        y_tok = acc[:, 2048:3072].rearrange("p (t h d) -> p t h d", t=NT, h=8)
        MT = side[:, 4096:6144].rearrange("p (q c d) -> p q c d", q=4, c=NC)
        NN = ring[:, c5:c5 + 2048].rearrange("p (q c d) -> p q c d", q=4, c=NC)
        SS = xn_sb[:, :].rearrange("p (q c d) -> p q c d", q=4, c=NC)
        W2 = [acc[:, 4096 + i * 1024:4096 + (i + 1) * 1024] for i in range(2)]
        exp_v = [side[:, 6144 + i * 512:6144 + (i + 1) * 512] for i in range(2)]
        exp_g = [ring[:, c5 + 2048 + i * 256:c5 + 2048 + (i + 1) * 256] for i in range(2)]
        AKT = [ring[:, c5 + 2560 + i * 128:c5 + 2560 + (i + 1) * 128] for i in range(2)]
        RKT = [ring[:, c5 + 2816 + i * 128:c5 + 2816 + (i + 1) * 128] for i in range(2)]

        QA, QTA, QB, QTB, PTA, PTB, OTM, UH = range(8)

        with nc.Block() as block:
            def mat(b, i, n=1):
                return W2[b][:, i * P:(i + n) * P]

            def inst(u):
                h, t = u // NT, u % NT
                jo = (h % 2) * 64
                return h, t, slice(jo, jo + 64), h // 2, u % 2

            @block.gpsimd
            def _(pool):
                cm = chunk_of.unsqueeze(2).broadcast_to((P, 4, 64))
                for u in range(16):
                    h, t, js, q, b = inst(u)
                    if u >= 2:
                        pool.wait_ge(sem("i_maps"), u - 1)
                    for i, src in enumerate((b_tk, v_tk)):
                        p_step(pool.tensor_tensor(exp_v[b][:, i * S:(i + 1) * S].rearrange("p (c d) -> p c d", c=4),
                                                  src[:, t, h * 64:(h + 1) * 64].unsqueeze(1).broadcast_to((P, 4, 64)), cm, ALU.mult))
                    pool.memset(small[:, 60:61], 0.0).then_inc(sem("i_spread"), 1)
                    pool.wait_ge(sem("i_spread"), u + 1)

            @block.tensor
            def _(pe):
                def start_(u):
                    h, t, js, q, b = inst(u)
                    B = 4 * b
                    T = slice(t * P, (t + 1) * P)
                    if u >= 2:
                        pe.wait_ge(sem("i_end"), u - 1)
                    pe.matmul(ps[B][:, 0:S], ch4(bT_)[js, q, T], tl[js, 0:2, q, T], start=True, stop=True)
                    pe.matmul(ps[B + 1][:, 0:S], ch4(kT_)[js, q, T], tl[js, 0:2, q, T], start=True, stop=True)
                    pe.matmul(ps[B + 2][:, 0:P], ch4(aT_)[js, q, T], ch4(bT_)[js, q, T], start=True, stop=True).then_inc(
                        sem("i_prod"), 1)

                def steps(u):
                    h, t, js, q, b = inst(u)
                    B = 4 * b
                    hs = slice(h * 64, (h + 1) * 64)
                    def level(n, Q, QT, last_level):
                        def f():
                            pe.wait_ge(sem(f"i_q{b}"), 4 * (u // 2) + n)
                            if n == 1:
                                pe.wait_ge(sem(f"i_pt{b}"), 5 * (u // 2) + 1)
                            pe.matmul(ps[B][:, 0:P], mat(b, QT), mat(b, Q), start=True, stop=True)
                            if not last_level:
                                last = pe.matmul(ps[B][:, P:S], mat(b, Q), mat(b, QT), start=True, stop=True)
                            else:
                                last = pe.matmul(ps[B][:, P:S], mat(b, Q), mat(b, QT), start=True, stop=True)
                            last.then_inc(sem(f"i_sq{b}"), 1)
                        return f

                    def grow(n, Q, PT):
                        def f():
                            pe.wait_ge(sem(f"i_q{b}"), 4 * (u // 2) + n)
                            pe.wait_ge(sem(f"i_pt{b}"), 5 * (u // 2) + n - 1)
                            pe.matmul(ps[B + 1][:, 0:P], mat(b, Q), mat(b, PT), start=True, stop=True).then_inc(sem(f"i_gr{b}"), 1)
                        return f

                    def off1():
                        pe.wait_ge(sem(f"i_pt{b}"), 5 * (u // 2) + 4)
                        pe.transpose(ps[B + 2][:, 0:P], mat(b, PTB), ident[:, :]).then_inc(sem(f"i_pd{b}"), 1)

                    def off2():
                        pe.wait_ge(sem(f"i_off{b}"), 2 * (u // 2) + 1)
                        pe.matmul(ps[B + 2][:, P:S], mat(b, OTM), mat(b, QA), start=True, stop=True).then_inc(sem(f"i_xt{b}"), 1)
                        pe.matmul(ps[B + 3][:, 0:64], AKT[b], v_tk[:, t, hs], start=True, stop=True)
                        pe.matmul(ps[B + 3][:, 64:128], RKT[b], v_tk[:, t, hs], start=True, stop=True).then_inc(sem(f"i_u{b}"), 1)

                    def off3():
                        pe.wait_ge(sem(f"i_off{b}"), 2 * (u // 2) + 2)
                        pe.matmul(ps[B + 1][:, 0:P], mat(b, QB), mat(b, PTB), start=True, stop=True).then_inc(sem(f"i_gr{b}"), 1)

                    def solve():
                        pe.wait_ge(sem(f"i_pt{b}"), 5 * (u // 2) + 5)
                        pe.wait_ge(sem(f"i_ud{b}"), u // 2 + 1)
                        pe.matmul(ps[B][:, 0:64], mat(b, PTA), mat(b, UH)[:, 0:64], start=True, stop=True)
                        pe.matmul(ps[B][:, 64:P], mat(b, PTA), a_tk[:, t, hs], start=True, stop=True)
                        pe.matmul(ps[B + 1][js, 0:P], a_tk[:, t, hs], mat(b, PTA), start=True, stop=True).then_inc(sem("i_sol"), 1)

                    def maps():
                        pe.wait_ge(sem("i_gh"), u + 1)
                        pe.wait_ge(sem("i_spread"), u + 1)
                        pe.matmul(ps[B + 2][js, 0:S], mat(b, UH)[:, 64:P], exp_v[b][:, 0:S], start=True, stop=True)
                        pe.matmul(ps[B + 2][js, S:2 * S], b_tk[:, t, hs], exp_g[b], start=True, stop=False)
                        pe.matmul(ps[B + 2][js, S:2 * S], k_tk[:, t, hs], exp_v[b][:, S:2 * S], start=False, stop=True).then_inc(
                            sem("i_maps"), 1)
                    return [lambda: start_(u), level(1, QA, QTA, False), level(2, QB, QTB, False), grow(2, QB, PTA),
                            level(3, QA, QTA, True), grow(3, QA, PTB), grow(4, QB, PTA), off1, off2, off3, solve, maps]
                for pair in range(8):
                    for fa, fb in zip(steps(2 * pair), steps(2 * pair + 1)):
                        fa()
                        fb()

            @block.scalar
            def _(act):
                def steps(u):
                    h, t, js, q, b = inst(u)
                    B = 4 * b

                    def sq(n, dst):
                        def f():
                            act.wait_ge(sem(f"i_sq{b}"), 3 * (u // 2) + n)
                            act.activation(mat(b, dst, 2), ps[B][:, 0:S], ACT.Copy).then_inc(sem(f"i_q{b}"), 1)
                        return f

                    def uh():
                        act.wait_ge(sem(f"i_u{b}"), u // 2 + 1)
                        act.activation(mat(b, UH)[:, 0:64], ps[B + 3][:, 0:64], ACT.Copy).then_inc(sem(f"i_ud{b}"), 1)
                        act.activation(Yv[:, t, h, :], ps[B + 3][:, 64:P], ACT.Copy)

                    def sol():
                        act.wait_ge(sem("i_sol"), u + 1)
                        act.activation(HT[js, 2 * q + t, :], ps[B + 1][js, 0:P], ACT.Copy)

                    def nmap():
                        act.wait_ge(sem("i_maps"), u + 1)
                        act.wait_ge(sem("i_mdone"), u + 1)
                        act.activation(NN[js, q, 4 * t:4 * t + 4, :], ps[B + 2][js, S:2 * S].rearrange("p (c d) -> p c d", c=4),
                                       ACT.Copy).then_inc(sem("i_end"), 1)
                    return [sq(1, QB), sq(2, QA), sq(3, QB), uh, sol, nmap]
                for pair in range(8):
                    for fa, fb in zip(steps(2 * pair), steps(2 * pair + 1)):
                        fa()
                        fb()

            @block.vector
            def _(v):
                v_step(v.memset(SS[:, :, 0, :], 0.0))

                def steps(u):
                    h, t, js, q, b = inst(u)
                    B = 4 * b

                    def first():
                        v.wait_ge(sem("i_prod"), u + 1)
                        v.tensor_tensor(mat(b, QTA), ps[B][:, P:S], M_16, ALU.mult)
                        v_step(v.tensor_tensor(mat(b, QA), ps[B + 2][:, 0:P], M_16L, ALU.mult))
                        v.tensor_tensor(mat(b, PTA), mat(b, QTA), ident[:, :], ALU.add).then_inc(sem(f"i_q{b}"), 1)
                        v.wait_ge(sem(f"i_q{b}"), 4 * (u // 2) + 1)
                        v.tensor_tensor(rbT[:, u, :], ps[B][:, 0:P], M_INCL, ALU.mult)
                        v.tensor_tensor(mat(b, OTM), ps[B][:, P:S], M_OFF, ALU.mult)
                        v.tensor_tensor(RKT[b], ps[B + 1][:, 0:P], M_INCL, ALU.mult)
                        v.tensor_tensor(AKT[b], ps[B + 1][:, P:S], M_STRICT, ALU.mult).then_inc(sem(f"i_pt{b}"), 1)

                    def grown(n, src, dst):
                        def f():
                            v.wait_ge(sem(f"i_gr{b}"), 4 * (u // 2) + n)
                            v.tensor_tensor(mat(b, dst), ps[B + 1][:, 0:P], mat(b, src), ALU.add).then_inc(sem(f"i_pt{b}"), 1)
                            v.wait_ge(sem(f"i_pt{b}"), 5 * (u // 2) + n + 1)
                        return f

                    def pd():
                        v.wait_ge(sem(f"i_pd{b}"), u // 2 + 1)
                        v.tensor_copy(mat(b, QA), ps[B + 2][:, 0:P]).then_inc(sem(f"i_off{b}"), 1)

                    def xt():
                        v.wait_ge(sem(f"i_xt{b}"), u // 2 + 1)
                        v.tensor_copy(mat(b, QB), ps[B + 2][:, P:S]).then_inc(sem(f"i_off{b}"), 1)

                    def sol():
                        v.wait_ge(sem("i_sol"), u + 1)
                        v_step(v.tensor_copy(Gs[:, t, h, :], ps[B][:, 0:64]))
                        v.tensor_copy(mat(b, UH)[:, 64:P], ps[B][:, 64:P])
                        v.tensor_tensor(exp_g[b].rearrange("p (c d) -> p c d", c=4),
                                        Gs[:, t, h, :].unsqueeze(1).broadcast_to((P, 4, 64)),
                                        chunk_of.unsqueeze(2).broadcast_to((P, 4, 64)), ALU.mult).then_inc(sem("i_gh"), 1)

                    def maps():
                        v.wait_ge(sem("i_maps"), u + 1)
                        v.tensor_tensor(MT[js, q, 4 * t:4 * t + 4, :], ps[B + 2][js, 0:S].rearrange("p (c d) -> p c d", c=4),
                                        ident[js, js].unsqueeze(1).broadcast_to((64, 4, 64)), ALU.add).then_inc(sem("i_mdone"), 1)
                    return [first, grown(1, PTA, PTB), grown(2, PTB, PTA), grown(3, PTA, PTB), pd, xt, grown(4, PTB, PTA), sol, maps]
                for pair in range(8):
                    for fa, fb in zip(steps(2 * pair), steps(2 * pair + 1)):
                        fa()
                        fb()

        if debug and until <= 7.2:
            debug(nc, sem, locals())
            return

        sa_sb = [acc[:, 4096 + t * 512:4096 + (t + 1) * 512].rearrange("p (h d) -> p h d", h=8) for t in range(NT)]
        sq7 = acc[:, 5120:6144]
        st7 = small[:, 24:40]
        orT = ch4(side[:, 0:1024])

        with nc.Block() as block:
            @block.tensor
            def _(pe):
                for c in range(NC - 1):
                    if c:
                        pe.wait_ge(sem("state"), 2 * c)
                    for par in range(2):
                        js = slice(par * 64, par * 64 + 64)
                        for q in range(4):
                            last = pe.matmul(ps[par][js, q * 64:(q + 1) * 64], MT[js, q, c, :], SS[js, q, c, :], start=True, stop=True)
                        last.then_inc(sem("state_psum"), 1)
                pe.wait_ge(sem("state"), 2 * (NC - 1))
                for t in range(NT):
                    if t:
                        pe.wait_ge(sem("sa_done"), 2)
                        pe.wait_ge(sem("y_out"), 1)
                    for par in range(2):
                        js = slice(par * 64, par * 64 + 64)
                        for q in range(4):
                            for c in range(4):
                                last = pe.matmul(ps[par][c * C:(c + 1) * C, q * 64:(q + 1) * 64], HT[js, 2 * q + t, c * C:(c + 1) * C],
                                                 SS[js, q, 4 * t + c, :], start=True, stop=True)
                    last.then_inc(sem("sa_psum"), 1)
                    for par in range(2):
                        js = slice(par * 64, par * 64 + 64)
                        for q in range(4):
                            for c in range(4):
                                o = t * P + c * C
                                last = pe.matmul(ps[2 + par][c * C:(c + 1) * C, q * 64:(q + 1) * 64], ch4(rT_)[js, q, o:o + C],
                                                 SS[js, q, 4 * t + c, :], start=True, stop=True)
                    pe.wait_ge(sem("sa_done"), 2 * t + 2)
                    for h in range(8):
                        last = pe.matmul(ps[4][:, h * 64:(h + 1) * 64], rbT[:, 2 * h + t, :], sa_sb[t][:, h, :], start=True, stop=True)
                    last.then_inc(sem("y_psum"), 1)
                pe.wait_ge(sem("y_normed"), 1)
                yf = acc[:, 2048:3072].rearrange("p (t d) -> p t d", t=NT)
                for c in range(4):
                    for t in range(NT):
                        last = pe.transpose(ps[6 + c // 2][:, (c % 2) * S + t * P:(c % 2) * S + (t + 1) * P],
                                            yf[:, t, c * P:(c + 1) * P], ident[:, :])
                last.then_inc(sem("yT_psum"), 1)

            @block.scalar
            def _(act):
                act.wait_ge(sem("y_centred"), 1)
                act.activation(sq7, acc[:, 2048:3072], ACT.Square).then_inc(sem("y_sq"), 1)
                act.wait_ge(sem("y_var"), 1)
                act.activation(st7, st7, ACT.Sqrt).then_inc(sem("y_root"), 1)

            @block.vector
            def _(v):
                for c in range(NC - 1):
                    for par in range(2):
                        js = slice(par * 64, par * 64 + 64)
                        v.wait_ge(sem("state_psum"), 2 * c + par + 1)
                        s_ = SS[js, :, c + 1, :]
                        v_step(v.tensor_tensor(s_, ps[par][js, 0:S].rearrange("p (q d) -> p q d", q=4), NN[js, :, c, :], ALU.add))
                        v.tensor_tensor(s_, s_, wC[js, :, c].unsqueeze(2).broadcast_to((64, 4, 64)), ALU.mult).then_inc(sem("state"), 1)
                for t in range(NT):
                    v.wait_ge(sem("sa_psum"), t + 1)
                    gq = Gs[:, t, :, :].rearrange("p (q r) d -> p r q d", r=2)
                    sq_ = sa_sb[t].rearrange("p (q r) d -> p r q d", r=2)
                    for par in range(2):
                        v.tensor_tensor(sq_[:, par, :, :], ps[par][:, 0:S].rearrange("p (q d) -> p q d", q=4), gq[:, par, :, :],
                                        ALU.add).then_inc(sem("sa_done"), 1)
                    v.wait_ge(sem("y_psum"), t + 1)
                    v_step(v.tensor_tensor(y_tok[:, t, :, :], ps[4][:, :].rearrange("p (h d) -> p h d", h=8), Yv[:, t, :, :], ALU.add))
                    yq = y_tok[:, t, :, :].rearrange("p (q r) d -> p r q d", r=2)
                    for par in range(2):
                        ins = v.tensor_tensor(yq[:, par, :, :], ps[2 + par][:, 0:S].rearrange("p (q d) -> p q d", q=4),
                                              yq[:, par, :, :], ALU.add)
                    ins.then_inc(sem("y_out"), 1)
                v.wait_ge(sem("y_out"), 2)
                yg = acc[:, 2048:3072].rearrange("p (g d) -> p g d", d=64)
                v_step(v.tensor_reduce(st7, yg, X, ALU.add))
                v_step(v.tensor_scalar(st7, st7, -1.0 / 64, None, ALU.mult))
                v.tensor_tensor(yg, yg, st7.unsqueeze(2).broadcast_to((P, 16, 64)), ALU.add).then_inc(sem("y_centred"), 1)
                v.wait_ge(sem("y_sq"), 1)
                v_step(v.tensor_reduce(st7, sq7.rearrange("p (g d) -> p g d", d=64), X, ALU.add))
                v.tensor_scalar(st7, st7, 1.0 / 64, 64e-5, ALU.mult, ALU.add).then_inc(sem("y_var"), 1)
                v.wait_ge(sem("y_root"), 1)
                v_step(v.reciprocal(st7, st7))
                v.tensor_tensor(yg, yg, st7.unsqueeze(2).broadcast_to((P, 16, 64)), ALU.mult).then_inc(sem("y_normed"), 1)
                v.wait_ge(sem("yT_psum"), 1)
                for c in range(4):
                    ins = v.tensor_scalar(orT[:, c, :], ps[6 + c // 2][:, (c % 2) * S:(c % 2 + 1) * S], colB("rwkv_ln_w_2", c),
                                          colB("rwkv_ln_b_2", c), ALU.mult, ALU.add)
                v_step(ins)
                v_step(v.tensor_tensor(side[:, 0:1024], side[:, 0:1024], bonus, ALU.add))
                v_step(v.tensor_tensor(side[:, 0:1024], side[:, 0:1024], gg, ALU.mult))

        if debug and until <= 7.5:
            debug(nc, sem, locals())
            return

        give_back()
        mrg = acc[:, 2048:4096].rearrange("p (c s) -> p c s", c=8)
        mrg_half = acc[:, 0:2048].rearrange("p (c s) -> p c s", c=8)
        gates_sb = ring[:, 4 * CELL:5 * CELL].rearrange("p (c s) -> p c s", c=16)

        with nc.Block() as block:
            @block.sync
            def _(sp):
                for i in range(8, 11):
                    p2_load(sp, i, p2(i), w_cols(w_in, GA0 + (i - GATE0) * 512, GA0 + (i - GATE0 + 1) * 512))
                for i, name in ((BRA, "w_branch_attn_2"), (BRR, "w_branch_rwkv_2")):
                    sp.wait_ge(sem("p3_used"), i - MIX_CELLS - GATE0 + 1)
                    p2_load(sp, i, p2(i, 4, 1024), inp[name][0].rearrange("(c p) n -> p c n", p=P))
                for i in range(2):
                    sp.wait_ge(sem("p3_used"), OUT0 + i - MIX_CELLS - GATE0 + 1)
                    p2_load(sp, OUT0 + i, p2(OUT0 + i), w_cols(inp["w_out_2"][0], i * 512, (i + 1) * 512))

            @block.tensor
            def _(pe):
                for m in range(16):
                    if m % 4 == 0:
                        p2_ready(pe, GATE0 + m // 4)
                    if m >= 4:
                        pe.wait_ge(sem("side_gate_out"), m - 3)
                    for c in range(KC):
                        last = pe.matmul(ps[m % 4][:, 0:S], p2(GATE0 + m // 4)[:, c, (m % 4) * P:(m % 4 + 1) * P], hT[:, c, :],
                                         start=(c == 0), stop=(c == KC - 1))
                    if m % 4 == 3:
                        last.then_inc(sem("p3_used"), 1)
                    else:
                        last.then_inc(sem("gates"), 1)
                for m in range(16):
                    if m % 8 == 0:
                        p2_ready(pe, BRA + m // 8)
                    if m >= 4:
                        pe.wait_ge(sem("branch_out"), m - 3)
                    src_ = oaT if m < 8 else orT
                    for c in range(4):
                        last = pe.matmul(ps[4 + m % 4][:, 0:S], p2(BRA + m // 8, 4, 1024)[:, c, (m % 8) * P:(m % 8 + 1) * P],
                                         src_[:, c, :], start=(c == 0), stop=(c == 3))
                    last.then_inc(sem("branch"), 1)
                pe.wait_ge(sem("branch_out"), 16)
                for g in range(4):
                    t, n = g // 2, g % 2
                    if t == 0:
                        p2_ready(pe, OUT0 + n)
                    for c in range(KC):
                        last = pe.matmul(ps[g][:, :], mrg[:, c, t * P:(t + 1) * P], p2(OUT0 + n)[:, c, :],
                                         start=(c == 0), stop=(c == KC - 1))
                    last.then_inc(sem("y3"), 1)
                hT_tensor(pe, 3)

            @block.scalar
            def _(act):
                for m in range(16):
                    if m % 4 == 3:
                        act.wait_ge(sem("p3_used"), m // 4 + 1)
                    else:
                        act.wait_ge(sem("gates"), 3 * (m // 4) + m % 4 + 1)
                    act.activation(gates_sb[:, m, :], ps[m % 4][:, 0:S], ACT.Sigmoid).then_inc(sem("side_gate_out"), 1)
                rms_scalar(act, 4, xn_sb)

            @block.vector
            def _(v):
                for m in range(16):
                    v.wait_ge(sem("branch"), m + 1)
                    v.wait_ge(sem("side_gate_out"), m + 1)
                    if m < 8:
                        v.tensor_tensor(mrg[:, m, :], ps[4 + m % 4][:, 0:S], gates_sb[:, m, :], ALU.mult).then_inc(sem("branch_out"), 1)
                    else:
                        v_step(v.tensor_tensor(mrg_half[:, m - 8, :], ps[4 + m % 4][:, 0:S], gates_sb[:, m, :], ALU.mult))
                        v.tensor_tensor(mrg[:, m - 8, :], mrg[:, m - 8, :], mrg_half[:, m - 8, :], ALU.add).then_inc(sem("branch_out"), 1)
                residual(v, 0, None, 0, "y3")
                rms_vector(v, 4, xn3)
                v.tensor_copy(small[:, 20:21], small[:, 14:15]).then_inc(sem("mod_done"), 1)
                hT_vector(v, 3)

        with nc.Block() as block:
            @block.sync
            def _(sp):
                load_router(sp, 1, inp["router_group_w_2"][0], inp["router_expert_w_2"][0], None, inp["router_expert_bias_2"])
        if debug and until <= 8:
            debug(nc, sem, locals())
            return
        route(1, 32, False)
        experts(1, 32, inp["expert_w_gate_2"][0], inp["expert_w_up_2"][0], inp["expert_w_down_2"][0])

        with nc.Block() as block:
            @block.sync
            def _(sp):
                sp.dma_start(out[0].rearrange("(t p) d -> p t d", p=P), x3).then_inc(sem("stored"), 16)
                sp.wait_ge(sem("stored"), 16)
        if debug:
            debug(nc, sem, locals())


OUT_SHAPE = (1, S, D)


def kernel(**inputs):
    import concourse.bacc as bacc
    from concourse.bass_utils import run_bass_kernel_spmd

    nc = bacc.Bacc("TRN2", target_bir_lowering=False, num_devices=1)
    arrays, inp = {}, {}
    for name, value in inputs.items():
        a = np.ascontiguousarray(value)
        if a.size == 0:
            continue
        arrays["in_" + name] = a
        inp[name] = nc.dram_tensor("in_" + name, a.shape, mybir.dt.from_np(a.dtype), kind="ExternalInput").ap()
    out = nc.dram_tensor("out_x", OUT_SHAPE, F32, kind="ExternalOutput").ap()
    build(nc, inp, out)
    r = run_bass_kernel_spmd(nc, [arrays], core_ids=[0])
    return r.results[0]["out_x"]
```

```python
import math
from contextlib import ExitStack

import numpy as np

import concourse.bass as bass
from concourse import mybir

F32 = mybir.dt.float32
I32 = mybir.dt.int32
ALU = mybir.AluOpType
ACT = mybir.ActivationFunctionType
X = mybir.AxisListType.X

P = 128
S = 256
D = 1024
NT = S // P
KC = D // P
EPS = 1e-6
CELL = 4096
SLOTS = 64
ROUNDS = S // SLOTS
FE = 512
FC = FE // P
BIG = 3.0e38

ROWS_A = [("norm_mix", 8), ("norm_ffn", 8), ("mix_norm_g_2", 8), ("moe_norm_g_2", 8),
          ("ada_b", 48)]
ROWS_B = [("ada_b_2", 48), ("rwkv_w0_2", 4), ("rwkv_a0_2", 4), ("rwkv_k_k_2", 4), ("rwkv_k_a_2", 4),
          ("rwkv_r_k_2", 4), ("rwkv_ln_w_2", 4), ("rwkv_ln_b_2", 4), ("kv_norm_g_2", 2), ("attn_subln", 1)]


def row_starts(rows):
    at, out = 0, {}
    for name, n in rows:
        out[name] = at
        at += n
    return out, at


def build(nc, inp, out, debug=None, until=99):
    ctx = ExitStack()
    with ctx:
        def sb(name, cols, dt=F32, parts=P):
            return ctx.enter_context(nc.sbuf_tensor(name, [parts, cols], dt))

        sems = {}

        def sem(name):
            if name not in sems:
                sems[name] = nc.alloc_semaphore(name)
            return sems[name]

        KEPT = {"v_chain", "p_chain", "ssq", "ms_done", "root", "x_ready", "xn_ready", "hT_psum", "hT_done", 
                "modc_psum", "g_psum", "g_out", "prio", "logits", "masked", "places", "g_shifted", "g_exp", "d12",
                "d12_exp", "nf_loaded", "ada2_used0", "ada2_used1", "ada2_used2", "p2_used", "p2_loaded0",
                "p2_loaded1", "p2_loaded2", "p2_loaded3", "branch_loaded0", "branch_loaded1", "out_loaded0"}

        def give_back():
            old = sorted(n for n in sems if n not in KEPT)
            nc.clear_and_free_semaphores([sems.pop(n) for n in old])
            nc.all_engine_barrier()

        def chain(eng, name):
            count = [0]

            def step(ins):
                count[0] += 1
                ins.then_inc(sem(name), 1)
                eng.wait_ge(sem(name), count[0])
            return step

        v_step = chain(nc.vector, "v_chain")
        p_step = chain(nc.gpsimd, "p_chain")

        ring = sb("ring", 6 * CELL)
        side = sb("side", 2 * CELL)
        acc = sb("acc", 6 * D)
        tmp = sb("tmp", CELL)
        x_sb = sb("x_sb", NT * D)
        xn_sb = sb("xn_sb", NT * D)
        hT_sb = sb("hT_sb", KC * S)
        gate_rows = sb("gate_rows", 2 * D)
        ident = sb("ident", P)
        ones = sb("ones", P)
        before = sb("before", P)
        headones = sb("headones", P)
        slot_ids = sb("slot_ids", SLOTS)
        colsA = sb("colsA", P)
        colsB = sb("colsB", P)
        cond = sb("cond", 2 * KC)
        modc = sb("modc", 4 * KC)
        small = sb("small", 64)
        NE_MAX = 32
        TAB = ROUNDS * NE_MAX + 2
        pos_t = sb("pos_t", NT * TAB)
        mask_t = sb("mask_t", NT * TAB)
        gate_t = sb("gate_t", NT * TAB)
        rounds_i = sb("rounds_i", 1, I32)
        qk_cols = sb("qk_cols", 2)

        ps = [ctx.enter_context(nc.psum_tensor(f"ps{i}", [P, 512], F32)) for i in range(8)]

        x3 = x_sb[:, :].rearrange("p (t d) -> p t d", t=NT)
        xn3 = xn_sb[:, :].rearrange("p (t d) -> p t d", t=NT)
        hT = hT_sb[:, :].rearrange("p (c s) -> p c s", c=KC)
        g_b = gate_rows[:, :].rearrange("p (g d) -> p g d", g=2)

        def cell(i, kc=8, w=512):
            return ring[:, i * CELL:i * CELL + kc * w].rearrange("p (c n) -> p c n", c=kc)

        def w_cols(ap, a, b):
            return ap[:, a:b].rearrange("(c p) n -> p c n", p=P)

        stA, nA = row_starts(ROWS_A)
        stB, nB = row_starts(ROWS_B)
        MU0 = nB + 2
        NB_ALL = MU0 + 15
        rowsA = tmp[:, 0:P]
        rowsB = tmp[:, P:2 * P]
        rowsC = tmp[0:16, 2 * P:3 * P]

        def colA(name, i=0, n=1):
            return colsA[:, stA[name] + i:stA[name] + i + n]

        def colB(name, i=0, n=1):
            return colsB[:, stB[name] + i:stB[name] + i + n]

        lam_in = tmp[:, 512:768].rearrange("p (v d) -> p v d", v=4)
        lam = small[:, 0:8]

        AW = 256
        N_ADA_P = 6 * D // AW
        FIRST_ADA = 8
        ADA_TENSOR = (2, 5)

        def side_slot(i):
            if i < FIRST_ADA:
                a = side[:, i * 2048:(i + 1) * 2048] if i < 4 else ring[:, CELL + (i - 4) // 2 * 2 * CELL + i % 2 * 2048:
                                                                        CELL + (i - 4) // 2 * 2 * CELL + (i % 2 + 1) * 2048]
            else:
                a = side[:, ada_turn(i) * 2048:(ada_turn(i) + 1) * 2048]
            return a.rearrange("p (c n) -> p c n", c=8)

        def ada_turn(i):
            return i if i < FIRST_ADA else (i - FIRST_ADA) % 3

        def ada_earlier(i):
            return 0 if i < FIRST_ADA else 1 + (i - FIRST_ADA) // 3

        def load_ada(sp, pieces_):
            for i in pieces_:
                if ada_earlier(i):
                    sp.wait_ge(sem(f"ada_used{ada_turn(i)}"), ada_earlier(i))
                sp.dma_start(side_slot(i), w_cols(inp["ada_w"][0], i * AW, (i + 1) * AW)).then_inc(
                    sem(f"ada_loaded{ada_turn(i)}"), 16)

        def ada_ready(eng, i):
            eng.wait_ge(sem(f"ada_loaded{ada_turn(i)}"), 16 * (ada_earlier(i) + 1))

        ada_count = [0]

        def ada_op(v, i, k):
            a = acc[:, i * AW:(i + 1) * AW]
            w = side_slot(i)
            s = cond[:, k:k + 1]
            if k == 0:
                ada_ready(v, i)
                ins = v.tensor_scalar(a, w[:, k, :], s, None, ALU.mult)
            else:
                v.wait_ge(sem("ada_chain"), ada_count[0])
                ins = v.scalar_tensor_tensor(a, w[:, k, :], s, a, ALU.mult, ALU.add)
            if k < KC - 1:
                ins.then_inc(sem("ada_chain"), 1)
                ada_count[0] += 1
            else:
                ins.then_inc(sem(f"ada_used{ada_turn(i)}"), 1)

        ADA2_AHEAD = 8
        ADA2_PER_PAIR = (N_ADA_P - ADA2_AHEAD) // 8

        def ada2_slot(j):
            a = side[:, j * 2048:(j + 1) * 2048] if j < 3 else acc[:, (j - 2) * 2048:(j - 1) * 2048]
            return a.rearrange("p (c n) -> p c n", c=8)

        def load_ada2(sp, pieces_):
            for i in pieces_:
                if i >= 5:
                    sp.wait_ge(sem(f"ada2_used{i % 5}"), 1)
                sp.dma_start(ada2_slot(i % 5), w_cols(inp["ada_w_2"][0], i * AW, (i + 1) * AW)).then_inc(
                    sem(f"ada2_loaded{i % 5}"), 16)

        def sum_ada2(v, i):
            for k in range(KC):
                for j in (i, i + 1):
                    a = acc[:, j * AW:(j + 1) * AW]
                    w = ada2_slot(j % 5)
                    s = cond[:, KC + k:KC + k + 1]
                    if k == 0:
                        v.wait_ge(sem(f"ada2_loaded{j % 5}"), 16 * (j // 5 + 1))
                        ins = v.tensor_scalar(a, w[:, k, :], s, None, ALU.mult)
                    else:
                        v.wait_ge(sem("ada2_pair"), (i // 2) * 2 * (KC - 1) + 2 * (k - 1) + j - i + 1)
                        ins = v.scalar_tensor_tensor(a, w[:, k, :], s, a, ALU.mult, ALU.add)
                    ins.then_inc(sem("ada2_pair" if k < KC - 1 else f"ada2_used{j % 5}"), 1)

        def ada_wait(eng, n):
            last = {}
            for i in range(n):
                last[ada_turn(i)] = ada_earlier(i) + 1
            for slot, uses in last.items():
                eng.wait_ge(sem(f"ada_used{slot}"), uses)

        def ada_product(pe, i, bank):
            ada_ready(pe, i)
            for j in range(2):
                for k in range(KC):
                    last = pe.matmul(ps[bank][:, 2 * i + j:2 * i + j + 1], side_slot(i)[:, k, j * P:(j + 1) * P],
                                     cond[:, k:k + 1], start=(k == 0), stop=(k == KC - 1))
            last.then_inc(sem(f"ada_used{ada_turn(i)}"), 1)

        def ada_columns(pe, vecs, bank, name, chunks=None):
            for n, m in enumerate(vecs):
                for j in range(KC):
                    if chunks is None or n * KC + j in chunks:
                        last = pe.matmul(ps[bank][:, n * KC + j:n * KC + j + 1], acc[:, m * D + j * P:m * D + (j + 1) * P],
                                         ones[:, 0:1], start=True, stop=True)
            last.then_inc(sem(name), 1)

        def ada_rows(pe, m, bank0, name):
            for n in range(2):
                last = pe.matmul(ps[bank0 + n][:, :], ones[:, :], acc[:, m * D + n * 512:m * D + (n + 1) * 512],
                                 start=True, stop=True)
            last.then_inc(sem(name), 1)

        NORMS = ["norm1", "norm2", "final1", "norm3", "norm4"]

        def rms_scalar(act, n, scr):
            if n:
                act.wait_ge(sem("x_ready"), n)
            for t in range(NT):
                act.activation(scr[:, t * D:(t + 1) * D], x3[:, t, :], ACT.Square,
                               accum_out=small[:, 8 + t:9 + t]).then_inc(sem("ssq"), 1)
            act.wait_ge(sem("ms_done"), n + 1)
            act.activation(small[:, 12:14], small[:, 10:12], ACT.Sqrt).then_inc(sem("root"), 1)

        def rms_vector(v, n, out3, weight=None, name="xn_ready"):
            v.wait_ge(sem("ssq"), NT * (n + 1))
            v.tensor_scalar(small[:, 10:12], small[:, 8:10], 1.0 / D, EPS, ALU.mult, ALU.add).then_inc(
                sem("ms_done"), 1)
            v.wait_ge(sem("root"), n + 1)
            v_step(v.reciprocal(small[:, 14:16], small[:, 12:14]))
            for t in range(NT):
                if weight is None:
                    ins = v.tensor_scalar(out3[:, t, :], x3[:, t, :], small[:, 14 + t:15 + t], None, ALU.mult)
                else:
                    ins = v.scalar_tensor_tensor(out3[:, t, :], x3[:, t, :], small[:, 14 + t:15 + t], weight,
                                                 ALU.mult, ALU.mult)
            ins.then_inc(sem(name), 1)

        def hT_tensor(pe, n):
            pe.wait_ge(sem("xn_ready"), n + 1)
            for c in range(KC):
                b = ps[4 + c // 2]
                for t in range(NT):
                    o = (c % 2) * S + t * P
                    last = pe.transpose(b[:, o:o + P], xn3[:, t, c * P:(c + 1) * P], ident[:, :])
                if c % 2:
                    last.then_inc(sem("hT_psum"), 1)

        def hT_vector(v, n):
            for c in range(KC):
                if c % 2 == 0:
                    v.wait_ge(sem("hT_psum"), 4 * n + c // 2 + 1)
                o = (c % 2) * S
                v.tensor_scalar(hT[:, c, :], ps[4 + c // 2][:, o:o + S], modc[:, (2 * (n % 2)) * KC + c:(2 * (n % 2)) * KC + c + 1],
                                modc[:, (2 * (n % 2) + 1) * KC + c:(2 * (n % 2) + 1) * KC + c + 1],
                                ALU.mult, ALU.add).then_inc(sem("hT_done"), 1)

        def load_attn(sp, cells):
            for i in cells:
                sp.dma_start(cell(i), w_cols(inp["attn_w_in"][0], i * 512, (i + 1) * 512)).then_inc(
                    sem(f"m1_loaded{i}"), 16)

        MOE = [[inp["expert_w_gate"][0], inp["expert_w_up"][0], inp["expert_w_down"][0]],
               [inp["expert_w_gate_2"][0], inp["expert_w_up_2"][0], inp["expert_w_down_2"][0]]]

        def expert_cell(i):
            return cell(i) if i % 3 < 2 else cell(i, 4, 1024)

        def load_expert(sp, k, cells):
            for i in cells:
                sp.dma_start(expert_cell(i), MOE[k][i % 3][i // 3:i // 3 + 1, :, :].rearrange("o (c p) n -> p (o c) n", p=P)).then_inc(
                    sem(f"moe{k}_loaded{i}"), 16)

        with nc.Block() as block:
            @block.sync
            def _(sp):
                for i, name in enumerate(("c", "c_2")):
                    sp.dma_start(rowsC[8 * i:8 * i + 8, :], inp[name].rearrange("a (r n) -> (a r) n", n=P)).then_inc(
                        sem("c_loaded"), 16)
                load_ada(sp, range(1))
                sp.dma_start(x3, inp["x"][0].rearrange("(t p) d -> p t d", p=P)).then_inc(sem("x_loaded"), 16)
                load_ada(sp, range(1, 4))
                sp.wait_ge(sem("rows_zero"), 1)
                for rows, st, spec in ((rowsA, stA, ROWS_A), (rowsB, stB, ROWS_B)):
                    for name, n in spec:
                        src = inp[name]
                        src = src.rearrange("a h d -> (a h d)") if name == "rwkv_r_k_2" else src.rearrange("a n -> (a n)")
                        sp.dma_start(rows[st[name]:st[name] + n, :], src.rearrange("(r n) -> r n", n=P)).then_inc(
                            sem("rows_loaded"), 16)
                for i, name in enumerate(("q_norm_g_2", "k_norm_g_2")):
                    for h in range(2):
                        sp.dma_start(rowsB[nB + i:nB + i + 1, h * 64:(h + 1) * 64], inp[name]).then_inc(
                            sem("rows_loaded"), 16)
                mu = inp["rwkv_mu_2"].rearrange("a n -> (a n)")
                sp.dma_start(rowsB[MU0:MU0 + 14, :], mu[0:14 * P].rearrange("(r n) -> r n", n=P)).then_inc(
                    sem("rows_loaded"), 16)
                sp.dma_start(rowsB[MU0 + 14:MU0 + 15, 0:32], mu[14 * P:14 * P + 32].rearrange("(a n) -> a n", a=1)).then_inc(
                    sem("rows_loaded"), 16)
                load_ada(sp, range(4, 8))
                load_attn(sp, (0, 2, 4))
                for i, name in enumerate(("attn_lam_q1", "attn_lam_k1", "attn_lam_q2", "attn_lam_k2")):
                    sp.dma_start(lam_in[:, i, :], inp[name][0:1, :].broadcast_to((P, 64))).then_inc(
                        sem("lam_loaded"), 16)
                for i, m in enumerate((2, 5)):
                    sp.dma_start(g_b[:, i, :], inp["ada_b"][0:1, m * D:(m + 1) * D].broadcast_to((P, D))).then_inc(
                        sem("gb_loaded"), 16)
            N_ROW_DMAS = len(ROWS_A) + len(ROWS_B) + 6

            @block.gpsimd
            def _(pool):
                p_step(pool.memset(ident[:, :], 0.0))
                pool.affine_select(out=ident[:, :], in_=ident[:, :], compare_op=ALU.not_equal, fill=1.0, base=0,
                                   pattern=[[-1, P]], channel_multiplier=1).then_inc(sem("ident"), 1)
                pool.memset(tmp[:, 0:2 * P], 0.0).then_inc(sem("rows_zero"), 1)
                pool.wait_ge(sem("rows_zero"), 1)
                p_step(pool.memset(ones[:, :], 1.0))
                p_step(pool.memset(headones[:, :], 1.0))
                p_step(pool.affine_select(out=before[:, :], in_=ones[:, :], compare_op=ALU.is_gt, fill=0.0, base=0,
                                          pattern=[[1, P]], channel_multiplier=-1))
                p_step(pool.memset(headones[0:64, 64:128], 0.0))
                p_step(pool.memset(headones[64:128, 0:64], 0.0))
                pool.iota(slot_ids[:, :], pattern=[[1, SLOTS]], base=0, channel_multiplier=0,
                          allow_small_or_imprecise_dtypes=True).then_inc(sem("const"), 1)

            @block.tensor
            def _(pe):
                pe.wait_ge(sem("ident"), 1)
                pe.wait_ge(sem("c_loaded"), 32)
                pe.transpose(ps[2][:, 0:16], rowsC, ident[0:16, 0:16]).then_inc(sem("c_psum"), 1)
                hT_tensor(pe, 0)
                pe.wait_ge(sem("cond"), 1)
                for i in ADA_TENSOR:
                    ada_product(pe, i, 1)
                    if i == ADA_TENSOR[0]:
                        pe.wait_ge(sem("const"), 1)
                        pe.wait_ge(sem("rows_loaded"), 16 * N_ROW_DMAS)
                        pe.transpose(ps[0][:, 0:P], rowsA, ident[:, :])
                        pe.transpose(ps[0][:, P:2 * P], rowsB, ident[:, :]).then_inc(sem("cols_psum"), 1)
                ada_wait(pe, 8)
                ada_columns(pe, (0, 1), 1, "modc_psum", [c for c in range(2 * KC) if c // 2 not in ADA_TENSOR])

            @block.scalar
            def _(act):
                act.wait_ge(sem("c_psum"), 1)
                act.activation(cond[:, :], ps[2][:, 0:16], ACT.Sigmoid).then_inc(sem("sig_c"), 1)
                act.wait_ge(sem("x_loaded"), 16)
                rms_scalar(act, 0, xn_sb)

            @block.vector
            def _(v):
                v.wait_ge(sem("sig_c"), 1)
                v.tensor_tensor(cond[:, :], cond[:, :], ps[2][:, 0:16], ALU.mult).then_inc(sem("cond"), 1)
                v.wait_ge(sem("cond"), 1)
                rms_vector(v, 0, xn3)
                for i in range(FIRST_ADA):
                    for k in range(KC):
                        if i not in ADA_TENSOR:
                            ada_op(v, i, k)
                v.wait_ge(sem("cols_psum"), 1)
                v.tensor_copy(colsA[:, :], ps[0][:, 0:P]).then_inc(sem("cols_done"), 1)
                v.tensor_copy(colsB[:, :], ps[0][:, P:2 * P]).then_inc(sem("cols_done"), 1)
                v.wait_ge(sem("cols_done"), 2)

        H = 8
        U = H * NT
        qkT = tmp[:, :].rearrange("p (w h s) -> p w h s", w=2, h=H)
        v3 = xn3
        sub08 = qk_cols[:, 0:1]
        LAM_INIT = 0.8 - 0.6 * math.exp(0.0)
        sS = acc[:, 0:1536].rearrange("p (b n) -> p b n", b=3)
        aT = acc[:, 1536:2048].rearrange("p (b n) -> p b n", b=2)
        o_heads = side[:, 6144:8192]
        o3 = o_heads.rearrange("p (t d) -> p t d", t=NT)
        dist = (pos_t[:, 0:S], mask_t[:, 0:S])
        st_a = gate_t[:, 0:256]
        ADA_STEPS = (0, 2, 2, 1, 2, 3, 3, 3, 0)
        ada_at = [8 + sum(ADA_STEPS[:h]) for h in range(H + 2)]

        def fill_modc(v, vec_scale, vec_shift, psc, shift_at, scale_at, norm_col, ada_shift, ada_scale):
            v_step(v.tensor_tensor(modc[:, vec_shift:vec_shift + KC], psc[:, shift_at:shift_at + KC], ada_shift, ALU.add))
            v_step(v.tensor_tensor(modc[:, vec_scale:vec_scale + KC], psc[:, scale_at:scale_at + KC], ada_scale, ALU.add))
            v_step(v.scalar_tensor_tensor(modc[:, vec_scale:vec_scale + KC], modc[:, vec_scale:vec_scale + KC], 1.0,
                                          norm_col, ALU.add, ALU.mult))

        with nc.Block() as block:
            @block.sync
            def _(sp):
                load_ada(sp, range(8, 12))
                load_attn(sp, (1, 3, 5))
                load_ada(sp, range(12, 24))
                sp.wait_ge(sem("v_psum"), H // 2)
                sp.dma_start(cell(4), w_cols(inp["attn_w_out"][0], 0, 512)).then_inc(sem("wo1_loaded0"), 16)
                load_expert(sp, 0, (0, 2))
                sp.wait_ge(sem("v_psum"), H)
                sp.dma_start(cell(5), w_cols(inp["attn_w_out"][0], 512, 1024)).then_inc(sem("wo1_loaded1"), 16)
                load_expert(sp, 0, (1, 3))
                ada_wait(sp, N_ADA_P)
                load_ada2(sp, range(3))

            @block.gpsimd
            def _(pool):
                for t in range(NT):
                    last = pool.iota(dist[t], pattern=[[-1, S]], base=t * P, channel_multiplier=1,
                                     allow_small_or_imprecise_dtypes=True)
                    last.then_inc(sem("dist"), 1)

            @block.tensor
            def _(pe):
                def project_qk(h, w, half):
                    if half == 0:
                        if h % 4 == 0:
                            pe.wait_ge(sem(f"m1_loaded{2 * w + h // 4}"), 16)
                        if h and w == 0:
                            pe.wait_ge(sem("qk_out"), h)
                    for c in range(4 * half, 4 * half + 4):
                        last = pe.matmul(ps[6][:, w * S:(w + 1) * S], cell(2 * w + h // 4)[:, c, (h % 4) * P:(h % 4 + 1) * P],
                                         hT[:, c, :], start=(c == 0), stop=(c == KC - 1))
                    if half and w:
                        last.then_inc(sem("qk_psum"), 1)

                def project_v(h, t):
                    if t == 0:
                        if h % 4 == 0:
                            pe.wait_ge(sem(f"m1_loaded{4 + h // 4}"), 16)
                        if h:
                            pe.wait_ge(sem("v_out"), h)
                    for c in range(KC):
                        last = pe.matmul(ps[7][:, t * P:(t + 1) * P], hT[:, c, t * P:(t + 1) * P],
                                         cell(4 + h // 4)[:, c, (h % 4) * P:(h % 4 + 1) * P],
                                         start=(c == 0), stop=(c == KC - 1))
                    if t:
                        last.then_inc(sem("v_psum"), 1)

                def scores(u):
                    h, t = u // NT, u % NT
                    if t == 0:
                        pe.wait_ge(sem("qk_out"), h + 1)
                    if u >= 2:
                        pe.wait_ge(sem("att_biased"), u - 1)
                    for w in range(2):
                        last = pe.matmul(ps[2 * (u % 2) + w][:, 0:S], qkT[w * 64:(w + 1) * 64, 0, h, t * P:(t + 1) * P],
                                         qkT[w * 64:(w + 1) * 64, 1, h, :], start=True, stop=True)
                    last.then_inc(sem("att_scores"), 1)

                def turn(u):
                    pe.wait_ge(sem("att_a"), u + 1)
                    if u:
                        pe.wait_ge(sem("att_aT"), u)
                    for k in range(2):
                        last = pe.transpose(ps[4][:, k * P:(k + 1) * P], sS[:, u % 3, k * P:(k + 1) * P], ident[:, :])
                    last.then_inc(sem("att_aT_psum"), 1)

                def av(u):
                    h = u // NT
                    pe.wait_ge(sem("att_aT"), u + 1)
                    pe.wait_ge(sem("v_out"), h + 1)
                    if u:
                        pe.wait_ge(sem("att_o"), u)
                    for k in range(2):
                        last = pe.matmul(ps[5][:, 0:P], aT[:, u % 2, k * P:(k + 1) * P],
                                         v3[:, k, h * P:(h + 1) * P], start=(k == 0), stop=(k == 1))
                    last.then_inc(sem("att_av"), 1)

                pe.wait_ge(sem("hT_done"), KC)
                for h in range(H + 1):
                    a, b = 2 * h - 2, 2 * h - 1
                    if h < H:
                        project_qk(h, 0, 0)
                    if h:
                        scores(a)
                    if h < H:
                        project_qk(h, 0, 1)
                    if h:
                        scores(b)
                    if h < H:
                        project_qk(h, 1, 0)
                        project_qk(h, 1, 1)
                    else:
                        ada_wait(pe, 24)
                        pe.wait_ge(sem("v_out"), H)
                        ada_rows(pe, 2, 6, "g_psum")
                    if h:
                        turn(a)
                    if h < H:
                        project_v(h, 0)
                    if h:
                        turn(b)
                        av(a)
                    if h < H:
                        project_v(h, 1)
                    else:
                        ada_rows(pe, 5, 0, "g_psum")
                        ada_columns(pe, (3, 4), 2, "modc_psum")
                    if h:
                        av(b)

            @block.scalar
            def _(act):
                act.wait_ge(sem("lam_sums"), 1)
                act.activation(lam[:, 2:4], lam[:, 0:2], ACT.Exp).then_inc(sem("lam_exp"), 1)

                def exponentials(u):
                    act.wait_ge(sem("att_max"), u + 1)
                    for w in range(2):
                        x = sS[:, u % 3, w * S:(w + 1) * S]
                        act.activation(x, x, ACT.Exp, bias=st_a[:, 4 * u + w:4 * u + w + 1], scale=0.125,
                                       accum_out=st_a[:, 4 * u + 2 + w:4 * u + 3 + w]).then_inc(sem("att_exp"), 1)

                def take_turned(u):
                    act.wait_ge(sem("att_aT_psum"), u + 1)
                    act.activation(aT[:, u % 2, :], ps[4][:, 0:S], ACT.Copy).then_inc(sem("att_aT"), 1)

                for h in range(H + 1):
                    a, b = 2 * h - 2, 2 * h - 1
                    if h:
                        exponentials(a)
                        exponentials(b)
                    if h < H:
                        act.wait_ge(sem("qk_psum"), h + 1)
                        act.activation(qkT[:, :, h, :], ps[6][:, :].rearrange("p (w s) -> p w s", w=2), ACT.Copy).then_inc(
                            sem("qk_out"), 1)
                    if h:
                        take_turned(a)
                        take_turned(b)
                    if h < H:
                        act.wait_ge(sem("v_psum"), h + 1)
                        act.activation(v3[:, :, h * P:(h + 1) * P], ps[7][:, 0:S].rearrange("p (t d) -> p t d", t=NT),
                                       ACT.Copy).then_inc(sem("v_out"), 1)

            @block.vector
            def _(v):
                v.wait_ge(sem("modc_psum"), 1)
                fill_modc(v, 0, KC, ps[1], 0, KC, colA("norm_mix", 0, KC), colA("ada_b", 0, KC), colA("ada_b", KC, KC))
                hT_vector(v, 0)
                v.wait_ge(sem("lam_loaded"), 64)
                for i in range(2):
                    v_step(v.tensor_tensor(lam_in[:, 2 * i, :], lam_in[:, 2 * i, :], lam_in[:, 2 * i + 1, :], ALU.mult))
                    ins = v.tensor_reduce(lam[:, i:i + 1], lam_in[:, 2 * i, :], X, ALU.add)
                ins.then_inc(sem("lam_sums"), 1)
                v_step(v.tensor_scalar(sub08, colB("attn_subln"), 1.0 - LAM_INIT, None, ALU.mult))
                v.wait_ge(sem("lam_exp"), 1)
                v_step(v.tensor_tensor(lam[:, 4:5], lam[:, 2:3], lam[:, 3:4], ALU.subtract))
                v_step(v.tensor_scalar(lam[:, 5:6], lam[:, 4:5], -1.0, -LAM_INIT, ALU.mult, ALU.add))
                v.wait_ge(sem("dist"), 2)
                for t in range(NT):
                    ins = v.scalar_tensor_tensor(dist[t], dist[t], -1.0, dist[t], ALU.mult, ALU.max)
                v_step(ins)

                def first(u):
                    h, t = u // NT, u % NT
                    v.wait_ge(sem("att_scores"), u + 1)
                    if u >= 3:
                        v.wait_ge(sem("att_aT_psum"), u - 2)
                    for w in range(2):
                        ins = v.scalar_tensor_tensor(sS[:, u % 3, w * S:(w + 1) * S], dist[t], -8.0 * 2.0 ** -(h + 1),
                                                     ps[2 * (u % 2) + w][:, 0:S], ALU.mult, ALU.add)
                    ins.then_inc(sem("att_biased"), 1)
                    v.wait_ge(sem("att_biased"), u + 1)
                    v_step(v.tensor_reduce(st_a[:, 192 + 2 * (u % 2):194 + 2 * (u % 2)],
                                           sS[:, u % 3, :].rearrange("p (w s) -> p w s", w=2), X, ALU.max))
                    v.tensor_scalar(st_a[:, 4 * u:4 * u + 2], st_a[:, 192 + 2 * (u % 2):194 + 2 * (u % 2)], -0.125, None,
                                    ALU.mult).then_inc(sem("att_max"), 1)

                def second(u):
                    v.wait_ge(sem("att_exp"), 2 * u + 2)
                    r = st_a[:, 64 + 4 * u:64 + 4 * u + 2]
                    x = sS[:, u % 3, :]
                    v_step(v.reciprocal(r, st_a[:, 4 * u + 2:4 * u + 4]))
                    v.tensor_scalar(r[:, 1:2], r[:, 1:2], lam[:, 5:6], None, ALU.mult)
                    v_step(v.tensor_scalar(x[:, 0:S], x[:, 0:S], r[:, 0:1], None, ALU.mult))
                    v.scalar_tensor_tensor(x[:, 0:S], x[:, S:2 * S], r[:, 1:2], x[:, 0:S],
                                           ALU.mult, ALU.add).then_inc(sem("att_a"), 1)

                def third(u):
                    h, t = u // NT, u % NT
                    v.wait_ge(sem("att_av"), u + 1)
                    v.tensor_copy(o3[:, t, h * P:(h + 1) * P], ps[5][:, 0:P]).then_inc(sem("att_o"), 1)

                for h in range(H + 1):
                    a, b = 2 * h - 2, 2 * h - 1
                    todo = [(i, k) for i in range(ada_at[h], ada_at[h + 1]) for k in range(KC)]

                    def fill(n):
                        for _ in range(min(n, len(todo))):
                            ada_op(v, *todo.pop(0))
                    if h:
                        first(a)
                        fill(1)
                        first(b)
                        second(a)
                        fill(1)
                        second(b)
                        fill(5)
                        third(a)
                        fill(5)
                        third(b)
                    fill(KC * 3)
                v.wait_ge(sem("gb_loaded"), 32)
                for i in range(2):
                    v.wait_ge(sem("g_psum"), i + 1)
                    for n in range(2):
                        a = g_b[:, i, n * 512:(n + 1) * 512]
                        ins = v.tensor_tensor(a, ps[(6, 0)[i] + n][:, :], a, ALU.add)
                    ins.then_inc(sem("g_out"), 1)
                v.wait_ge(sem("modc_psum"), 2)
                fill_modc(v, 2 * KC, 3 * KC, ps[2], 0, KC, colA("norm_ffn", 0, KC), colA("ada_b", 3 * KC, KC), colA("ada_b", 4 * KC, KC))

        NG = 4

        def load_router(sp, k, wg, we, bg, be):
            ne = be.shape[1]
            rw = tmp[:, 2048:2048 + KC * (NG + ne)].rearrange("p (c n) -> p c n", c=KC)
            sp.dma_start(rw[:, :, 0:NG], wg.rearrange("(c p) g -> p c g", p=P)).then_inc(sem(f"router{k}"), 16)
            sp.dma_start(rw[:, :, NG:], we.rearrange("(c p) g -> p c g", p=P)).then_inc(sem(f"router{k}"), 16)
            if bg is not None:
                sp.dma_start(tmp[:, 2400:2400 + NG], bg.broadcast_to((P, NG))).then_inc(sem(f"router{k}"), 16)
            sp.dma_start(tmp[:, 2400 + NG:2400 + NG + ne], be.broadcast_to((P, ne))).then_inc(sem(f"router{k}"), 16)

        oT = hT

        def residual(v, i, banks, first_bank, name):
            for g in range(4):
                t, n = g // 2, g % 2
                v.wait_ge(sem(name), g + 1)
                y = tmp[:, g * 512:(g + 1) * 512]
                v_step(v.tensor_tensor(y, ps[first_bank + g][:, :], g_b[:, i, n * 512:(n + 1) * 512], ALU.mult))
                xs = x3[:, t, n * 512:(n + 1) * 512]
                ins = v.tensor_tensor(xs, xs, y, ALU.add)
                ins.then_inc(sem(name + "_x"), 1)
            v.wait_ge(sem(name + "_x"), 4)
            v.tensor_copy(small[:, 21:22], small[:, 14:15]).then_inc(sem("x_ready"), 1)

        with nc.Block() as block:
            @block.sync
            def _(sp):
                load_router(sp, 0, inp["router_group_w"][0], inp["router_expert_w"][0].rearrange("d g e -> d (g e)"),
                            inp["router_group_b"], inp["router_expert_b"].rearrange("a g e -> a (g e)"))
                load_ada2(sp, range(3, ADA2_AHEAD))
                sp.wait_ge(sem("y1"), 4)
                load_expert(sp, 0, (4, 5))

            @block.tensor
            def _(pe):
                pe.wait_ge(sem("o_normed"), 1)
                for c in range(H):
                    b = ps[4 + c // 2]
                    for t in range(NT):
                        o = (c % 2) * S + t * P
                        last = pe.transpose(b[:, o:o + P], o3[:, t, c * P:(c + 1) * P], ident[:, :])
                    last.then_inc(sem("oT_psum"), 1)
                for g in range(4):
                    t, n = g // 2, g % 2
                    if t == 0:
                        pe.wait_ge(sem(f"wo1_loaded{n}"), 16)
                    pe.wait_ge(sem("oT_done"), H)
                    for c in range(KC):
                        last = pe.matmul(ps[g][:, :], oT[:, c, t * P:(t + 1) * P], cell(4 + n)[:, c, :],
                                         start=(c == 0), stop=(c == KC - 1))
                    last.then_inc(sem("y1"), 1)
                hT_tensor(pe, 1)

            @block.scalar
            def _(act):
                for t in range(NT):
                    act.activation(tmp[:, t * D:(t + 1) * D], o3[:, t, :], ACT.Square).then_inc(sem("o_sq"), 1)
                act.wait_ge(sem("o_ms"), 1)
                act.activation(st_a[:, 16:32], st_a[:, 0:16], ACT.Sqrt).then_inc(sem("o_root"), 1)
                rms_scalar(act, 1, xn_sb)

            @block.vector
            def _(v):
                v.wait_ge(sem("o_sq"), 2)
                v_step(v.tensor_reduce(st_a[:, 32:48], tmp[:, 0:2 * D].rearrange("p (g d) -> p g d", d=P), X, ALU.add))
                v.tensor_scalar(st_a[:, 0:16], st_a[:, 32:48], 1.0 / P, EPS, ALU.mult, ALU.add).then_inc(sem("o_ms"), 1)
                v.wait_ge(sem("o_root"), 1)
                v_step(v.reciprocal(st_a[:, 48:64], st_a[:, 16:32]))
                og = o_heads.rearrange("p (g d) -> p g d", d=P)
                v.tensor_tensor(og, og, st_a[:, 48:64].unsqueeze(2).broadcast_to((P, 16, P)), ALU.mult).then_inc(sem("o_normed"), 1)
                for c in range(H):
                    v.wait_ge(sem("oT_psum"), 2 * (c // 2) + 2)
                    o = (c % 2) * S
                    v.tensor_scalar(oT[:, c, :], ps[4 + c // 2][:, o:o + S], sub08, None, ALU.mult).then_inc(sem("oT_done"), 1)
                for i in range(0, ADA2_AHEAD, 2):
                    sum_ada2(v, i)
                residual(v, 0, None, 0, "y1")
                rms_vector(v, 1, xn3)
                hT_vector(v, 1)


        def route(k, ne, has_bg):
            EP = ne // NG
            NR = NG + ne
            W_TAB = ROUNDS * ne + 2
            rw = tmp[:, 2048:2048 + KC * NR].rearrange("p (c n) -> p c n", c=KC)
            bias = tmp[:, 2400:2400 + NR]
            pos = pos_t[:, 0:NT * W_TAB].rearrange("p (t n) -> p t n", t=NT)
            mask = mask_t[:, 0:NT * W_TAB].rearrange("p (t n) -> p t n", t=NT)
            gate = gate_t[:, 0:NT * W_TAB].rearrange("p (t n) -> p t n", t=NT)
            at = [2500]

            def t2(*dims):
                n = int(np.prod(dims))
                a = tmp[:, at[0]:at[0] + n]
                at[0] += n
                if len(dims) == 2:
                    return a.rearrange("p (t n) -> p t n", t=dims[0])
                if len(dims) == 3:
                    return a.rearrange("p (t g n) -> p t g n", t=dims[0], g=dims[1])
                return a
            L = t2(NT, NR)
            prio = t2(8)
            gm, em, zs, v1, m1, v2, m2, d12, w1, w2, gw = [t2(NT) for _ in range(11)]
            ohg, gs = t2(NT, NG), t2(NT, NG)
            prod = t2(NT, NG, EP)
            esel, e2, oh1, oh2, ew, em_ = [t2(NT, EP) for _ in range(6)]
            cnt, thr, rf = t2(ne), t2(4), t2(4)

            def per(a, n):
                return a.unsqueeze(2).broadcast_to((P, NT, n))

            with nc.Block() as block:
                @block.gpsimd
                def _(pool):
                    pool.iota(prio, pattern=[[-1, 8]], base=8, channel_multiplier=0,
                              allow_small_or_imprecise_dtypes=True).then_inc(sem("prio"), 1)

                @block.tensor
                def _(pe):
                    pe.wait_ge(sem(f"router{k}"), 64 if has_bg else 48)
                    for t in range(NT):
                        for c in range(KC):
                            last = pe.matmul(ps[0][:, t * NR:(t + 1) * NR], hT[:, c, t * P:(t + 1) * P], rw[:, c, :],
                                             start=(c == 0), stop=(c == KC - 1))
                    last.then_inc(sem("logits"), 1)
                    pe.wait_ge(sem("masked"), k + 1)
                    pe.matmul(ps[1][:, 0:ne], before[:, :], mask[:, 0, 0:ne], start=True, stop=True)
                    pe.matmul(ps[1][:, ne:2 * ne], ones[:, :], mask[:, 0, 0:ne], start=True, stop=False)
                    pe.matmul(ps[1][:, ne:2 * ne], before[:, :], mask[:, 1, 0:ne], start=False, stop=True)
                    pe.matmul(ps[1][:, 2 * ne:3 * ne], ones[:, :], mask[:, 0, 0:ne], start=True, stop=False)
                    pe.matmul(ps[1][:, 2 * ne:3 * ne], ones[:, :], mask[:, 1, 0:ne], start=False, stop=True).then_inc(
                        sem("places"), 1)

                @block.scalar
                def _(act):
                    act.wait_ge(sem("g_shifted"), k + 1)
                    act.activation(gs, gs, ACT.Exp).then_inc(sem("g_exp"), 1)
                    act.wait_ge(sem("d12"), k + 1)
                    act.activation(d12, d12, ACT.Exp).then_inc(sem("d12_exp"), 1)

                @block.vector
                def _(v):
                    v_step(v.memset(pos, 0.0))
                    v_step(v.memset(mask, 0.0))
                    v_step(v.memset(gate, 0.0))
                    v.wait_ge(sem("prio"), k + 1)
                    v.wait_ge(sem("logits"), k + 1)
                    if has_bg:
                        v_step(v.tensor_tensor(L, ps[0][:, 0:NT * NR].rearrange("p (t n) -> p t n", t=NT),
                                               bias.unsqueeze(1).broadcast_to((P, NT, NR)), ALU.add))
                    else:
                        v_step(v.tensor_copy(L, ps[0][:, 0:NT * NR].rearrange("p (t n) -> p t n", t=NT)))
                        v_step(v.tensor_tensor(L[:, :, NG:], L[:, :, NG:],
                                               bias[:, NG:].unsqueeze(1).broadcast_to((P, NT, ne)), ALU.add))
                    G = L[:, :, 0:NG]
                    E4 = L[:, :, NG:].rearrange("p t (g e) -> p t g e", g=NG)

                    def first_max(src, n, top, best, oh):
                        v_step(v.tensor_reduce(top, src, X, ALU.max))
                        v_step(v.tensor_tensor(oh, src, per(top, n), ALU.is_equal))
                        v_step(v.tensor_tensor(oh, oh, prio[:, 0:n].unsqueeze(1).broadcast_to((P, NT, n)), ALU.mult))
                        v_step(v.tensor_reduce(best, oh, X, ALU.max))
                        v_step(v.tensor_tensor(oh, oh, per(best, n), ALU.is_equal))
                    first_max(G, NG, gm, em, ohg)
                    v.tensor_tensor(gs, G, per(gm, NG), ALU.subtract).then_inc(sem("g_shifted"), 1)
                    v_step(v.tensor_tensor(prod, E4, ohg.unsqueeze(3).broadcast_to((P, NT, NG, EP)), ALU.mult))
                    v_step(v.tensor_reduce(esel, prod.rearrange("p t g e -> p t e g"), X, ALU.add))
                    first_max(esel, EP, v1, m1, oh1)
                    v_step(v.scalar_tensor_tensor(e2, oh1, -BIG, esel, ALU.mult, ALU.add))
                    first_max(e2, EP, v2, m2, oh2)
                    v.tensor_tensor(d12, v2, v1, ALU.subtract).then_inc(sem("d12"), 1)
                    v.wait_ge(sem("g_exp"), k + 1)
                    v_step(v.tensor_reduce(zs, gs, X, ALU.add))
                    v_step(v.reciprocal(gw, zs))
                    v.wait_ge(sem("d12_exp"), k + 1)
                    v_step(v.tensor_scalar(w1, d12, 1.0, None, ALU.add))
                    v_step(v.reciprocal(w1, w1))
                    v_step(v.tensor_tensor(w1, w1, gw, ALU.mult))
                    v_step(v.tensor_tensor(w2, w1, d12, ALU.mult))
                    v_step(v.tensor_tensor(em_, oh1, oh2, ALU.add))
                    v_step(v.tensor_tensor(oh1, oh1, per(w1, EP), ALU.mult))
                    v_step(v.tensor_tensor(oh2, oh2, per(w2, EP), ALU.mult))
                    v_step(v.tensor_tensor(ew, oh1, oh2, ALU.add))
                    for dst, src in ((mask, em_), (gate, ew)):
                        ins = v.tensor_tensor(dst[:, :, 0:ne].rearrange("p t (g e) -> p t g e", g=NG),
                                              ohg.unsqueeze(3).broadcast_to((P, NT, NG, EP)),
                                              src.unsqueeze(2).broadcast_to((P, NT, NG, EP)), ALU.mult)
                        if dst is mask:
                            ins.then_inc(sem("masked"), 1)
                        else:
                            v_step(ins)
                    v.wait_ge(sem("masked"), k + 1)
                    for q in range(1, ROUNDS):
                        v.tensor_copy(mask[:, :, q * ne:(q + 1) * ne], mask[:, :, 0:ne])
                        v.tensor_copy(gate[:, :, q * ne:(q + 1) * ne], gate[:, :, 0:ne])
                    v.wait_ge(sem("places"), k + 1)
                    pp = ps[1][:, 0:NT * ne].rearrange("p (t n) -> p t n", t=NT)
                    for q in range(ROUNDS):
                        v.tensor_scalar(pos[:, :, q * ne:(q + 1) * ne], pp, -float(q * SLOTS), None, ALU.add)
                    v_step(v.tensor_reduce(cnt[:, 0:1], ps[1][:, 2 * ne:3 * ne], X, ALU.max))
                    for q in range(1, ROUNDS):
                        v_step(v.tensor_scalar(thr[:, q:q + 1], cnt[:, 0:1], float(q * SLOTS), None, ALU.is_gt))
                    v_step(v.tensor_tensor(rf[:, 0:1], thr[:, 1:2], thr[:, 2:3], ALU.add))
                    v_step(v.tensor_tensor(rf[:, 0:1], rf[:, 0:1], thr[:, 3:4], ALU.add))
                    v_step(v.tensor_scalar(rounds_i[:, :], rf[:, 0:1], 1.0, None, ALU.add))

        def experts(k, ne, sides=None, more_loads=None, ahead=True):
            NP = ne // 2
            W_TAB = ROUNDS * ne + 2
            pos = pos_t[:, 0:NT * W_TAB].rearrange("p (t n) -> p t n", t=NT)
            mask = mask_t[:, 0:NT * W_TAB].rearrange("p (t n) -> p t n", t=NT)
            gate = gate_t[:, 0:NT * W_TAB].rearrange("p (t n) -> p t n", t=NT)
            xg = hT_sb[:, 0:1024].rearrange("p (c n) -> p c n", c=KC)
            outb = hT_sb[:, 1024:2048]
            hid = tmp[:, 0:FE]
            hidT = tmp[:, FE:2 * FE].rearrange("p (f n) -> p f n", f=FC)
            oh = tmp[:, 1024:1280].rearrange("p (t n) -> p t n", t=NT)
            ohw = tmp[:, 1280:1536].rearrange("p (t n) -> p t n", t=NT)
            pT = tmp[:, 1536:1792]
            zero = tmp[:, 1792:1792 + 512]
            y_ps, gate_ps, up_ps, out_ps = ps[0:4], ps[4], ps[5], ps[6:8]
            n = f"{k}"

            def dst(e, j):
                return expert_cell(3 * e + j)

            def load_pair(sp, pair, it):
                for j in range(3):
                    sp.wait_ge(sem(("gate_used", "up_used", "down_used")[j] + n), it)
                    for e in range(2):
                        w = MOE[k][j][bass.ds(2 * pair + e, 1), :, :].rearrange("o (c p) n -> p (o c) n", p=P)
                        sp.dma_start(dst(e, j), w).then_inc(sem(f"moe{n}_loaded{3 * e + j}"), 16)

            with nc.Block() as block:
                @block.sync
                def _(sp):
                    if not ahead:
                        load_expert(sp, k, (0, 3, 1, 4, 2, 5))
                    if sides is not None:
                        sides(sp, 0)
                    with sp.Fori(1, NP) as pair:
                        load_pair(sp, pair, pair)
                        if sides is not None:
                            sides(sp, pair)
                    rounds = sp.value_load(rounds_i[0:1, 0:1], min_val=1, max_val=ROUNDS)
                    with sp.If(rounds > 1):
                        with sp.Fori(1, rounds) as q:
                            with sp.Fori(0, NP) as pair:
                                load_pair(sp, pair, q * NP + pair)
                    sp.nop()
                    if more_loads is not None:
                        more_loads(sp)

                @block.tensor
                def _(pe):
                    rounds = pe.value_load(rounds_i[0:1, 0:1], min_val=1, max_val=ROUNDS)

                    def gather(half):
                        for c in range(4 * half, 4 * half + 4):
                            for t in range(NT):
                                last = pe.matmul((gate_ps, up_ps)[half][:, (c % 4) * P:(c % 4 + 1) * P],
                                                 xn3[:, t, c * P:(c + 1) * P], oh[:, t, :],
                                                 start=(t == 0), stop=(t == NT - 1))
                        last.then_inc(sem("gat_psum" + n), 1)

                    def project(j, bank):
                        for c in range(KC):
                            for e in range(2):
                                last = pe.matmul(bank[e * SLOTS:(e + 1) * SLOTS, :], xg[:, c, e * SLOTS:(e + 1) * SLOTS],
                                                 dst(e, j)[:, c, :], start=(c == 0), stop=(c == KC - 1))
                        return last

                    def down():
                        for h in range(2):
                            for f in range(FC):
                                for e in range(2):
                                    last = pe.matmul(out_ps[h][e * SLOTS:(e + 1) * SLOTS, :],
                                                     hidT[:, f, e * SLOTS:(e + 1) * SLOTS],
                                                     dst(e, 2)[:, f, h * 512:(h + 1) * 512],
                                                     start=(f == 0), stop=(f == FC - 1))
                        last.then_inc(sem("down_used" + n), 1)

                    def scatter(stop):
                        for t in range(NT):
                            for h in range(2):
                                last = pe.matmul(y_ps[2 * t + h][:, :], pT[:, t * P:(t + 1) * P], outb[:, h * 512:(h + 1) * 512],
                                                 start=False, stop=stop, skip_group_check=True)
                        return last

                    pe.wait_ge(sem("moe_zero" + n), 1)
                    for b in range(4):
                        pe.matmul(y_ps[b][:, :], zero[:, 0:P], zero, start=True, stop=False, skip_group_check=True)
                    pe.wait_ge(sem("oh_done" + n), 1)
                    gather(0)
                    gather(1)
                    with pe.Fori(0, rounds * NP) as it:
                        pe.wait_ge(sem("gat_done" + n), 2 * it + 2)
                        for e in range(2):
                            pe.wait_ge(sem(f"moe{n}_loaded{3 * e}"), 16 * it + 16)
                        project(0, gate_ps).then_inc(sem("gate_used" + n), 1)
                        pe.wait_ge(sem("out0_done" + n), it + 1)
                        pe.wait_ge(sem("out1_done" + n), it + 1)
                        pe.wait_ge(sem("pT_done" + n), it + 1)
                        scatter(False)
                        pe.wait_ge(sem("oh_done" + n), it + 1)
                        for t in range(NT):
                            last = pe.transpose(out_ps[1][:, t * P:(t + 1) * P], ohw[:, t, :], ident[:, :])
                        last.then_inc(sem("pT_psum" + n), 1)
                        for e in range(2):
                            pe.wait_ge(sem(f"moe{n}_loaded{3 * e + 1}"), 16 * it + 16)
                        project(1, up_ps).then_inc(sem("up_used" + n), 1)
                        pe.wait_ge(sem("hid_done" + n), it + 1)
                        for f in range(FC):
                            last = pe.transpose(out_ps[0][:, f * P:(f + 1) * P], hid[:, f * P:(f + 1) * P], ident[:, :])
                        last.then_inc(sem("hidT_psum" + n), 1)
                        pe.wait_ge(sem("oh_done" + n), it + 2)
                        gather(0)
                        gather(1)
                        pe.wait_ge(sem("pT_done" + n), it + 2)
                        pe.wait_ge(sem("hidT_done" + n), it + 1)
                        for e in range(2):
                            pe.wait_ge(sem(f"moe{n}_loaded{3 * e + 2}"), 16 * it + 16)
                        down()
                    pe.wait_ge(sem("out0_done" + n), rounds * NP + 1)
                    pe.wait_ge(sem("out1_done" + n), rounds * NP + 1)
                    scatter(True).then_inc(sem("y_done" + n), 1)

                @block.scalar
                def _(act):
                    rounds = act.value_load(rounds_i[0:1, 0:1], min_val=1, max_val=ROUNDS)

                    def take(half, count):
                        act.wait_ge(sem("gat_psum" + n), count)
                        for c in range(4 * half, 4 * half + 4):
                            last = act.activation(xg[:, c, :], (gate_ps, up_ps)[half][:, (c % 4) * P:(c % 4 + 1) * P],
                                                  ACT.Identity, scale=modc[:, 2 * KC + c:2 * KC + c + 1],
                                                  bias=modc[:, 3 * KC + c:3 * KC + c + 1])
                        last.then_inc(sem("gat_done" + n), 1)
                    take(0, 1)
                    take(1, 2)
                    with act.Fori(0, rounds * NP) as it:
                        act.wait_ge(sem("gate_used" + n), it + 1)
                        act.activation(hid, gate_ps[:, :], ACT.Sigmoid).then_inc(sem("sig_done" + n), 1)
                        take(0, 2 * it + 3)
                        take(1, 2 * it + 4)
                        act.wait_ge(sem("down_used" + n), it + 1)
                        act.activation(outb[:, 512:1024], out_ps[1][:, :], ACT.Copy).then_inc(sem("out1_done" + n), 1)

                @block.vector
                def _(v):
                    rounds = v.value_load(rounds_i[0:1, 0:1], min_val=1, max_val=ROUNDS)

                    def slots_of(col):
                        for e in range(2):
                            for t in range(NT):
                                if isinstance(col, int):
                                    p1, m1, g1 = [a[:, t, col + e:col + e + 1] for a in (pos, mask, gate)]
                                else:
                                    p1, m1, g1 = [a[:, t, bass.ds(col + e, 1)] for a in (pos, mask, gate)]
                                v.tensor_scalar(oh[:, t, e * SLOTS:(e + 1) * SLOTS], slot_ids[:, :], p1, m1,
                                                ALU.is_equal, ALU.mult)
                                last = v.tensor_scalar(ohw[:, t, e * SLOTS:(e + 1) * SLOTS], slot_ids[:, :], p1, g1,
                                                       ALU.is_equal, ALU.mult)
                        last.then_inc(sem("oh_done" + n), 1)

                    def body(it, side):
                        v.wait_ge(sem("sig_done" + n), it + 1)
                        v.tensor_tensor(hid, gate_ps[:, :], hid, ALU.mult).then_inc(sem("silu" + n), 1)
                        v.wait_ge(sem("pT_psum" + n), it + 1)
                        v.tensor_copy(pT, out_ps[1][:, 0:256]).then_inc(sem("pT_done" + n), 1)
                        slots_of(2 * it + 2)
                        v.wait_ge(sem("silu" + n), it + 1)
                        v.wait_ge(sem("up_used" + n), it + 1)
                        v.tensor_tensor(hid, up_ps[:, :], hid, ALU.mult).then_inc(sem("hid_done" + n), 1)
                        v.wait_ge(sem("hidT_psum" + n), it + 1)
                        v.tensor_copy(hidT, out_ps[0][:, :].rearrange("p (f n) -> p f n", f=FC)).then_inc(
                            sem("hidT_done" + n), 1)
                        if side is not None:
                            side(v, it)
                        v.wait_ge(sem("down_used" + n), it + 1)
                        v.tensor_copy(outb[:, 0:512], out_ps[0][:, :]).then_inc(sem("out0_done" + n), 1)

                    v.memset(zero, 0.0).then_inc(sem("moe_zero" + n), 1)
                    v.memset(pT, 0.0).then_inc(sem("pT_done" + n), 1)
                    v.memset(outb[:, 0:512], 0.0).then_inc(sem("out0_done" + n), 1)
                    v.memset(outb[:, 512:1024], 0.0).then_inc(sem("out1_done" + n), 1)
                    slots_of(0)
                    if sides is None:
                        with v.Fori(0, rounds * NP) as it:
                            body(it, None)
                    else:
                        with v.Fori(0, NP) as it:
                            body(it, sides)
                        with v.If(rounds > 1):
                            with v.Fori(NP, rounds * NP) as it:
                                body(it, None)
                        v.nop()
                    v.wait_ge(sem("y_done" + n), 1)
                    for g in range(4):
                        t, h = g // 2, g % 2
                        y = tmp[:, 2304 + (g % 2) * 512:2304 + (g % 2 + 1) * 512]
                        v_step(v.tensor_tensor(y, y_ps[g][:, :], g_b[:, 1, h * 512:(h + 1) * 512], ALU.mult))
                        xs = x3[:, t, h * 512:(h + 1) * 512]
                        ins = v.tensor_tensor(xs, xs, y, ALU.add)
                        if g < 3:
                            v_step(ins)
                        else:
                            ins.then_inc(sem("x_ready"), 1)

        def ada2_side(eng, it):
            n2 = ADA2_PER_PAIR
            for j in range(n2):
                ws = ada2_slot(j)
                before_ = len([i for i in range(ADA2_AHEAD) if i % 5 == j])
                first_col = ADA2_AHEAD * AW + j * AW
                if eng is nc.sync:
                    cols = (slice(first_col, first_col + AW) if isinstance(it, int) else
                            bass.ds(it * (n2 * AW) + first_col, AW))
                    eng.wait_ge(sem(f"ada2_used{j}"), it + before_)
                    eng.dma_start(ws, inp["ada_w_2"][0][:, cols].rearrange("(c p) n -> p c n", p=P)).then_inc(
                        sem(f"ada2_loaded{j}"), 16)
                else:
                    a = acc[:, bass.ds(it * (n2 * AW) + first_col, AW)]
                    eng.wait_ge(sem(f"ada2_loaded{j}"), 16 * it + 16 * (before_ + 1))
                    for c in range(KC):
                        s = cond[:, KC + c:KC + c + 1]
                        if c == 0:
                            ins = eng.tensor_scalar(a, ws[:, c, :], s, None, ALU.mult)
                        else:
                            ins = eng.scalar_tensor_tensor(a, ws[:, c, :], s, a, ALU.mult, ALU.add)
                        if c < KC - 1:
                            ins.then_inc(sem("ada2_chain"), 1)
                            eng.wait_ge(sem("ada2_chain"), it * (n2 * (KC - 1)) + j * (KC - 1) + c + 1)
                        else:
                            ins.then_inc(sem(f"ada2_used{j}"), 1)

        route(0, 16, True)
        if until > 4:
            experts(0, 16, sides=ada2_side,
                    more_loads=lambda sp: sp.dma_start(
                        g_b[:, 0, :], inp["norm_final"].rearrange("(a n) -> a n", a=1).broadcast_to((P, D))).then_inc(
                            sem("nf_loaded"), 16))
        if debug and until <= 5:
            debug(nc, sem, locals())
            return

        give_back()
        w_in = inp["w_in_2"][0]
        MIX_CELLS = 4
        SH0 = 1064
        GA0 = SH0 + 1824
        pieces = [(0, 512), (512, 1024), (SH0, SH0 + 512), (SH0 + 512, SH0 + 1024), (SH0 + 1024, SH0 + 1536),
                  (SH0 + 1536, GA0)]
        LORA, GATE0 = 6, 7

        def p2_wait(sp, i):
            if i >= MIX_CELLS:
                sp.wait_ge(sem("p2_used"), i - MIX_CELLS + 1)

        def p2_load(sp, i, dst, src):
            sp.dma_start(dst, src).then_inc(sem(f"p2_loaded{i % MIX_CELLS}"), 16)

        p2_loads = {}
        count = [0] * MIX_CELLS
        for i in range(GATE0 + 4):
            count[i % MIX_CELLS] += 5 if i == LORA else 1
            p2_loads[i] = 16 * count[i % MIX_CELLS]

        def p2_ready(pe, i):
            pe.wait_ge(sem(f"p2_loaded{i % MIX_CELLS}"), p2_loads[i])

        def p2(i, kc=8, w=512):
            return cell(i % MIX_CELLS, kc, w)

        q_tok = tmp[:, 0:1024].rearrange("p (t d) -> p t d", t=NT)
        kvl = tmp[:, 1024:1536].rearrange("p (t d) -> p t d", t=NT)
        qiT = tmp[:, 1536:2048].rearrange("p (c s) -> p c s", c=2)
        kiT = tmp[:, 2048:2304]
        wi_w = tmp[:, 3008:3072].rearrange("p (c n) -> p c n", c=KC)
        krep = tmp[:, 3072:4096].rearrange("p (c n) -> p c n", c=KC)
        w_idx = small[:, 24:40]
        omm = small[:, 40:55]
        mixed = ring[:, 4 * CELL:4 * CELL + 15 * S].rearrange("p (c s) -> p c s", c=15)
        lora = p2(LORA, 1, 4096)[:, 0, :]
        M_STRICT, M_INCL = pos_t[:, 0:P], pos_t[:, P:2 * P]
        M_16, M_OFF = mask_t[:, 0:P], mask_t[:, P:2 * P]
        M_16L = gate_t[:, 0:P]
        chunk_of = gate_t[:, P:P + 4]

        with nc.Block() as block:
            @block.sync
            def _(sp):
                for i in range(4):
                    p2_load(sp, i, p2(i), w_cols(w_in, *pieces[i]))
                for i, m in enumerate((2, 5)):
                    sp.dma_start(side[:, i * D:(i + 1) * D], inp["ada_b_2"][0:1, m * D:(m + 1) * D].broadcast_to((P, D))).then_inc(
                        sem("gb2_loaded"), 16)
                for r in range(4):
                    sp.dma_start(krep[:, :, r * 32:(r + 1) * 32], w_cols(w_in, 1024, 1056)).then_inc(sem("ki_loaded"), 16)
                sp.dma_start(wi_w, w_cols(w_in, 1056, 1064)).then_inc(sem("ki_loaded"), 16)
                p2_wait(sp, 4)
                p2_load(sp, 4, p2(4), w_cols(w_in, *pieces[4]))
                p2_wait(sp, 5)
                p2_load(sp, 5, p2(5)[:, :, 0:288], w_cols(w_in, *pieces[5]))
                p2_wait(sp, LORA)
                sp.wait_ge(sem("lora_zero"), 1)
                p2_load(sp, LORA, lora[0:64, 0:512], inp["rwkv_w2_2"][0])
                p2_load(sp, LORA, lora[64:128, 0:512], inp["rwkv_a2_2"][0])
                p2_load(sp, LORA, lora[:, 512:1024], inp["rwkv_g2_2"][0][0:128, :])
                p2_load(sp, LORA, lora[0:32, 1024:1536], inp["rwkv_g2_2"][0][128:160, :])
                p2_load(sp, LORA, lora[:, 1536:3584].rearrange("p (c n) -> p c n", c=2),
                        inp["w_kv_up_2"][0].rearrange("(c p) n -> p c n", p=P))
                p2_wait(sp, GATE0)
                p2_load(sp, GATE0, p2(GATE0), w_cols(w_in, GA0, GA0 + 512))

            @block.gpsimd
            def _(pool):
                pool.memset(mixed[:, 14, :], 0.0).then_inc(sem("mixed_zero"), 1)
                pool.wait_ge(sem("mixed_zero"), 1)
                for m in (M_STRICT, M_INCL, M_16, M_OFF, M_16L, chunk_of):
                    p_step(pool.memset(m, 0.0 if m is M_OFF else 1.0))

                def block_mask(m, size, upper, strict):
                    v3_ = m.rearrange("p (b n) -> p b n", n=size)
                    s_ = 1 if upper else -1
                    p_step(pool.affine_select(out=v3_, in_=v3_, compare_op=ALU.is_gt if strict else ALU.is_ge, fill=0.0,
                                              base=0, pattern=[[s_ * size, P // size], [s_, size]], channel_multiplier=-s_))
                    p_step(pool.affine_select(out=v3_, in_=v3_, compare_op=ALU.is_ge, fill=0.0, base=0,
                                              pattern=[[-size, P // size], [0, size]], channel_multiplier=1))
                    p_step(pool.affine_select(out=v3_, in_=v3_, compare_op=ALU.is_gt, fill=0.0, base=size,
                                              pattern=[[size, P // size], [0, size]], channel_multiplier=-1))
                block_mask(M_STRICT, 32, True, True)
                block_mask(M_INCL, 32, True, False)
                block_mask(M_16, 16, True, True)
                block_mask(M_16L, 16, False, True)
                p_step(pool.tensor_tensor(M_OFF, M_STRICT, M_16, ALU.subtract))
                p_step(pool.affine_select(out=chunk_of, in_=chunk_of, compare_op=ALU.is_ge, fill=0.0, base=0,
                                          pattern=[[-32, 4]], channel_multiplier=1))
                p_step(pool.affine_select(out=chunk_of, in_=chunk_of, compare_op=ALU.is_gt, fill=0.0, base=32,
                                          pattern=[[32, 4]], channel_multiplier=-1))
                pool.wait_ge(sem("p2_used"), LORA - MIX_CELLS + 1)
                pool.memset(lora[:, 1024:1536], 0.0).then_inc(sem("lora_zero"), 1)

            @block.tensor
            def _(pe):
                ada_columns(pe, (0, 1), 1, "modc_psum")
                ada_columns(pe, (3, 4), 2, "modc_psum")
                hT_tensor(pe, 2)
                pe.wait_ge(sem("hT_done"), 3 * KC)
                for t in range(NT):
                    if t == 0:
                        p2_ready(pe, 0)
                    for c in range(KC):
                        last = pe.matmul(ps[t][:, :], hT[:, c, t * P:(t + 1) * P], p2(0)[:, c, :], start=(c == 0), stop=(c == KC - 1))
                    last.then_inc(sem("pj_q"), 1)
                last_q = last
                p2_ready(pe, 1)
                for t in range(NT):
                    for c in range(KC):
                        last = pe.matmul(ps[2][:, t * S:(t + 1) * S], hT[:, c, t * P:(t + 1) * P], p2(1)[:, c, 0:S],
                                         start=(c == 0), stop=(c == KC - 1))
                last.then_inc(sem("pj_kv"), 1)
                for j in range(2):
                    for c in range(KC):
                        last = pe.matmul(ps[3][:, j * S:(j + 1) * S], p2(1)[:, c, S + j * P:S + (j + 1) * P], hT[:, c, :],
                                         start=(c == 0), stop=(c == KC - 1))
                last.then_inc(sem("pj_qi"), 1)
                pe.wait_ge(sem("ki_loaded"), 80)
                pe.wait_ge(sem("hT_done"), 3 * KC)
                for c in range(KC):
                    last = pe.matmul(ps[4][:, 0:S], krep[:, c, :], hT[:, c, :], start=(c == 0), stop=(c == KC - 1))
                for t in range(NT):
                    for c in range(KC):
                        last = pe.matmul(ps[4][:, S + t * 8:S + (t + 1) * 8], hT[:, c, t * P:(t + 1) * P], wi_w[:, c, :],
                                         start=(c == 0), stop=(c == KC - 1))
                last.then_inc(sem("pj_ki"), 1)
                pe.wait_ge(sem("pj_q_out"), 2)
                ada_rows(pe, 2, 0, "g_psum")
                pe.wait_ge(sem("g_out"), 3)
                ada_rows(pe, 5, 0, "g_psum")
                pe.wait_ge(sem("g_out"), 4)
                pe.wait_ge(sem("pj_kv_out"), 1)
                pe.wait_ge(sem("pj_qi_out"), 1)
                for i in range(2):
                    pe.matmul(ps[5][:, 0:1], ident[:, :], ones[:, 0:1], start=True, stop=True).then_inc(sem("p2_used"), 1)
                for m in range(15):
                    i = 2 + m // 4 if m < 12 else 5
                    o = (m % 4) * P if m < 12 else (m - 12) * P
                    n = 32 if m == 14 else P
                    if o == 0:
                        p2_ready(pe, i)
                    if m >= 4:
                        pe.wait_ge(sem("mixed_done"), m - 3)
                    for c in range(KC):
                        last = pe.matmul(ps[m % 4][0:n, 0:S], p2(i)[:, c, o:o + n], hT[:, c, :], start=(c == 0), stop=(c == KC - 1))
                    last.then_inc(sem("pj_shift"), 1)
                    if m in (3, 7, 11, 14):
                        pe.matmul(ps[5][:, 0:1], ident[:, :], ones[:, 0:1], start=True, stop=True).then_inc(sem("p2_used"), 1)

            @block.scalar
            def _(act):
                rms_scalar(act, 2, xn_sb)
                rms_scalar(act, 3, xn_sb)
                for t in range(NT):
                    act.wait_ge(sem("pj_q"), t + 1)
                    act.activation(q_tok[:, t, :], ps[t][:, :], ACT.Copy).then_inc(sem("pj_q_out"), 1)
                act.wait_ge(sem("pj_kv"), 1)
                act.activation(tmp[:, 1024:1536], ps[2][:, :], ACT.Copy).then_inc(sem("pj_kv_out"), 1)
                act.wait_ge(sem("pj_qi"), 1)
                act.activation(tmp[:, 1536:2048], ps[3][:, :], ACT.Copy).then_inc(sem("pj_qi_out"), 1)
                act.wait_ge(sem("pj_ki"), 1)
                act.activation(kiT, ps[4][:, 0:S], ACT.Copy).then_inc(sem("pj_ki_out"), 1)
                act.activation(w_idx, ps[4][:, S:S + 16], ACT.Copy, scale=1.0 / 16.0).then_inc(sem("pj_ki_out"), 1)
                act.wait_ge(sem("omm"), 1)
                act.wait_ge(sem("mixed_zero"), 1)
                for m in range(15):
                    n = 32 if m == 14 else P
                    act.wait_ge(sem("pj_shift"), m + 1)
                    act.activation(mixed[0:n, m, :], ps[m % 4][0:n, 0:S], ACT.Copy, scale=omm[0:n, m:m + 1]).then_inc(
                        sem("mixed_own"), 1)

            @block.vector
            def _(v):
                v.wait_ge(sem("nf_loaded"), 16)
                rms_vector(v, 2, x3, weight=g_b[:, 0, :], name="x_ready")
                rms_vector(v, 3, xn3)
                v.wait_ge(sem("modc_psum"), 3)
                fill_modc(v, 0, KC, ps[1], 0, KC, colA("mix_norm_g_2", 0, KC), colB("ada_b_2", 0, KC), colB("ada_b_2", KC, KC))
                v.wait_ge(sem("modc_psum"), 4)
                fill_modc(v, 2 * KC, 3 * KC, ps[2], 0, KC, colA("moe_norm_g_2", 0, KC), colB("ada_b_2", 3 * KC, KC),
                          colB("ada_b_2", 4 * KC, KC))
                hT_vector(v, 2)
                v.tensor_scalar(omm, colsB[:, MU0:MU0 + 15], -1.0, 1.0, ALU.mult, ALU.add).then_inc(sem("omm"), 1)
                v.wait_ge(sem("gb2_loaded"), 32)
                for i in range(2):
                    v.wait_ge(sem("g_psum"), i + 3)
                    for n in range(2):
                        a = g_b[:, i, n * 512:(n + 1) * 512]
                        ins = v.tensor_tensor(a, ps[n][:, :], side[:, i * D + n * 512:i * D + (n + 1) * 512], ALU.add)
                    ins.then_inc(sem("g_out"), 1)
                for m in range(15):
                    n = 32 if m == 14 else P
                    v.wait_ge(sem("mixed_own"), m + 1)
                    a = mixed[0:n, m, 1:S]
                    v.scalar_tensor_tensor(a, ps[m % 4][0:n, 0:S - 1], colsB[0:n, MU0 + m:MU0 + m + 1], a, ALU.mult, ALU.add).then_inc(
                        sem("mixed_done"), 1)

        if debug and until <= 6:
            debug(nc, sem, locals())
            return

        give_back()
        k_tok = side[:, 0:1024].rearrange("p (t d) -> p t d", t=NT)
        vv_tok = side[:, 1024:2048].rearrange("p (t d) -> p t d", t=NT)
        qT2 = side[:, 2048:3072].rearrange("p (c s) -> p c s", c=4)
        kT2 = side[:, 3072:4096].rearrange("p (c s) -> p c s", c=4)
        latT = side[:, 4096:4608].rearrange("p (c s) -> p c s", c=2)
        work = side[:, 4608:5120].rearrange("p (t s) -> p t s", t=NT)
        drop = side[:, 5120:5632].rearrange("p (t s) -> p t s", t=NT)
        dst2 = side[:, 5632:6144].rearrange("p (t s) -> p t s", t=NT)
        o_tok = side[:, 6144:7168].rearrange("p (t d) -> p t d", t=NT)
        oaT = side[:, 7168:8192].rearrange("p (c s) -> p c s", c=4)
        sq6 = acc[:, 0:1024]
        rl = acc[:, 1024:2048].rearrange("p (b s) -> p b s", b=4)
        lg = acc[:, 2048:2560].rearrange("p (b s) -> p b s", b=2)
        ee = acc[:, 2560:3072].rearrange("p (b s) -> p b s", b=2)
        eT = acc[:, 3072:3584].rearrange("p (b s) -> p b s", b=2)
        st6 = acc[:, 3584:3840]
        TAKEN = -3.3e38
        TOPK = 64
        kv_up = lora[:, 1536:3584].rearrange("p (c n) -> p c n", c=2)

        def load_gates(sp, i):
            p2_load(sp, GATE0 + i, p2(GATE0 + i), w_cols(w_in, GA0 + i * 512, GA0 + (i + 1) * 512))

        gates_sb = p2(GATE0).rearrange("p (k t) (w n) -> p w k t n", t=NT, w=4)

        with nc.Block() as block:
            @block.sync
            def _(sp):
                load_gates(sp, 1)
                load_gates(sp, 2)

            @block.gpsimd
            def _(pool):
                pool.iota(dst2, pattern=[[P, NT], [-1, S]], base=0, channel_multiplier=1,
                          allow_small_or_imprecise_dtypes=True).then_inc(sem("dst2"), 1)
                for t in range(NT):
                    pool.wait_ge(sem("idx_score"), t + 1)
                    pool.affine_select(out=work[:, t, :], in_=work[:, t, :], compare_op=ALU.is_ge, fill=-BIG, base=t * P,
                                       pattern=[[-1, S]], channel_multiplier=1).then_inc(sem("idx_causal"), 1)
                pool.wait_ge(sem("drop_raw"), 1)
                for t in range(NT):
                    pool.affine_select(out=drop[:, t, :], in_=drop[:, t, :], compare_op=ALU.is_ge, fill=-1.0, base=t * P,
                                       pattern=[[-1, S]], channel_multiplier=1).then_inc(sem("drop"), 1)

            @block.tensor
            def _(pe):
                def dots(u):
                    t, h = u // 8, u % 8
                    r = 32 * (h % 4)
                    if u >= 4:
                        pe.wait_ge(sem("idx_relu"), u - 3)
                    pe.matmul(ps[h % 4][:, 0:S], qiT[r:r + 32, h // 4, t * P:(t + 1) * P], kiT[r:r + 32, :],
                              start=True, stop=True).then_inc(sem("idx_dots"), 1)
                for u in range(4):
                    dots(u)
                pe.wait_ge(sem("lat_normed"), 1)
                for c in range(2):
                    for t in range(NT):
                        last = pe.transpose(ps[4][:, c * S + t * P:c * S + (t + 1) * P], kvl[:, t, c * P:(c + 1) * P], ident[:, :])
                last.then_inc(sem("lat_psum"), 1)
                pe.wait_ge(sem("q_normed"), 1)
                for c in range(4):
                    for t in range(NT):
                        last = pe.transpose(ps[5 + c // 2][:, (c % 2) * S + t * P:(c % 2) * S + (t + 1) * P],
                                            q_tok[:, t, c * P:(c + 1) * P], ident[:, :])
                last.then_inc(sem("q_psum"), 1)
                for u in range(4, 8):
                    dots(u)
                p2_ready(pe, LORA)
                pe.wait_ge(sem("latT_done"), 2)
                for n in range(2):
                    for t in range(NT):
                        if n == 0 and t == 1:
                            pe.wait_ge(sem("latT_done"), 2)
                        if n == 1:
                            pe.wait_ge(sem("kv_out"), t + 1)
                            if t == 0:
                                pe.wait_ge(sem("qT_done"), 4)
                        b = ps[7] if (t == 0) else ps[4]
                        for c in range(2):
                            last = pe.matmul(b[:, :], latT[:, c, t * P:(t + 1) * P], kv_up[:, c, n * 512:(n + 1) * 512],
                                             start=(c == 0), stop=(c == 1))
                        last.then_inc(sem("kv_psum"), 1)
                for u in range(8, 16):
                    dots(u)
                pe.wait_ge(sem("k_normed"), 1)
                for c in range(4):
                    for t in range(NT):
                        last = pe.transpose(ps[5 + c // 2][:, (c % 2) * S + t * P:(c % 2) * S + (t + 1) * P],
                                            k_tok[:, t, c * P:(c + 1) * P], ident[:, :])
                last.then_inc(sem("k_psum"), 1)

                def scores(u):
                    h, t = u // NT, u % NT
                    jo = (h % 2) * 64
                    if u == 0:
                        pe.wait_ge(sem("kT_done"), 4)
                        pe.wait_ge(sem("idx_relu"), 16)
                    if u >= 4:
                        pe.wait_ge(sem("sa_biased"), u - 3)
                    pe.matmul(ps[u % 4][:, 0:S], qT2[jo:jo + 64, h // 2, t * P:(t + 1) * P], kT2[jo:jo + 64, h // 2, :],
                              start=True, stop=True).then_inc(sem("sa_scores"), 1)

                def turn(u):
                    pe.wait_ge(sem("sa_exp"), u + 1)
                    if u >= 2:
                        pe.wait_ge(sem("sa_eT"), u - 1)
                    if u == 0:
                        pe.wait_ge(sem("kv_out"), 4)
                    for k in range(2):
                        last = pe.transpose(ps[4 + u % 2][:, k * P:(k + 1) * P], ee[:, u % 2, k * P:(k + 1) * P], ident[:, :])
                    last.then_inc(sem("sa_eT_psum"), 1)

                def av(u):
                    h = u // NT
                    pe.wait_ge(sem("sa_eT"), u + 1)
                    if u >= 2:
                        pe.wait_ge(sem("sa_o"), u - 1)
                    for k in range(2):
                        last = pe.matmul(ps[6 + u % 2][:, 0:64], eT[:, u % 2, k * P:(k + 1) * P],
                                         vv_tok[:, k, h * 64:(h + 1) * 64], start=(k == 0), stop=(k == 1))
                    last.then_inc(sem("sa_av"), 1)
                scores(0)
                scores(1)
                for u in range(17):
                    if u + 2 < 16:
                        scores(u + 2)
                    if u < 16:
                        turn(u)
                    if u >= 1:
                        av(u - 1)
                pe.wait_ge(sem("sa_o"), 16)
                pe.wait_ge(sem("sa_eT"), 16)
                for c in range(4):
                    for t in range(NT):
                        last = pe.transpose(ps[4 + c // 2][:, (c % 2) * S + t * P:(c % 2) * S + (t + 1) * P],
                                            o_tok[:, t, c * P:(c + 1) * P], ident[:, :])
                last.then_inc(sem("oa_psum"), 1)

            @block.scalar
            def _(act):
                for t in range(NT):
                    act.activation(sq6[:, t * S:(t + 1) * S], kvl[:, t, :], ACT.Square,
                                   accum_out=st6[:, t:t + 1]).then_inc(sem("lat_sq"), 1)
                act.wait_ge(sem("lat_ms"), 1)
                act.activation(st6[:, 4:6], st6[:, 2:4], ACT.Sqrt).then_inc(sem("lat_root"), 1)
                act.activation(acc[:, 4096:5120], tmp[:, 0:1024], ACT.Square).then_inc(sem("q_sq"), 1)
                act.wait_ge(sem("q_ms"), 1)
                act.activation(st6[:, 32:48], st6[:, 16:32], ACT.Sqrt).then_inc(sem("q_root"), 1)

                def relu(u):
                    act.wait_ge(sem("idx_dots"), u + 1)
                    if u >= 4:
                        act.wait_ge(sem("idx_added"), u - 3)
                    act.activation(rl[:, u % 4, :], ps[u % 4][:, 0:S], ACT.Relu).then_inc(sem("idx_relu"), 1)
                for u in range(8):
                    relu(u)
                for i in range(4):
                    n, t = i // 2, i % 2
                    act.wait_ge(sem("kv_psum"), i + 1)
                    act.activation((k_tok, vv_tok)[n][:, t, :], (ps[7] if t == 0 else ps[4])[:, :], ACT.Copy).then_inc(
                        sem("kv_out"), 1)
                act.wait_ge(sem("kv_out"), 2)
                act.activation(sq6, side[:, 0:1024], ACT.Square).then_inc(sem("k_sq"), 1)
                act.wait_ge(sem("k_ms"), 1)
                act.activation(st6[:, 64:80], st6[:, 48:64], ACT.Sqrt).then_inc(sem("k_root"), 1)
                for u in range(8, 16):
                    relu(u)
                for u in range(17):
                    if u < 16:
                        act.wait_ge(sem("sa_max"), u + 1)
                        if u >= 2:
                            act.wait_ge(sem("sa_eT_psum"), u - 1)
                        act.activation(ee[:, u % 2, :], lg[:, u % 2, :], ACT.Exp, bias=st6[:, 96 + u:97 + u],
                                       accum_out=st6[:, 112 + u:113 + u]).then_inc(sem("sa_exp"), 1)
                    if u >= 1:
                        act.wait_ge(sem("sa_eT_psum"), u)
                        if u >= 3:
                            act.wait_ge(sem("sa_av"), u - 2)
                        act.activation(eT[:, (u - 1) % 2, :], ps[4 + (u - 1) % 2][:, 0:S], ACT.Copy).then_inc(sem("sa_eT"), 1)

            @block.vector
            def _(v):
                v_step(v.tensor_scalar(qk_cols[:, 1:2], colsB[:, nB:nB + 1], 0.125, None, ALU.mult))
                v.wait_ge(sem("lat_sq"), 2)
                v.tensor_scalar(st6[:, 2:4], st6[:, 0:2], 1.0 / S, EPS, ALU.mult, ALU.add).then_inc(sem("lat_ms"), 1)
                v.wait_ge(sem("lat_root"), 1)
                v_step(v.reciprocal(st6[:, 6:8], st6[:, 4:6]))
                v.tensor_tensor(kvl, kvl, st6[:, 6:8].unsqueeze(2).broadcast_to((P, NT, S)), ALU.mult).then_inc(sem("lat_normed"), 1)

                def head_norm(sq, st, sq_sem, ms_sem, root_sem, a, done):
                    v.wait_ge(sem(sq_sem), 1)
                    v_step(v.tensor_reduce(st6[:, st:st + 16], sq.rearrange("p (g d) -> p g d", d=64), X, ALU.add))
                    v.tensor_scalar(st6[:, st:st + 16], st6[:, st:st + 16], 1.0 / 64, EPS, ALU.mult, ALU.add).then_inc(sem(ms_sem), 1)
                    v.wait_ge(sem(root_sem), 1)
                    v_step(v.reciprocal(st6[:, st:st + 16], st6[:, st + 16:st + 32]))
                    g = a.rearrange("p (g d) -> p g d", d=64)
                    v.tensor_tensor(g, g, st6[:, st:st + 16].unsqueeze(2).broadcast_to((P, 16, 64)), ALU.mult).then_inc(sem(done), 1)
                head_norm(acc[:, 4096:5120], 16, "q_sq", "q_ms", "q_root", tmp[:, 0:1024], "q_normed")
                v.wait_ge(sem("lat_psum"), 1)
                for c in range(2):
                    v.tensor_scalar(latT[:, c, :], ps[4][:, c * S:(c + 1) * S], colB("kv_norm_g_2", c), None, ALU.mult).then_inc(
                        sem("latT_done"), 1)
                v.wait_ge(sem("q_psum"), 1)
                for c in range(4):
                    v.tensor_scalar(qT2[:, c, :], ps[5 + c // 2][:, (c % 2) * S:(c % 2 + 1) * S], qk_cols[:, 1:2], None,
                                    ALU.mult).then_inc(sem("qT_done"), 1)

                def add_head(u):
                    t, h = u // 8, u % 8
                    v.wait_ge(sem("idx_relu"), u + 1)
                    w = w_idx[:, t * 8 + h:t * 8 + h + 1]
                    if h == 0:
                        ins = v.tensor_scalar(work[:, t, :], rl[:, u % 4, :], w, None, ALU.mult)
                    else:
                        ins = v.scalar_tensor_tensor(work[:, t, :], rl[:, u % 4, :], w, work[:, t, :], ALU.mult, ALU.add)
                    ins.then_inc(sem("idx_added"), 1)
                    v.wait_ge(sem("idx_added"), u + 1)
                    if h == 7:
                        v.tensor_copy(st6[:, 200 + t:201 + t], work[:, t, 0:1]).then_inc(sem("idx_score"), 1)
                for u in range(8):
                    add_head(u)
                head_norm(sq6, 48, "k_sq", "k_ms", "k_root", side[:, 0:1024], "k_normed")
                for u in range(8, 16):
                    add_head(u)
                v.wait_ge(sem("k_psum"), 1)
                for c in range(4):
                    v.tensor_scalar(kT2[:, c, :], ps[5 + c // 2][:, (c % 2) * S:(c % 2 + 1) * S], colsB[:, nB + 1:nB + 2], None,
                                    ALU.mult).then_inc(sem("kT_done"), 1)
                for r in range(TOPK // 8):
                    for t in range(NT):
                        if r == 0:
                            v.wait_ge(sem("idx_causal"), t + 1)
                        top = st6[:, 160 + 8 * t:168 + 8 * t]
                        v_step(v.max(top, work[:, t, :]))
                        v_step(v.match_replace(work[:, t, :], top, work[:, t, :], TAKEN))
                v.tensor_scalar(drop, work, TAKEN, 1.0, ALU.is_equal, ALU.subtract).then_inc(sem("drop_raw"), 1)
                v.wait_ge(sem("dst2"), 1)
                v.wait_ge(sem("drop"), 2)

                def first(u):
                    h, t = u // NT, u % NT
                    b = lg[:, u % 2, :]
                    v.wait_ge(sem("sa_scores"), u + 1)
                    v.scalar_tensor_tensor(b, dst2[:, t, :], -2.0 ** -(h + 1), ps[u % 4][:, 0:S], ALU.mult, ALU.add).then_inc(
                        sem("sa_biased"), 1)
                    v.wait_ge(sem("sa_biased"), u + 1)
                    v_step(v.scalar_tensor_tensor(b, drop[:, t, :], 1.0e30, b, ALU.mult, ALU.add))
                    v_step(v.tensor_reduce(st6[:, 208 + u % 2:209 + u % 2], b, X, ALU.max))
                    v.tensor_scalar(st6[:, 96 + u:97 + u], st6[:, 208 + u % 2:209 + u % 2], -1.0, None, ALU.mult).then_inc(
                        sem("sa_max"), 1)

                def last_(u):
                    h, t = u // NT, u % NT
                    v.wait_ge(sem("sa_av"), u + 1)
                    v_step(v.reciprocal(st6[:, 128 + u:129 + u], st6[:, 112 + u:113 + u]))
                    v.tensor_scalar(o_tok[:, t, h * 64:(h + 1) * 64], ps[6 + u % 2][:, 0:64], st6[:, 128 + u:129 + u], None,
                                    ALU.mult).then_inc(sem("sa_o"), 1)
                first(0)
                for u in range(17):
                    if u + 1 < 16:
                        if u >= 1:
                            v.wait_ge(sem("sa_exp"), u)
                        first(u + 1)
                    if u >= 1:
                        last_(u - 1)
                v.wait_ge(sem("oa_psum"), 1)
                for c in range(4):
                    v.tensor_copy(oaT[:, c, :], ps[4 + c // 2][:, (c % 2) * S:(c % 2 + 1) * S])

        if debug and until <= 7:
            debug(nc, sem, locals())
            return

        C = 32
        NC = S // C
        r_, k_, v_ = [mixed[:, 4 * i:4 * i + 4, :] for i in range(3)]
        c5 = 5 * CELL

        def ch4(a):
            return a.rearrange("p (c s) -> p c s", c=4)
        aa, LL, kk, gg = [ring[:, c5 + i * 1024:c5 + (i + 1) * 1024] for i in range(4)]
        eP, ePrev, eN, bonus, t1, t2_ = [acc[:, i * 1024:(i + 1) * 1024] for i in range(6)]
        tl = tmp[:, :].rearrange("p (w c s) -> p w c s", w=4, c=4)
        rT_, aT_, kT_, bT_ = [tmp[:, i * 1024:(i + 1) * 1024] for i in range(4)]
        toks = side[:, 0:4096].rearrange("p (w t d) -> p w t d", w=4, t=NT)
        v_tk, k_tk, b_tk, a_tk = [toks[:, i, :, :] for i in range(4)]
        tw = side[:, 4096:4352]
        sgl = side[:, 4352:4864].rearrange("p (c s) -> p c s", c=2)
        omka = small[:, 56:60]
        wC = colsB[:, NB_ALL:NB_ALL + 32].rearrange("p (c n) -> p c n", c=4)
        assert NB_ALL + 32 <= P
        EXPM = math.exp(-0.5)

        with nc.Block() as block:
            @block.gpsimd
            def _(pool):
                p_step(pool.memset(t1, 1.0))
                pool.memset(t1.rearrange("p (n c) -> p n c", c=C)[:, :, 0:1], 0.0).then_inc(sem("scan_mask"), 1)

            @block.tensor
            def _(pe):
                pe.wait_ge(sem("tanh"), 1)
                for c in range(4):
                    last = pe.matmul(ps[c // 2][:, (c % 2) * S:(c % 2 + 1) * S], lora[0:64, c * P:(c + 1) * P], tw[0:64, :],
                                     start=True, stop=True)
                last.then_inc(sem("w_psum"), 1)
                for c in range(4):
                    last = pe.matmul(ps[2 + c // 2][:, (c % 2) * S:(c % 2 + 1) * S], lora[64:128, c * P:(c + 1) * P],
                                     mixed[64:128, 12, :], start=True, stop=True)
                last.then_inc(sem("a_psum"), 1)
                pe.wait_ge(sem("sgl"), 1)
                for c in range(4):
                    for k in range(2):
                        last = pe.matmul(ps[4 + c // 2][:, (c % 2) * S:(c % 2 + 1) * S],
                                         lora[:, 512 * (k + 1) + c * P:512 * (k + 1) + (c + 1) * P], sgl[:, k, :],
                                         start=(k == 0), stop=(k == 1))
                last.then_inc(sem("gate_psum"), 1)
                pe.wait_ge(sem("kk_sq"), 1)
                for n in range(2):
                    last = pe.matmul(ps[6 + n][:, :], headones[:, :], t2_[:, n * 512:(n + 1) * 512], start=True, stop=True)
                last.then_inc(sem("kk_psum"), 1)
                pe.wait_ge(sem("wa_out"), 8)

                def turn(w, src, banks, name):
                    for c in range(4):
                        for t in range(NT):
                            last = pe.transpose(ps[banks + t][:, c * P:(c + 1) * P], ch4(src)[:, c, t * P:(t + 1) * P], ident[:, :])
                    last.then_inc(sem("tok_psum"), 1)
                turn(0, ring[:, 4 * CELL + 2048:4 * CELL + 3072], 0, "v")
                p2_ready(pe, GATE0)
                for m in range(4):
                    for t in range(NT):
                        for c in range(KC):
                            last = pe.matmul(ps[2 + m // 2][:, (m % 2) * S + t * P:(m % 2) * S + (t + 1) * P],
                                             p2(GATE0)[:, c, m * P:(m + 1) * P], hT[:, c, t * P:(t + 1) * P],
                                             start=(c == 0), stop=(c == KC - 1))
                    if m % 2:
                        last.then_inc(sem("side_gate"), 1)
                pe.wait_ge(sem("rk_done"), 1)
                pe.wait_ge(sem("kk_root"), 1)
                for n in range(2):
                    last = pe.matmul(ps[6 + n][:, :], headones[:, :], t2_[:, n * 512:(n + 1) * 512], start=True, stop=True)
                last.then_inc(sem("bonus_psum"), 1)
                pe.wait_ge(sem("tilde"), 1)
                pe.wait_ge(sem("side_gate_out"), 2)
                turn(1, kT_, 2, "k")
                pe.wait_ge(sem("tilde"), 2)
                pe.wait_ge(sem("gate_out"), 1)
                turn(2, bT_, 4, "b")
                pe.wait_ge(sem("tilde"), 3)
                pe.wait_ge(sem("tok_out"), 1)
                turn(3, aT_, 0, "a")

            @block.scalar
            def _(act):
                act.activation(tw[0:64, :], mixed[0:64, 12, :], ACT.Tanh).then_inc(sem("tanh"), 1)
                act.activation(sgl, mixed[:, 13:15, :], ACT.Sigmoid).then_inc(sem("sgl"), 1)
                act.wait_ge(sem("w_psum"), 1)
                for c in range(4):
                    act.activation(ch4(ePrev)[:, c, :], ps[c // 2][:, (c % 2) * S:(c % 2 + 1) * S], ACT.Sigmoid,
                                   bias=colB("rwkv_w0_2", c)).then_inc(sem("wa_out"), 1)
                act.wait_ge(sem("a_psum"), 1)
                for c in range(4):
                    act.activation(ch4(aa)[:, c, :], ps[2 + c // 2][:, (c % 2) * S:(c % 2 + 1) * S], ACT.Sigmoid,
                                   bias=colB("rwkv_a0_2", c)).then_inc(sem("wa_out"), 1)
                act.wait_ge(sem("gate_psum"), 1)
                for n in range(2):
                    last = act.activation(gg[:, n * 512:(n + 1) * 512], ps[4 + n][:, :], ACT.Copy)
                last.then_inc(sem("gate_out"), 1)
                act.wait_ge(sem("kk_psum"), 1)
                for n in range(2):
                    last = act.activation(bonus[:, n * 512:(n + 1) * 512], ps[6 + n][:, :], ACT.Sqrt)
                last.then_inc(sem("kk_root"), 1)
                act.wait_ge(sem("tok_psum"), 1)

                def tok(w, banks):
                    act.wait_ge(sem("tok_psum"), w + 1)
                    for t in range(NT):
                        last = act.activation(toks[:, w, t, :], ps[banks + t][:, :], ACT.Copy)
                    last.then_inc(sem("tok_out"), 1)
                tok(0, 0)
                act.wait_ge(sem("logdecay"), 1)
                act.activation(eP, LL, ACT.Exp).then_inc(sem("eP"), 1)
                act.activation(eN, LL, ACT.Exp, scale=-1.0).then_inc(sem("eN"), 1)
                act.wait_ge(sem("logprev"), 1)
                act.activation(ePrev, ePrev, ACT.Exp).then_inc(sem("ePrev"), 1)
                for n in range(2):
                    act.wait_ge(sem("side_gate"), n + 1)
                    act.activation(gates_sb[:, 0, 2 * n:2 * n + 2, :, :], ps[2 + n][:, :].rearrange("p (k t n) -> p k t n", k=2, t=NT),
                                   ACT.Sigmoid).then_inc(sem("side_gate_out"), 1)
                tok(1, 2)
                tok(2, 4)
                tok(3, 0)

            @block.vector
            def _(v):
                v_step(v.tensor_scalar(omka, colB("rwkv_k_a_2", 0, 4), -1.0, 1.0, ALU.mult, ALU.add))
                for c in range(4):
                    ins = v.tensor_scalar(ch4(kk)[:, c, :], k_[:, c, :], colB("rwkv_k_k_2", c), None, ALU.mult)
                v_step(ins)
                v.tensor_tensor(t2_, kk, kk, ALU.mult).then_inc(sem("kk_sq"), 1)
                v.wait_ge(sem("wa_out"), 4)
                v_step(v.tensor_scalar(ePrev, ePrev, -EXPM, None, ALU.mult))
                v.wait_ge(sem("scan_mask"), 1)
                v.tensor_tensor_scan(LL, t1, ePrev, 0.0, ALU.mult, ALU.add).then_inc(sem("logdecay"), 1)
                v.wait_ge(sem("logdecay"), 1)
                v.tensor_tensor(ePrev, LL, ePrev, ALU.subtract).then_inc(sem("logprev"), 1)
                v.wait_ge(sem("wa_out"), 8)
                for c in range(4):
                    ins = v.tensor_scalar(ch4(t1)[:, c, :], ch4(aa)[:, c, :], colB("rwkv_k_a_2", c), omka[:, c:c + 1],
                                          ALU.mult, ALU.add)
                v_step(ins)
                v_step(v.tensor_tensor(k_, k_, ch4(t1), ALU.mult))
                v.wait_ge(sem("kk_root"), 1)
                v_step(v.tensor_scalar(bonus, bonus, 1e-12, None, ALU.max))
                v_step(v.reciprocal(bonus, bonus))
                v_step(v.tensor_tensor(kk, kk, bonus, ALU.mult))
                for c in range(4):
                    ins = v.scalar_tensor_tensor(ch4(t2_)[:, c, :], k_[:, c, :], colB("rwkv_r_k_2", c), r_[:, c, :],
                                                 ALU.mult, ALU.mult)
                ins.then_inc(sem("rk_done"), 1)
                v.wait_ge(sem("eN"), 1)
                v.tensor_tensor(ch4(kT_), k_, ch4(eN), ALU.mult).then_inc(sem("tilde"), 1)
                v_step(v.tensor_tensor(t1, kk, aa, ALU.mult))
                v.tensor_tensor(bT_, t1, eN, ALU.mult).then_inc(sem("tilde"), 1)
                v.wait_ge(sem("ePrev"), 1)
                v.scalar_tensor_tensor(aT_, kk, -1.0, ePrev, ALU.mult, ALU.mult).then_inc(sem("tilde"), 1)
                v.wait_ge(sem("eP"), 1)
                v_step(v.tensor_tensor(ch4(rT_), r_, ch4(eP), ALU.mult))
                v_step(v.tensor_copy(wC, ch4(eP).rearrange("p c (n i) -> p c n i", i=C)[:, :, :, C - 1]))
                v.wait_ge(sem("bonus_psum"), 1)
                for n in range(2):
                    v_step(v.tensor_tensor(bonus[:, n * 512:(n + 1) * 512].rearrange("p (c s) -> p c s", c=2),
                                           ps[6 + n][:, :].rearrange("p (c s) -> p c s", c=2), v_[:, 2 * n:2 * n + 2, :], ALU.mult))

        if debug and until <= 7.1:
            debug(nc, sem, locals())
            return

        rbT = ring[:, 4 * CELL:4 * CELL + 2048].rearrange("p (u n) -> p u n", u=16)
        HT = ring[:, 4 * CELL + 2048:4 * CELL + 3072].rearrange("p (u n) -> p u n", u=8)
        Gs = acc[:, 0:1024].rearrange("p (t h d) -> p t h d", t=NT, h=8)
        Yv = acc[:, 1024:2048].rearrange("p (t h d) -> p t h d", t=NT, h=8)
        y_tok = acc[:, 2048:3072].rearrange("p (t h d) -> p t h d", t=NT, h=8)
        MT = side[:, 4096:6144].rearrange("p (q c d) -> p q c d", q=4, c=NC)
        NN = ring[:, c5:c5 + 2048].rearrange("p (q c d) -> p q c d", q=4, c=NC)
        SS = xn_sb[:, :].rearrange("p (q c d) -> p q c d", q=4, c=NC)
        W2 = [acc[:, 4096 + i * 1024:4096 + (i + 1) * 1024] for i in range(2)]
        exp_v = [side[:, 6144 + i * 512:6144 + (i + 1) * 512] for i in range(2)]
        exp_g = [ring[:, c5 + 2048 + i * 256:c5 + 2048 + (i + 1) * 256] for i in range(2)]
        AKT = [ring[:, c5 + 2560 + i * 128:c5 + 2560 + (i + 1) * 128] for i in range(2)]
        RKT = [ring[:, c5 + 2816 + i * 128:c5 + 2816 + (i + 1) * 128] for i in range(2)]

        branch_w = [cell(i, 4, 1024) for i in range(2)]
        QA, QTA, QB, QTB, PTA, PTB, OTM, UH = range(8)

        with nc.Block() as block:
            def mat(b, i, n=1):
                return W2[b][:, i * P:(i + n) * P]

            def inst(u):
                h, t = 2 * (u // 4) + u % 2, u // 2 % NT
                jo = (h % 2) * 64
                return h, t, slice(jo, jo + 64), h // 2, u % 2

            @block.sync
            def _(sp):
                load_gates(sp, 3)
                for i, name in enumerate(("w_branch_attn_2", "w_branch_rwkv_2")):
                    sp.wait_ge(sem("side_gate"), 2 + 8 * (i + 1))
                    sp.dma_start(branch_w[i], inp[name][0].rearrange("(c p) n -> p c n", p=P)).then_inc(
                        sem(f"branch_loaded{i}"), 16)

            GATE_AFTER = (0, 10, 11)

            def gate_bank(i):
                return ps[(3, 3, 7)[i % 3]][:, P:2 * P]

            @block.gpsimd
            def _(pool):
                cm = chunk_of.unsqueeze(2).broadcast_to((P, 4, 64))
                for u in range(16):
                    h, t, js, q, b = inst(u)
                    if u >= 2:
                        pool.wait_ge(sem("i_maps"), u - 1)
                    for i, src in enumerate((b_tk, v_tk)):
                        p_step(pool.tensor_tensor(exp_v[b][:, i * S:(i + 1) * S].rearrange("p (c d) -> p c d", c=4),
                                                  src[:, t, h * 64:(h + 1) * 64].unsqueeze(1).broadcast_to((P, 4, 64)), cm, ALU.mult))
                    pool.memset(small[:, 60:61], 0.0).then_inc(sem("i_spread"), 1)
                    pool.wait_ge(sem("i_spread"), u + 1)

            @block.tensor
            def _(pe):
                def start_(u):
                    if u >= 2:
                        pe.wait_ge(sem("i_end"), u)
                    for i in range(3):
                        for w in (u, u + 1):
                            h, t, js, q, b = inst(w)
                            T = slice(t * P, (t + 1) * P)
                            left = (bT_, kT_, aT_)[i]
                            last = pe.matmul(ps[4 * b + i][:, 0:(S, S, P)[i]], ch4(left)[js, q, T],
                                             tl[js, 0:2, q, T] if i < 2 else ch4(bT_)[js, q, T], start=True, stop=True)
                            if i == 2:
                                last.then_inc(sem("i_prod"), 1)

                def maps(u):
                    pe.wait_ge(sem("i_gh"), u + 2)
                    pe.wait_ge(sem("i_spread"), u + 2)
                    for i in range(3):
                        for w in (u, u + 1):
                            h, t, js, q, b = inst(w)
                            hs = slice(h * 64, (h + 1) * 64)
                            left = (mat(b, UH)[:, 64:P], b_tk[:, t, hs], k_tk[:, t, hs])[i]
                            right = (exp_v[b][:, 0:S], exp_g[b], exp_v[b][:, S:2 * S])[i]
                            last = pe.matmul(ps[4 * b + 2][js, min(i, 1) * S:(min(i, 1) + 1) * S], left, right,
                                             start=(i < 2), stop=(i != 1))
                            if i == 2:
                                last.then_inc(sem("i_maps"), 1)

                def steps(u):
                    h, t, js, q, b = inst(u)
                    B = 4 * b
                    hs = slice(h * 64, (h + 1) * 64)
                    def level(n, Q, QT, last_level):
                        def f():
                            pe.wait_ge(sem(f"i_q{b}"), 4 * (u // 2) + n)
                            if n == 1:
                                pe.wait_ge(sem(f"i_pt{b}"), 5 * (u // 2) + 1)
                            last = pe.matmul(ps[B][:, 0:P], mat(b, QT), mat(b, Q), start=True, stop=True)
                            if not last_level:
                                last = pe.matmul(ps[B][:, P:S], mat(b, Q), mat(b, QT), start=True, stop=True)
                            last.then_inc(sem(f"i_sq{b}"), 1)
                        return f

                    def grow(n, Q, PT):
                        def f():
                            pe.wait_ge(sem(f"i_q{b}"), 4 * (u // 2) + n)
                            pe.wait_ge(sem(f"i_pt{b}"), 5 * (u // 2) + n - 1)
                            pe.matmul(ps[B + 1][:, 0:P], mat(b, Q), mat(b, PT), start=True, stop=True).then_inc(sem(f"i_gr{b}"), 1)
                        return f

                    def off1():
                        pe.wait_ge(sem(f"i_pt{b}"), 5 * (u // 2) + 4)
                        pe.transpose(ps[B + 2][:, 0:P], mat(b, PTB), ident[:, :]).then_inc(sem(f"i_pd{b}"), 1)

                    def off2():
                        pe.wait_ge(sem(f"i_off{b}"), 2 * (u // 2) + 1)
                        pe.matmul(ps[B + 2][:, P:S], mat(b, OTM), mat(b, QA), start=True, stop=True).then_inc(sem(f"i_xt{b}"), 1)
                        pe.wait_ge(sem("side_gate_out"), 2 + 3 * (u // 2) + (1, 0)[b])
                        pe.matmul(ps[B + 3][:, 0:64], AKT[b], v_tk[:, t, hs], start=True, stop=True)
                        pe.matmul(ps[B + 3][:, 64:128], RKT[b], v_tk[:, t, hs], start=True, stop=True).then_inc(sem(f"i_u{b}"), 1)

                    def off3():
                        pe.wait_ge(sem(f"i_off{b}"), 2 * (u // 2) + 2)
                        pe.matmul(ps[B + 1][:, 0:P], mat(b, QB), mat(b, PTB), start=True, stop=True).then_inc(sem(f"i_gr{b}"), 1)

                    def solve():
                        pe.wait_ge(sem(f"i_pt{b}"), 5 * (u // 2) + 5)
                        pe.wait_ge(sem(f"i_ud{b}"), u // 2 + 1)
                        pe.matmul(ps[B][:, 0:64], mat(b, PTA), mat(b, UH)[:, 0:64], start=True, stop=True)
                        pe.matmul(ps[B][:, 64:P], mat(b, PTA), a_tk[:, t, hs], start=True, stop=True)
                        pe.matmul(ps[B + 1][js, 0:P], a_tk[:, t, hs], mat(b, PTA), start=True, stop=True).then_inc(sem("i_sol"), 1)

                    return [lambda: None if u % 2 else start_(u), level(1, QA, QTA, False), level(2, QB, QTB, False),
                            grow(2, QB, PTA), level(3, QA, QTA, True), grow(3, QA, PTB), grow(4, QB, PTA), off1, off2, off3,
                            solve, lambda: maps(u - 1) if u % 2 else None]
                def gate_product(i):
                    m, t = 4 + i // NT, i % NT
                    if i % 8 == 0:
                        p2_ready(pe, GATE0 + m // 4)
                    if i % 3 == 0 and i:
                        pe.wait_ge(sem("side_gate_out"), 2 + i - 1)
                    if i % 3 == 2:
                        pe.wait_ge(sem("i_ud1"), i // 3 + 1)
                    for c in range(KC):
                        last = pe.matmul(gate_bank(i), p2(GATE0 + m // 4)[:, c, (m % 4) * P:(m % 4 + 1) * P],
                                         hT[:, c, t * P:(t + 1) * P], start=(c == 0), stop=(c == KC - 1))
                    last.then_inc(sem("side_gate"), 1)

                for pair in range(8):
                    for k, (fa, fb) in enumerate(zip(steps(2 * pair), steps(2 * pair + 1))):
                        fa()
                        fb()
                        if k in GATE_AFTER:
                            gate_product(3 * pair + GATE_AFTER.index(k))

            @block.scalar
            def _(act):
                def steps(u):
                    h, t, js, q, b = inst(u)
                    B = 4 * b

                    def sq(n, dst):
                        def f():
                            act.wait_ge(sem(f"i_sq{b}"), 3 * (u // 2) + n)
                            k = 2 if n < 3 else 1
                            act.activation(mat(b, dst, k), ps[B][:, 0:k * P], ACT.Copy).then_inc(sem(f"i_q{b}"), 1)
                        return f

                    def uh():
                        act.wait_ge(sem(f"i_u{b}"), u // 2 + 1)
                        act.activation(mat(b, UH)[:, 0:64], ps[B + 3][:, 0:64], ACT.Copy)
                        act.activation(Yv[:, t, h, :], ps[B + 3][:, 64:P], ACT.Copy).then_inc(sem(f"i_ud{b}"), 1)

                    def sol():
                        act.wait_ge(sem("i_sol"), u + 1)
                        act.activation(HT[js, 2 * q + t, :], ps[B + 1][js, 0:P], ACT.Copy)

                    def nmap():
                        act.wait_ge(sem("i_maps"), u + 1)
                        act.wait_ge(sem("i_mdone"), u + 1)
                        act.activation(NN[js, q, 4 * t:4 * t + 4, :], ps[B + 2][js, S:2 * S].rearrange("p (c d) -> p c d", c=4),
                                       ACT.Copy).then_inc(sem("i_end"), 1)
                    return [sq(1, QB), sq(2, QA), sq(3, QB), uh, sol, nmap]

                def gate_sigmoid(i):
                    m, t = 4 + i // NT, i % NT
                    act.wait_ge(sem("side_gate"), 2 + i + 1)
                    act.activation(gates_sb[:, m // 4, m % 4, t, :], gate_bank(i), ACT.Sigmoid).then_inc(sem("side_gate_out"), 1)

                for pair in range(8):
                    for k, (fa, fb) in enumerate(zip(steps(2 * pair), steps(2 * pair + 1))):
                        if k in (0, 5):
                            gate_sigmoid(3 * pair + k // 5)
                        fa()
                        fb()
                    gate_sigmoid(3 * pair + 2)

            @block.vector
            def _(v):
                v_step(v.memset(SS[:, :, 0, :], 0.0))

                def steps(u):
                    h, t, js, q, b = inst(u)
                    B = 4 * b

                    def first():
                        v.wait_ge(sem("i_prod"), u + 1)
                        v.tensor_tensor(mat(b, QTA), ps[B][:, P:S], M_16, ALU.mult)
                        v_step(v.tensor_tensor(mat(b, QA), ps[B + 2][:, 0:P], M_16L, ALU.mult))
                        v.tensor_tensor(mat(b, PTA), mat(b, QTA), ident[:, :], ALU.add).then_inc(sem(f"i_q{b}"), 1)
                        v.wait_ge(sem(f"i_q{b}"), 4 * (u // 2) + 1)
                        v.tensor_tensor(rbT[:, 2 * h + t, :], ps[B][:, 0:P], M_INCL, ALU.mult)
                        v.tensor_tensor(mat(b, OTM), ps[B][:, P:S], M_OFF, ALU.mult)
                        v.tensor_tensor(RKT[b], ps[B + 1][:, 0:P], M_INCL, ALU.mult)
                        v.tensor_tensor(AKT[b], ps[B + 1][:, P:S], M_STRICT, ALU.mult).then_inc(sem(f"i_pt{b}"), 1)

                    def grown(n, src, dst):
                        def f():
                            v.wait_ge(sem(f"i_gr{b}"), 4 * (u // 2) + n)
                            v.tensor_tensor(mat(b, dst), ps[B + 1][:, 0:P], mat(b, src), ALU.add).then_inc(sem(f"i_pt{b}"), 1)
                            v.wait_ge(sem(f"i_pt{b}"), 5 * (u // 2) + n + 1)
                        return f

                    def pd():
                        v.wait_ge(sem(f"i_pd{b}"), u // 2 + 1)
                        v.tensor_copy(mat(b, QA), ps[B + 2][:, 0:P]).then_inc(sem(f"i_off{b}"), 1)

                    def xt():
                        v.wait_ge(sem(f"i_xt{b}"), u // 2 + 1)
                        v.tensor_copy(mat(b, QB), ps[B + 2][:, P:S]).then_inc(sem(f"i_off{b}"), 1)

                    def sol():
                        v.wait_ge(sem("i_sol"), u + 1)
                        v_step(v.tensor_copy(Gs[:, t, h, :], ps[B][:, 0:64]))
                        v.tensor_copy(mat(b, UH)[:, 64:P], ps[B][:, 64:P])
                        v.tensor_tensor(exp_g[b].rearrange("p (c d) -> p c d", c=4),
                                        Gs[:, t, h, :].unsqueeze(1).broadcast_to((P, 4, 64)),
                                        chunk_of.unsqueeze(2).broadcast_to((P, 4, 64)), ALU.mult).then_inc(sem("i_gh"), 1)

                    def maps():
                        v.wait_ge(sem("i_maps"), u + 1)
                        v.tensor_tensor(MT[js, q, 4 * t:4 * t + 4, :], ps[B + 2][js, 0:S].rearrange("p (c d) -> p c d", c=4),
                                        ident[js, js].unsqueeze(1).broadcast_to((64, 4, 64)), ALU.add).then_inc(sem("i_mdone"), 1)
                    return [first, grown(1, PTA, PTB), grown(2, PTB, PTA), grown(3, PTA, PTB), pd, xt, grown(4, PTB, PTA), sol, maps]
                for pair in range(8):
                    for fa, fb in zip(steps(2 * pair), steps(2 * pair + 1)):
                        fa()
                        fb()

        if debug and until <= 7.2:
            debug(nc, sem, locals())
            return

        sa_sb = [acc[:, 4096 + t * 512:4096 + (t + 1) * 512].rearrange("p (h d) -> p h d", h=8) for t in range(NT)]
        sq7 = acc[:, 5120:6144]
        st7 = small[:, 24:40]
        orT = ch4(side[:, 0:1024])
        out_w = [cell(2), cell(4)]

        with nc.Block() as block:
            @block.sync
            def _(sp):
                sp.dma_start(out_w[0], w_cols(inp["w_out_2"][0], 0, 512)).then_inc(sem("out_loaded0"), 16)

            @block.tensor
            def _(pe):
                def attn_branch(m):
                    if m == 0:
                        pe.wait_ge(sem("branch_loaded0"), 16)
                    if m >= 2:
                        pe.wait_ge(sem("gated"), m - 1)
                    for c in range(4):
                        last = pe.matmul(ps[5 + m % 2][:, 0:S], branch_w[0][:, c, m * P:(m + 1) * P], oaT[:, c, :],
                                         start=(c == 0), stop=(c == 3))
                    last.then_inc(sem("attn_branch"), 1)

                for c in range(NC - 1):
                    if c:
                        attn_branch(c - 1)
                        pe.wait_ge(sem("state"), 2 * c)
                    for q in range(4):
                        for par in range(2):
                            js = slice(par * 64, par * 64 + 64)
                            last = pe.matmul(ps[par][js, q * 64:(q + 1) * 64], MT[js, q, c, :], SS[js, q, c, :], start=True, stop=True)
                            if q == 3:
                                last.then_inc(sem("state_psum"), 1)
                attn_branch(NC - 2)
                attn_branch(NC - 1)
                pe.wait_ge(sem("state"), 2 * (NC - 1))
                for t in range(NT):
                    if t:
                        pe.wait_ge(sem("sa_done"), 2)
                        pe.wait_ge(sem("y_out"), 1)
                    for par in range(2):
                        js = slice(par * 64, par * 64 + 64)
                        for q in range(4):
                            for c in range(4):
                                last = pe.matmul(ps[par][c * C:(c + 1) * C, q * 64:(q + 1) * 64], HT[js, 2 * q + t, c * C:(c + 1) * C],
                                                 SS[js, q, 4 * t + c, :], start=True, stop=True)
                    last.then_inc(sem("sa_psum"), 1)
                    for par in range(2):
                        js = slice(par * 64, par * 64 + 64)
                        for q in range(4):
                            for c in range(4):
                                o = t * P + c * C
                                last = pe.matmul(ps[2 + par][c * C:(c + 1) * C, q * 64:(q + 1) * 64], ch4(rT_)[js, q, o:o + C],
                                                 SS[js, q, 4 * t + c, :], start=True, stop=True)
                    pe.wait_ge(sem("sa_done"), 2 * t + 2)
                    for h in range(8):
                        last = pe.matmul(ps[4][:, h * 64:(h + 1) * 64], rbT[:, 2 * h + t, :], sa_sb[t][:, h, :], start=True, stop=True)
                    last.then_inc(sem("y_psum"), 1)
                pe.wait_ge(sem("y_normed"), 1)
                pe.wait_ge(sem("gated"), 8)
                yf = acc[:, 2048:3072].rearrange("p (t d) -> p t d", t=NT)
                for c in range(4):
                    for t in range(NT):
                        last = pe.transpose(ps[6 + c // 2][:, (c % 2) * S + t * P:(c % 2) * S + (t + 1) * P],
                                            yf[:, t, c * P:(c + 1) * P], ident[:, :])
                last.then_inc(sem("yT_psum"), 1)

            @block.scalar
            def _(act):
                act.wait_ge(sem("y_centred"), 1)
                act.activation(sq7, acc[:, 2048:3072], ACT.Square).then_inc(sem("y_sq"), 1)
                act.wait_ge(sem("y_var"), 1)
                act.activation(st7, st7, ACT.Sqrt).then_inc(sem("y_root"), 1)

            @block.vector
            def _(v):
                def gate_attn(m):
                    v.wait_ge(sem("attn_branch"), m + 1)
                    g = gates_sb[:, m // 4, m % 4, :, :]
                    v.tensor_tensor(g, ps[5 + m % 2][:, 0:S].rearrange("p (t n) -> p t n", t=NT), g, ALU.mult).then_inc(
                        sem("gated"), 1)

                for c in range(NC - 1):
                    for par in range(2):
                        js = slice(par * 64, par * 64 + 64)
                        v.wait_ge(sem("state_psum"), 2 * c + par + 1)
                        s_ = SS[js, :, c + 1, :]
                        v_step(v.tensor_tensor(s_, ps[par][js, 0:S].rearrange("p (q d) -> p q d", q=4), NN[js, :, c, :], ALU.add))
                        v.tensor_tensor(s_, s_, wC[js, :, c].unsqueeze(2).broadcast_to((64, 4, 64)), ALU.mult).then_inc(sem("state"), 1)
                    if c:
                        gate_attn(c - 1)
                gate_attn(NC - 2)
                gate_attn(NC - 1)
                for t in range(NT):
                    v.wait_ge(sem("sa_psum"), t + 1)
                    gq = Gs[:, t, :, :].rearrange("p (q r) d -> p r q d", r=2)
                    sq_ = sa_sb[t].rearrange("p (q r) d -> p r q d", r=2)
                    for par in range(2):
                        v.tensor_tensor(sq_[:, par, :, :], ps[par][:, 0:S].rearrange("p (q d) -> p q d", q=4), gq[:, par, :, :],
                                        ALU.add).then_inc(sem("sa_done"), 1)
                    v.wait_ge(sem("y_psum"), t + 1)
                    v_step(v.tensor_tensor(y_tok[:, t, :, :], ps[4][:, :].rearrange("p (h d) -> p h d", h=8), Yv[:, t, :, :], ALU.add))
                    yq = y_tok[:, t, :, :].rearrange("p (q r) d -> p r q d", r=2)
                    for par in range(2):
                        ins = v.tensor_tensor(yq[:, par, :, :], ps[2 + par][:, 0:S].rearrange("p (q d) -> p q d", q=4),
                                              yq[:, par, :, :], ALU.add)
                    ins.then_inc(sem("y_out"), 1)
                v.wait_ge(sem("y_out"), 2)
                yg = acc[:, 2048:3072].rearrange("p (g d) -> p g d", d=64)
                v_step(v.tensor_reduce(st7, yg, X, ALU.add))
                v_step(v.tensor_scalar(st7, st7, -1.0 / 64, None, ALU.mult))
                v.tensor_tensor(yg, yg, st7.unsqueeze(2).broadcast_to((P, 16, 64)), ALU.add).then_inc(sem("y_centred"), 1)
                v.wait_ge(sem("y_sq"), 1)
                v_step(v.tensor_reduce(st7, sq7.rearrange("p (g d) -> p g d", d=64), X, ALU.add))
                v.tensor_scalar(st7, st7, 1.0 / 64, 64e-5, ALU.mult, ALU.add).then_inc(sem("y_var"), 1)
                v.wait_ge(sem("y_root"), 1)
                v_step(v.reciprocal(st7, st7))
                v.tensor_tensor(yg, yg, st7.unsqueeze(2).broadcast_to((P, 16, 64)), ALU.mult).then_inc(sem("y_normed"), 1)
                v.wait_ge(sem("yT_psum"), 1)
                for c in range(4):
                    ins = v.tensor_scalar(orT[:, c, :], ps[6 + c // 2][:, (c % 2) * S:(c % 2 + 1) * S], colB("rwkv_ln_w_2", c),
                                          colB("rwkv_ln_b_2", c), ALU.mult, ALU.add)
                v_step(ins)
                v_step(v.tensor_tensor(side[:, 0:1024], side[:, 0:1024], bonus, ALU.add))
                v_step(v.tensor_tensor(side[:, 0:1024], side[:, 0:1024], gg, ALU.mult))

        if debug and until <= 7.5:
            debug(nc, sem, locals())
            return

        give_back()
        mrg = acc[:, 2048:4096].rearrange("p (c s) -> p c s", c=8)
        mrg_half = acc[:, 0:2048].rearrange("p (c s) -> p c s", c=8)

        with nc.Block() as block:
            @block.sync
            def _(sp):
                sp.dma_start(out_w[1], w_cols(inp["w_out_2"][0], 512, 1024)).then_inc(sem("out_loaded1"), 16)
                load_router(sp, 1, inp["router_group_w_2"][0], inp["router_expert_w_2"][0], None, inp["router_expert_bias_2"])
                load_expert(sp, 1, (5,))
                sp.wait_ge(sem("branch_out"), 8)
                load_expert(sp, 1, (0, 3, 1))
                sp.wait_ge(sem("y3"), 4)
                load_expert(sp, 1, (4, 2))

            @block.tensor
            def _(pe):
                pe.wait_ge(sem("branch_loaded1"), 16)
                for m in range(8):
                    if m >= 4:
                        pe.wait_ge(sem("branch_out"), m - 3)
                    for c in range(4):
                        last = pe.matmul(ps[4 + m % 4][:, 0:S], branch_w[1][:, c, m * P:(m + 1) * P],
                                         orT[:, c, :], start=(c == 0), stop=(c == 3))
                    last.then_inc(sem("branch"), 1)
                pe.wait_ge(sem("branch_out"), 8)
                for g in range(4):
                    t, n = g // 2, g % 2
                    if t == 0:
                        pe.wait_ge(sem(f"out_loaded{n}"), 16)
                    for c in range(KC):
                        last = pe.matmul(ps[g][:, :], mrg[:, c, t * P:(t + 1) * P], out_w[n][:, c, :],
                                         start=(c == 0), stop=(c == KC - 1))
                    last.then_inc(sem("y3"), 1)
                hT_tensor(pe, 3)

            @block.scalar
            def _(act):
                rms_scalar(act, 4, xn_sb)

            @block.vector
            def _(v):
                for m in range(8):
                    v.wait_ge(sem("branch"), m + 1)
                    y, h_, g_ = [a.rearrange("p (t n) -> p t n", t=NT) for a in
                                 (ps[4 + m % 4][:, 0:S], mrg_half[:, m, :], mrg[:, m, :])]
                    v_step(v.tensor_tensor(h_, y, gates_sb[:, 2 + m // 4, m % 4, :, :], ALU.mult))
                    v.tensor_tensor(g_, h_, gates_sb[:, m // 4, m % 4, :, :], ALU.add).then_inc(sem("branch_out"), 1)
                residual(v, 0, None, 0, "y3")
                rms_vector(v, 4, xn3)
                hT_vector(v, 3)

        if debug and until <= 8:
            debug(nc, sem, locals())
            return
        route(1, 32, False)
        experts(1, 32)

        with nc.Block() as block:
            @block.sync
            def _(sp):
                sp.dma_start(out[0].rearrange("(t p) d -> p t d", p=P), x3).then_inc(sem("stored"), 16)
                sp.wait_ge(sem("stored"), 16)
        if debug:
            debug(nc, sem, locals())


OUT_SHAPE = (1, S, D)


def kernel(**inputs):
    import concourse.bacc as bacc
    from concourse.bass_utils import run_bass_kernel_spmd

    nc = bacc.Bacc("TRN2", target_bir_lowering=False, num_devices=1)
    arrays, inp = {}, {}
    for name, value in inputs.items():
        a = np.ascontiguousarray(value)
        if a.size == 0:
            continue
        arrays["in_" + name] = a
        inp[name] = nc.dram_tensor("in_" + name, a.shape, mybir.dt.from_np(a.dtype), kind="ExternalInput").ap()
    out = nc.dram_tensor("out_x", OUT_SHAPE, F32, kind="ExternalOutput").ap()
    build(nc, inp, out)
    r = run_bass_kernel_spmd(nc, [arrays], core_ids=[0])
    return r.results[0]["out_x"]
```

```python
import math
from contextlib import ExitStack

import numpy as np

import concourse.bass as bass
from concourse import mybir

F32 = mybir.dt.float32
I32 = mybir.dt.int32
ALU = mybir.AluOpType
ACT = mybir.ActivationFunctionType
X = mybir.AxisListType.X

P = 128
S = 256
D = 1024
NT = S // P
KC = D // P
EPS = 1e-6
CELL = 4096
SLOTS = 64
ROUNDS = S // SLOTS
FE = 512
FC = FE // P
BIG = 3.0e38

ROWS_A = [("norm_mix", 8), ("norm_ffn", 8), ("mix_norm_g_2", 8), ("moe_norm_g_2", 8),
          ("ada_b", 48)]
ROWS_B = [("ada_b_2", 48), ("rwkv_w0_2", 4), ("rwkv_a0_2", 4), ("rwkv_k_k_2", 4), ("rwkv_k_a_2", 4),
          ("rwkv_r_k_2", 4), ("rwkv_ln_w_2", 4), ("rwkv_ln_b_2", 4), ("kv_norm_g_2", 2), ("attn_subln", 1)]


def row_starts(rows):
    at, out = 0, {}
    for name, n in rows:
        out[name] = at
        at += n
    return out, at


def build(nc, inp, out):
    ctx = ExitStack()
    with ctx:
        def sb(name, cols, dt=F32, parts=P):
            return ctx.enter_context(nc.sbuf_tensor(name, [parts, cols], dt))

        sems = {}

        def sem(name):
            if name not in sems:
                sems[name] = nc.alloc_semaphore(name)
            return sems[name]

        KEPT = {"v_chain", "p_chain", "ssq", "ms_done", "root", "x_ready", "x_new0", "xn_ready", "hT_psum", "hT_done_v",
                "hT_done_a", "modc_ready",
                "modc_psum", "g_psum", "g_out", "prio", "logits", "masked", "places", "g_shifted", "g_exp", "d12",
                "d12_exp", "nf_loaded", "ada2_used0", "ada2_used1", "ada2_used2", "pj_shift", "kv_up_loaded", "mixed_own", "mixed_done", "p2_loaded0",
                "p2_loaded1", "p2_loaded2", "p2_loaded3", "branch_loaded0", "branch_loaded1", "out_loaded0"}

        def give_back():
            old = sorted(n for n in sems if n not in KEPT)
            nc.clear_and_free_semaphores([sems.pop(n) for n in old])
            nc.all_engine_barrier()

        def chain(eng, name):
            count = [0]

            def step(ins):
                count[0] += 1
                ins.then_inc(sem(name), 1)
                eng.wait_ge(sem(name), count[0])
            return step

        v_step = chain(nc.vector, "v_chain")
        p_step = chain(nc.gpsimd, "p_chain")

        ring = sb("ring", 6 * CELL)
        side = sb("side", 2 * CELL)
        acc = sb("acc", 6 * D)
        tmp = sb("tmp", CELL)
        x_sb = sb("x_sb", NT * D)
        xn_sb = sb("xn_sb", NT * D)
        hT_sb = sb("hT_sb", KC * S)
        gate_rows = sb("gate_rows", 2 * D)
        ident = sb("ident", P)
        ones = sb("ones", P)
        before = sb("before", P)
        headones = sb("headones", P)
        slot_ids = sb("slot_ids", SLOTS)
        colsA = sb("colsA", P)
        colsB = sb("colsB", P)
        cond = sb("cond", 2 * KC)
        modc = sb("modc", 4 * KC)
        small = sb("small", 64)
        NE_MAX = 32
        TAB = ROUNDS * NE_MAX + 2
        pos_t = sb("pos_t", NT * TAB)
        mask_t = sb("mask_t", NT * TAB)
        gate_t = sb("gate_t", NT * TAB)
        rounds_i = sb("rounds_i", 1, I32)
        qk_cols = sb("qk_cols", 2)
        unused = sb("unused", P)

        ps = [ctx.enter_context(nc.psum_tensor(f"ps{i}", [P, 512], F32)) for i in range(8)]

        x3 = x_sb[:, :].rearrange("p (t d) -> p t d", t=NT)
        xn3 = xn_sb[:, :].rearrange("p (t d) -> p t d", t=NT)
        hT = hT_sb[:, :].rearrange("p (c s) -> p c s", c=KC)
        g_b = gate_rows[:, :].rearrange("p (g d) -> p g d", g=2)

        def cell(i, kc=8, w=512):
            return ring[:, i * CELL:i * CELL + kc * w].rearrange("p (c n) -> p c n", c=kc)

        def w_cols(ap, a, b):
            return ap[:, a:b].rearrange("(c p) n -> p c n", p=P)

        stA, nA = row_starts(ROWS_A)
        stB, nB = row_starts(ROWS_B)
        MU0 = nB + 2
        NB_ALL = MU0 + 15
        rowsA = tmp[:, 0:P]
        rowsB = tmp[:, P:2 * P]
        rowsC = tmp[0:16, 2 * P:3 * P]

        def colA(name, i=0, n=1):
            return colsA[:, stA[name] + i:stA[name] + i + n]

        def colB(name, i=0, n=1):
            return colsB[:, stB[name] + i:stB[name] + i + n]

        lam_in = tmp[:, 512:768].rearrange("p (v d) -> p v d", v=4)
        lam = small[:, 0:8]

        AW = 256
        N_ADA_P = 6 * D // AW
        FIRST_ADA = 8
        ADA_TENSOR = (2, 5)
        FIRST_COLS = FIRST_ADA - len(ADA_TENSOR)

        def side_slot(i):
            if i < FIRST_ADA:
                a = side[:, i * 2048:(i + 1) * 2048] if i < 4 else ring[:, CELL + (i - 4) // 2 * 2 * CELL + i % 2 * 2048:
                                                                        CELL + (i - 4) // 2 * 2 * CELL + (i % 2 + 1) * 2048]
            else:
                a = side[:, ada_turn(i) * 2048:(ada_turn(i) + 1) * 2048]
            return a.rearrange("p (c n) -> p c n", c=8)

        def ada_turn(i):
            return i if i < FIRST_ADA else (i - FIRST_ADA) % 3

        def ada_earlier(i):
            return 0 if i < FIRST_ADA else 1 + (i - FIRST_ADA) // 3

        def load_ada(sp, pieces_):
            for i in pieces_:
                if ada_earlier(i):
                    sp.wait_ge(sem(f"ada_used{ada_turn(i)}"), ada_earlier(i))
                sp.dma_start(side_slot(i), w_cols(inp["ada_w"][0], i * AW, (i + 1) * AW)).then_inc(
                    sem(f"ada_loaded{ada_turn(i)}"), 16)

        def ada_ready(eng, i):
            eng.wait_ge(sem(f"ada_loaded{ada_turn(i)}"), 16 * (ada_earlier(i) + 1))

        ada_count = [0]

        def ada_op(v, i, k):
            a = acc[:, i * AW:(i + 1) * AW]
            w = side_slot(i)
            s = cond[:, k:k + 1]
            if k == 0:
                ada_ready(v, i)
                ins = v.tensor_scalar(a, w[:, k, :], s, None, ALU.mult)
            else:
                v.wait_ge(sem("ada_chain"), ada_count[0])
                ins = v.scalar_tensor_tensor(a, w[:, k, :], s, a, ALU.mult, ALU.add)
            if k < KC - 1:
                ins.then_inc(sem("ada_chain"), 1)
                ada_count[0] += 1
            else:
                ins.then_inc(sem(f"ada_used{ada_turn(i)}"), 1)

        ADA2_AHEAD = 8
        ADA2_PER_PAIR = (N_ADA_P - ADA2_AHEAD) // 8

        def ada2_slot(j):
            a = side[:, j * 2048:(j + 1) * 2048] if j < 3 else acc[:, (j - 2) * 2048:(j - 1) * 2048]
            return a.rearrange("p (c n) -> p c n", c=8)

        def load_ada2(sp, pieces_):
            for i in pieces_:
                if i >= 5:
                    sp.wait_ge(sem(f"ada2_used{i % 5}"), 1)
                sp.dma_start(ada2_slot(i % 5), w_cols(inp["ada_w_2"][0], i * AW, (i + 1) * AW)).then_inc(
                    sem(f"ada2_loaded{i % 5}"), 16)

        def sum_ada2(v, i):
            for k in range(KC):
                for j in (i, i + 1):
                    a = acc[:, j * AW:(j + 1) * AW]
                    w = ada2_slot(j % 5)
                    s = cond[:, KC + k:KC + k + 1]
                    if k == 0:
                        v.wait_ge(sem(f"ada2_loaded{j % 5}"), 16 * (j // 5 + 1))
                        ins = v.tensor_scalar(a, w[:, k, :], s, None, ALU.mult)
                    else:
                        v.wait_ge(sem("ada2_pair"), (i // 2) * 2 * (KC - 1) + 2 * (k - 1) + j - i + 1)
                        ins = v.scalar_tensor_tensor(a, w[:, k, :], s, a, ALU.mult, ALU.add)
                    ins.then_inc(sem("ada2_pair" if k < KC - 1 else f"ada2_used{j % 5}"), 1)

        def ada_wait(eng, n):
            last = {}
            for i in range(n):
                last[ada_turn(i)] = ada_earlier(i) + 1
            for slot, uses in last.items():
                eng.wait_ge(sem(f"ada_used{slot}"), uses)

        def ada_product(pe, i, bank):
            ada_ready(pe, i)
            for j in range(2):
                for k in range(KC):
                    last = pe.matmul(ps[bank][:, 2 * i + j:2 * i + j + 1], side_slot(i)[:, k, j * P:(j + 1) * P],
                                     cond[:, k:k + 1], start=(k == 0), stop=(k == KC - 1))
            last.then_inc(sem(f"ada_used{ada_turn(i)}"), 1)

        def ada_columns(pe, vecs, bank, name, chunks=None):
            for n, m in enumerate(vecs):
                for j in range(KC):
                    if chunks is None or n * KC + j in chunks:
                        last = pe.matmul(ps[bank][:, n * KC + j:n * KC + j + 1], acc[:, m * D + j * P:m * D + (j + 1) * P],
                                         ones[:, 0:1], start=True, stop=True)
            last.then_inc(sem(name), 1)

        def ada_rows(pe, m, bank0, name):
            for n in range(2):
                last = pe.matmul(ps[bank0 + n][:, :], ones[:, :], acc[:, m * D + n * 512:m * D + (n + 1) * 512],
                                 start=True, stop=True)
            last.then_inc(sem(name), 1)


        def load_sqrt(act, col):
            act.activation(small[:, 16 + col:17 + col], ones[:, 0:1], ACT.Sqrt)

        def rms_scalar(act, n, scr, ready):
            for t in range(NT):
                act.wait_ge(sem(ready[0]), ready[1 + t])
                act.activation(scr[:, t * D:(t + 1) * D], x3[:, t, :], ACT.Square,
                               accum_out=small[:, 8 + t:9 + t]).then_inc(sem("ssq"), 1)
            act.wait_ge(sem("ms_done"), n + 1)
            act.activation(small[:, 12:14], small[:, 10:12], ACT.Sqrt).then_inc(sem("root"), 1)

        def rms_vector(v, n, out3, weight=None, name="xn_ready"):
            v.wait_ge(sem("ssq"), NT * (n + 1))
            v.tensor_scalar(small[:, 10:12], small[:, 8:10], 1.0 / D, EPS, ALU.mult, ALU.add).then_inc(
                sem("ms_done"), 1)
            v.wait_ge(sem("root"), n + 1)
            v_step(v.reciprocal(small[:, 14:16], small[:, 12:14]))
            for t in range(NT):
                if weight is None:
                    ins = v.tensor_scalar(out3[:, t, :], x3[:, t, :], small[:, 14 + t:15 + t], None, ALU.mult)
                else:
                    ins = v.scalar_tensor_tensor(out3[:, t, :], x3[:, t, :], small[:, 14 + t:15 + t], weight,
                                                 ALU.mult, ALU.mult)
            ins.then_inc(sem(name), 1)

        def hT_tensor(pe, n):
            pe.wait_ge(sem("xn_ready"), n + 1)
            for c in range(KC):
                b = ps[4 + c // 2]
                for t in range(NT):
                    o = (c % 2) * S + t * P
                    last = pe.transpose(b[:, o:o + P], xn3[:, t, c * P:(c + 1) * P], ident[:, :])
                if c % 2:
                    last.then_inc(sem("hT_psum"), 1)

        def hT_args(n, c):
            m = 2 * (n % 2) * KC
            o = (c % 2) * S
            return hT[:, c, :], ps[4 + c // 2][:, o:o + S], modc[:, m + c:m + c + 1], modc[:, m + KC + c:m + KC + c + 1]

        HT_VECTOR, HT_SCALAR = (0, 1, 4, 5), (2, 3, 6, 7)

        def hT_vector(v, n):
            for c in HT_VECTOR:
                v.wait_ge(sem("hT_psum"), 4 * n + c // 2 + 1)
                dst, src, scale, shift = hT_args(n, c)
                v.tensor_scalar(dst, src, scale, shift, ALU.mult, ALU.add).then_inc(sem("hT_done_v"), 1)

        def hT_scalar(act, n):
            act.wait_ge(sem("modc_ready"), (1, 2, 3, 4)[n])
            for c in HT_SCALAR:
                act.wait_ge(sem("hT_psum"), 4 * n + c // 2 + 1)
                dst, src, scale, shift = hT_args(n, c)
                act.activation(dst, src, ACT.Identity, scale=scale, bias=shift).then_inc(sem("hT_done_a"), 1)

        def hT_wait(eng, n, c=KC - 1):
            eng.wait_ge(sem("hT_done_v"), 4 * n + len([x for x in HT_VECTOR if x <= c]))
            a = len([x for x in HT_SCALAR if x <= c])
            if 4 * n + a:
                eng.wait_ge(sem("hT_done_a"), 4 * n + a)

        def router_tensor(pe, k, ne):
            pe.wait_ge(sem(f"router{k}"), 64 if k == 0 else 48)
            rw = tmp[:, 2048:2048 + KC * (4 + ne)].rearrange("p (c n) -> p c n", c=KC)
            for c in range(KC):
                hT_wait(pe, 2 * k + 1, c)
                for t in range(NT):
                    last = pe.matmul(ps[t][:, 0:4 + ne], hT[:, c, t * P:(t + 1) * P], rw[:, c, :],
                                     start=(c == 0), stop=(c == KC - 1))
            last.then_inc(sem("logits"), 1)

        def load_attn(sp, cells):
            for i in cells:
                sp.dma_start(cell(i), w_cols(inp["attn_w_in"][0], i * 512, (i + 1) * 512)).then_inc(
                    sem(f"m1_loaded{i}"), 16)

        MOE = [[inp["expert_w_gate"][0], inp["expert_w_up"][0], inp["expert_w_down"][0]],
               [inp["expert_w_gate_2"][0], inp["expert_w_up_2"][0], inp["expert_w_down_2"][0]]]

        def expert_cell(i):
            return cell(i) if i % 3 < 2 else cell(i, 4, 1024)

        def load_expert(sp, k, cells):
            for i in cells:
                sp.dma_start(expert_cell(i), MOE[k][i % 3][i // 3:i // 3 + 1, :, :].rearrange("o (c p) n -> p (o c) n", p=P)).then_inc(
                    sem(f"moe{k}_loaded{i}"), 16)

        with nc.Block() as block:
            @block.sync
            def _(sp):
                for i, name in enumerate(("c", "c_2")):
                    sp.dma_start(rowsC[8 * i:8 * i + 8, :], inp[name].rearrange("a (r n) -> (a r) n", n=P)).then_inc(
                        sem("c_loaded"), 16)
                load_ada(sp, range(1))
                sp.dma_start(x3, inp["x"][0].rearrange("(t p) d -> p t d", p=P)).then_inc(sem("x_loaded"), 16)
                load_ada(sp, range(1, 4))
                sp.wait_ge(sem("rows_zero"), 1)
                for rows, st, spec in ((rowsA, stA, ROWS_A), (rowsB, stB, ROWS_B)):
                    for name, n in spec:
                        src = inp[name]
                        src = src.rearrange("a h d -> (a h d)") if name == "rwkv_r_k_2" else src.rearrange("a n -> (a n)")
                        sp.dma_start(rows[st[name]:st[name] + n, :], src.rearrange("(r n) -> r n", n=P)).then_inc(
                            sem("rows_loaded"), 16)
                for i, name in enumerate(("q_norm_g_2", "k_norm_g_2")):
                    for h in range(2):
                        sp.dma_start(rowsB[nB + i:nB + i + 1, h * 64:(h + 1) * 64], inp[name]).then_inc(
                            sem("rows_loaded"), 16)
                mu = inp["rwkv_mu_2"].rearrange("a n -> (a n)")
                sp.dma_start(rowsB[MU0:MU0 + 14, :], mu[0:14 * P].rearrange("(r n) -> r n", n=P)).then_inc(
                    sem("rows_loaded"), 16)
                sp.dma_start(rowsB[MU0 + 14:MU0 + 15, 0:32], mu[14 * P:14 * P + 32].rearrange("(a n) -> a n", a=1)).then_inc(
                    sem("rows_loaded"), 16)
                load_ada(sp, range(4, 8))
                load_attn(sp, (0, 2, 4))
                for i, name in enumerate(("attn_lam_q1", "attn_lam_k1", "attn_lam_q2", "attn_lam_k2")):
                    sp.dma_start(lam_in[:, i, :], inp[name][0:1, :].broadcast_to((P, 64))).then_inc(
                        sem("lam_loaded"), 16)
                for i, m in enumerate((2, 5)):
                    sp.dma_start(g_b[:, i, :], inp["ada_b"][0:1, m * D:(m + 1) * D].broadcast_to((P, D))).then_inc(
                        sem("gb_loaded"), 16)
            N_ROW_DMAS = len(ROWS_A) + len(ROWS_B) + 6

            @block.gpsimd
            def _(pool):
                p_step(pool.memset(ident[:, :], 0.0))
                pool.affine_select(out=ident[:, :], in_=ident[:, :], compare_op=ALU.not_equal, fill=1.0, base=0,
                                   pattern=[[-1, P]], channel_multiplier=1).then_inc(sem("ident"), 1)
                pool.memset(tmp[:, 0:2 * P], 0.0).then_inc(sem("rows_zero"), 1)
                pool.wait_ge(sem("rows_zero"), 1)
                p_step(pool.memset(ones[:, :], 1.0))
                p_step(pool.memset(headones[:, :], 1.0))
                p_step(pool.affine_select(out=before[:, :], in_=ones[:, :], compare_op=ALU.is_gt, fill=0.0, base=0,
                                          pattern=[[1, P]], channel_multiplier=-1))
                p_step(pool.memset(headones[0:64, 64:128], 0.0))
                p_step(pool.memset(headones[64:128, 0:64], 0.0))
                pool.iota(slot_ids[:, :], pattern=[[1, SLOTS]], base=0, channel_multiplier=0,
                          allow_small_or_imprecise_dtypes=True).then_inc(sem("const"), 1)

            @block.tensor
            def _(pe):
                pe.wait_ge(sem("ident"), 1)
                pe.wait_ge(sem("c_loaded"), 32)
                pe.transpose(ps[2][:, 0:16], rowsC, ident[0:16, 0:16]).then_inc(sem("c_psum"), 1)
                hT_tensor(pe, 0)
                pe.wait_ge(sem("cond"), 1)
                pe.wait_ge(sem("const"), 1)
                for i in range(FIRST_ADA):
                    if i in ADA_TENSOR:
                        ada_product(pe, i, 1)
                    else:
                        pe.wait_ge(sem(f"ada_used{ada_turn(i)}"), 1)
                        ada_columns(pe, (0, 1), 1, "modc_psum", (2 * i, 2 * i + 1))
                    if i == 4:
                        pe.wait_ge(sem("rows_loaded"), 16 * N_ROW_DMAS)
                        pe.transpose(ps[0][:, 0:P], rowsA, ident[:, :])
                        pe.transpose(ps[0][:, P:2 * P], rowsB, ident[:, :]).then_inc(sem("cols_psum"), 1)

            @block.scalar
            def _(act):
                act.wait_ge(sem("c_psum"), 1)
                act.activation(cond[:, :], ps[2][:, 0:16], ACT.Sigmoid).then_inc(sem("sig_c"), 1)
                rms_scalar(act, 0, xn_sb, ("x_loaded", 16, 16))

            @block.vector
            def _(v):
                v.wait_ge(sem("sig_c"), 1)
                v.tensor_tensor(cond[:, :], cond[:, :], ps[2][:, 0:16], ALU.mult).then_inc(sem("cond"), 1)
                v.wait_ge(sem("cond"), 1)
                for i in range(FIRST_ADA):
                    for k in range(KC):
                        if i not in ADA_TENSOR:
                            ada_op(v, i, k)
                    if i == 0:
                        rms_vector(v, 0, xn3)
                v.wait_ge(sem("cols_psum"), 1)
                v.tensor_copy(colsA[:, :], ps[0][:, 0:P]).then_inc(sem("cols_done"), 1)
                v.tensor_copy(colsB[:, :], ps[0][:, P:2 * P]).then_inc(sem("cols_done"), 1)
                v.wait_ge(sem("cols_done"), 2)

        H = 8
        U = H * NT
        qkT = tmp[:, :].rearrange("p (w h s) -> p w h s", w=2, h=H)
        v3 = xn3
        sub08 = qk_cols[:, 0:1]
        LAM_INIT = 0.8 - 0.6 * math.exp(0.0)
        sS = acc[:, 0:1536].rearrange("p (b n) -> p b n", b=3)
        aT = acc[:, 1536:2048].rearrange("p (b n) -> p b n", b=2)
        o_heads = side[:, 6144:8192]
        o3 = o_heads.rearrange("p (t d) -> p t d", t=NT)
        dist = (pos_t[:, 0:S], mask_t[:, 0:S])
        st_a = gate_t[:, 0:256]
        ADA_STEPS = (0, 2, 2, 0, 3, 3, 3, 3, 0)
        ada_at = [8 + sum(ADA_STEPS[:h]) for h in range(H + 2)]

        def fill_modc(v, count, vec_scale, vec_shift, psc, shift_at, scale_at, norm_col, ada_shift, ada_scale):
            v_step(v.tensor_tensor(modc[:, vec_shift:vec_shift + KC], psc[:, shift_at:shift_at + KC], ada_shift, ALU.add))
            v_step(v.tensor_tensor(modc[:, vec_scale:vec_scale + KC], psc[:, scale_at:scale_at + KC], ada_scale, ALU.add))
            v.scalar_tensor_tensor(modc[:, vec_scale:vec_scale + KC], modc[:, vec_scale:vec_scale + KC], 1.0,
                                   norm_col, ALU.add, ALU.mult).then_inc(sem("modc_ready"), 1)
            v.wait_ge(sem("modc_ready"), count)

        with nc.Block() as block:
            @block.sync
            def _(sp):
                load_ada(sp, range(8, 12))
                load_attn(sp, (1, 3, 5))
                load_ada(sp, range(12, 24))
                sp.wait_ge(sem("v_psum"), H // 2)
                sp.dma_start(cell(4), w_cols(inp["attn_w_out"][0], 0, 512)).then_inc(sem("wo1_loaded0"), 16)
                load_expert(sp, 0, (0, 2))
                sp.wait_ge(sem("v_psum"), H)
                sp.dma_start(cell(5), w_cols(inp["attn_w_out"][0], 512, 1024)).then_inc(sem("wo1_loaded1"), 16)
                load_expert(sp, 0, (1, 3))
                ada_wait(sp, N_ADA_P)
                load_ada2(sp, range(3))

            @block.gpsimd
            def _(pool):
                for t in range(NT):
                    last = pool.iota(dist[t], pattern=[[-1, S]], base=t * P, channel_multiplier=1,
                                     allow_small_or_imprecise_dtypes=True)
                    last.then_inc(sem("dist"), 1)

            @block.tensor
            def _(pe):
                def project_qk(h, w, half):
                    if half == 0:
                        if h % 4 == 0:
                            pe.wait_ge(sem(f"m1_loaded{2 * w + h // 4}"), 16)
                        if h and w == 0:
                            pe.wait_ge(sem("qk_out"), h)
                    for c in range(4 * half, 4 * half + 4):
                        last = pe.matmul(ps[6][:, w * S:(w + 1) * S], cell(2 * w + h // 4)[:, c, (h % 4) * P:(h % 4 + 1) * P],
                                         hT[:, c, :], start=(c == 0), stop=(c == KC - 1))
                    if half and w:
                        last.then_inc(sem("qk_psum"), 1)

                def project_v(h, t):
                    if t == 0:
                        if h % 4 == 0:
                            pe.wait_ge(sem(f"m1_loaded{4 + h // 4}"), 16)
                        if h:
                            pe.wait_ge(sem("v_out"), h)
                    for c in range(KC):
                        last = pe.matmul(ps[7][:, t * P:(t + 1) * P], hT[:, c, t * P:(t + 1) * P],
                                         cell(4 + h // 4)[:, c, (h % 4) * P:(h % 4 + 1) * P],
                                         start=(c == 0), stop=(c == KC - 1))
                    if t:
                        last.then_inc(sem("v_psum"), 1)

                def scores(u):
                    h, t = u // NT, u % NT
                    if t == 0:
                        pe.wait_ge(sem("qk_out"), h + 1)
                    if u >= 2:
                        pe.wait_ge(sem("att_biased"), u - 1)
                    for w in range(2):
                        last = pe.matmul(ps[2 * (u % 2) + w][:, 0:S], qkT[w * 64:(w + 1) * 64, 0, h, t * P:(t + 1) * P],
                                         qkT[w * 64:(w + 1) * 64, 1, h, :], start=True, stop=True)
                    last.then_inc(sem("att_scores"), 1)

                def turn(u):
                    pe.wait_ge(sem("att_a"), u + 1)
                    if u:
                        pe.wait_ge(sem("att_aT"), u)
                    for k in range(2):
                        last = pe.transpose(ps[4][:, k * P:(k + 1) * P], sS[:, u % 3, k * P:(k + 1) * P], ident[:, :])
                    last.then_inc(sem("att_aT_psum"), 1)

                def av(u):
                    h = u // NT
                    pe.wait_ge(sem("att_aT"), u + 1)
                    pe.wait_ge(sem("v_out"), h + 1)
                    if u:
                        pe.wait_ge(sem("att_o"), u)
                    for k in range(2):
                        last = pe.matmul(ps[5][:, 0:P], aT[:, u % 2, k * P:(k + 1) * P],
                                         v3[:, k, h * P:(h + 1) * P], start=(k == 0), stop=(k == 1))
                    last.then_inc(sem("att_av"), 1)

                hT_wait(pe, 0)
                for h in range(H + 1):
                    a, b = 2 * h - 2, 2 * h - 1
                    if h < H:
                        project_qk(h, 0, 0)
                    if h:
                        scores(a)
                    if h < H:
                        project_qk(h, 0, 1)
                    if h:
                        scores(b)
                    if h < H:
                        project_qk(h, 1, 0)
                        project_qk(h, 1, 1)
                    else:
                        ada_wait(pe, 24)
                        pe.wait_ge(sem("v_out"), H)
                        ada_rows(pe, 2, 6, "g_psum")
                    if h:
                        turn(a)
                    if h < H:
                        project_v(h, 0)
                    if h:
                        turn(b)
                        av(a)
                    if h < H:
                        project_v(h, 1)
                    else:
                        ada_rows(pe, 5, 0, "g_psum")
                        ada_columns(pe, (3, 4), 2, "modc_psum")
                    if h:
                        av(b)

            @block.scalar
            def _(act):
                hT_scalar(act, 0)
                act.wait_ge(sem("lam_sums"), 1)
                act.activation(lam[:, 2:4], lam[:, 0:2], ACT.Exp).then_inc(sem("lam_exp"), 1)

                def exponentials(u):
                    act.wait_ge(sem("att_max"), u + 1)
                    for w in range(2):
                        x = sS[:, u % 3, w * S:(w + 1) * S]
                        act.activation(x, x, ACT.Exp, bias=st_a[:, 4 * u + w:4 * u + w + 1], scale=0.125,
                                       accum_out=st_a[:, 4 * u + 2 + w:4 * u + 3 + w]).then_inc(sem("att_exp"), 1)

                def take_turned(u):
                    act.wait_ge(sem("att_aT_psum"), u + 1)
                    act.activation(aT[:, u % 2, :], ps[4][:, 0:S], ACT.Copy).then_inc(sem("att_aT"), 1)

                def square(u):
                    h, t = u // NT, u % NT
                    act.wait_ge(sem("att_o"), u + 1)
                    if u:
                        act.wait_ge(sem("o_sq"), u)
                    act.activation(unused[:, :], o3[:, t, h * P:(h + 1) * P], ACT.Square,
                                   accum_out=st_a[:, 128 + t * H + h:129 + t * H + h]).then_inc(sem("o_sq"), 1)

                for h in range(H + 1):
                    a, b = 2 * h - 2, 2 * h - 1
                    if h:
                        exponentials(a)
                        exponentials(b)
                    if h == H:
                        load_sqrt(act, 0)
                    if h >= 2:
                        square(a - 2)
                        square(b - 2)
                    if h < H:
                        act.wait_ge(sem("qk_psum"), h + 1)
                        act.activation(qkT[:, :, h, :], ps[6][:, :].rearrange("p (w s) -> p w s", w=2), ACT.Copy).then_inc(
                            sem("qk_out"), 1)
                    if h:
                        take_turned(a)
                        take_turned(b)
                    if h < H:
                        act.wait_ge(sem("v_psum"), h + 1)
                        act.activation(v3[:, :, h * P:(h + 1) * P], ps[7][:, 0:S].rearrange("p (t d) -> p t d", t=NT),
                                       ACT.Copy).then_inc(sem("v_out"), 1)
                square(U - 2)
                square(U - 1)

            @block.vector
            def _(v):
                v.wait_ge(sem("modc_psum"), FIRST_COLS)
                fill_modc(v, 1, 0, KC, ps[1], 0, KC, colA("norm_mix", 0, KC), colA("ada_b", 0, KC), colA("ada_b", KC, KC))
                hT_vector(v, 0)
                v.wait_ge(sem("lam_loaded"), 64)
                for i in range(2):
                    v_step(v.tensor_tensor(lam_in[:, 2 * i, :], lam_in[:, 2 * i, :], lam_in[:, 2 * i + 1, :], ALU.mult))
                    ins = v.tensor_reduce(lam[:, i:i + 1], lam_in[:, 2 * i, :], X, ALU.add)
                ins.then_inc(sem("lam_sums"), 1)
                v_step(v.tensor_scalar(sub08, colB("attn_subln"), 1.0 - LAM_INIT, None, ALU.mult))
                v.wait_ge(sem("lam_exp"), 1)
                v_step(v.tensor_tensor(lam[:, 4:5], lam[:, 2:3], lam[:, 3:4], ALU.subtract))
                v_step(v.tensor_scalar(lam[:, 5:6], lam[:, 4:5], -1.0, -LAM_INIT, ALU.mult, ALU.add))
                v.wait_ge(sem("dist"), 2)
                for t in range(NT):
                    ins = v.scalar_tensor_tensor(dist[t], dist[t], -1.0, dist[t], ALU.mult, ALU.max)
                v_step(ins)

                def first(u):
                    h, t = u // NT, u % NT
                    v.wait_ge(sem("att_scores"), u + 1)
                    if u >= 3:
                        v.wait_ge(sem("att_aT_psum"), u - 2)
                    for w in range(2):
                        ins = v.scalar_tensor_tensor(sS[:, u % 3, w * S:(w + 1) * S], dist[t], -8.0 * 2.0 ** -(h + 1),
                                                     ps[2 * (u % 2) + w][:, 0:S], ALU.mult, ALU.add)
                    ins.then_inc(sem("att_biased"), 1)
                    v.wait_ge(sem("att_biased"), u + 1)
                    v_step(v.tensor_reduce(st_a[:, 192 + 2 * (u % 2):194 + 2 * (u % 2)],
                                           sS[:, u % 3, :].rearrange("p (w s) -> p w s", w=2), X, ALU.max))
                    v.tensor_scalar(st_a[:, 4 * u:4 * u + 2], st_a[:, 192 + 2 * (u % 2):194 + 2 * (u % 2)], -0.125, None,
                                    ALU.mult).then_inc(sem("att_max"), 1)

                def second(u):
                    v.wait_ge(sem("att_exp"), 2 * u + 2)
                    r = st_a[:, 64 + 4 * u:64 + 4 * u + 2]
                    x = sS[:, u % 3, :]
                    v_step(v.reciprocal(r, st_a[:, 4 * u + 2:4 * u + 4]))
                    v.tensor_scalar(r[:, 1:2], r[:, 1:2], lam[:, 5:6], None, ALU.mult)
                    v_step(v.tensor_scalar(x[:, 0:S], x[:, 0:S], r[:, 0:1], None, ALU.mult))
                    v.scalar_tensor_tensor(x[:, 0:S], x[:, S:2 * S], r[:, 1:2], x[:, 0:S],
                                           ALU.mult, ALU.add).then_inc(sem("att_a"), 1)

                def third(u):
                    h, t = u // NT, u % NT
                    v.wait_ge(sem("att_av"), u + 1)
                    v.tensor_copy(o3[:, t, h * P:(h + 1) * P], ps[5][:, 0:P]).then_inc(sem("att_o"), 1)

                for h in range(H + 1):
                    a, b = 2 * h - 2, 2 * h - 1
                    todo = [(i, k) for i in range(ada_at[h], ada_at[h + 1]) for k in range(KC)]

                    def fill(n):
                        for _ in range(min(n, len(todo))):
                            ada_op(v, *todo.pop(0))
                    if h:
                        first(a)
                        fill(1)
                        first(b)
                        second(a)
                        fill(1)
                        second(b)
                        fill(5)
                        third(a)
                        fill(5)
                        third(b)
                    fill(KC * 3)
                v.wait_ge(sem("gb_loaded"), 32)
                for i in range(2):
                    v.wait_ge(sem("g_psum"), i + 1)
                    for n in range(2):
                        a = g_b[:, i, n * 512:(n + 1) * 512]
                        ins = v.tensor_tensor(a, ps[(6, 0)[i] + n][:, :], a, ALU.add)
                    ins.then_inc(sem("g_out"), 1)
                v.wait_ge(sem("modc_psum"), FIRST_COLS + 1)
                fill_modc(v, 2, 2 * KC, 3 * KC, ps[2], 0, KC, colA("norm_ffn", 0, KC), colA("ada_b", 3 * KC, KC), colA("ada_b", 4 * KC, KC))

        NG = 4

        def load_router(sp, k, wg, we, bg, be):
            ne = be.shape[1]
            rw = tmp[:, 2048:2048 + KC * (NG + ne)].rearrange("p (c n) -> p c n", c=KC)
            sp.dma_start(rw[:, :, 0:NG], wg.rearrange("(c p) g -> p c g", p=P)).then_inc(sem(f"router{k}"), 16)
            sp.dma_start(rw[:, :, NG:], we.rearrange("(c p) g -> p c g", p=P)).then_inc(sem(f"router{k}"), 16)
            if bg is not None:
                sp.dma_start(tmp[:, 2400:2400 + NG], bg.broadcast_to((P, NG))).then_inc(sem(f"router{k}"), 16)
            sp.dma_start(tmp[:, 2400 + NG:2400 + NG + ne], be.broadcast_to((P, ne))).then_inc(sem(f"router{k}"), 16)

        oT = hT

        def residual(v, g, i, name):
            t, n = g // 2, g % 2
            v.wait_ge(sem(name), g + 1)
            y = tmp[:, g * 512:(g + 1) * 512]
            v_step(v.tensor_tensor(y, ps[g][:, :], g_b[:, i, n * 512:(n + 1) * 512], ALU.mult))
            xs = x3[:, t, n * 512:(n + 1) * 512]
            v.tensor_tensor(xs, xs, y, ALU.add).then_inc(sem(name + "_x"), 1)

        with nc.Block() as block:
            @block.sync
            def _(sp):
                load_router(sp, 0, inp["router_group_w"][0], inp["router_expert_w"][0].rearrange("d g e -> d (g e)"),
                            inp["router_group_b"], inp["router_expert_b"].rearrange("a g e -> a (g e)"))
                load_ada2(sp, range(3, ADA2_AHEAD))
                sp.wait_ge(sem("y1"), 4)
                load_expert(sp, 0, (4, 5))

            @block.tensor
            def _(pe):
                pe.wait_ge(sem("o_normed"), 1)
                for c in range(H):
                    b = ps[4 + c // 2]
                    for t in range(NT):
                        o = (c % 2) * S + t * P
                        last = pe.transpose(b[:, o:o + P], o3[:, t, c * P:(c + 1) * P], ident[:, :])
                    last.then_inc(sem("oT_psum"), 1)
                for g in range(4):
                    t, n = g // 2, g % 2
                    if t == 0:
                        pe.wait_ge(sem(f"wo1_loaded{n}"), 16)
                    pe.wait_ge(sem("oT_done"), H)
                    for c in range(KC):
                        last = pe.matmul(ps[g][:, :], oT[:, c, t * P:(t + 1) * P], cell(4 + n)[:, c, :],
                                         start=(c == 0), stop=(c == KC - 1))
                    last.then_inc(sem("y1"), 1)
                hT_tensor(pe, 1)
                router_tensor(pe, 0, 16)

            @block.scalar
            def _(act):
                act.wait_ge(sem("o_ms"), 1)
                act.activation(st_a[:, 16:32], st_a[:, 0:16], ACT.Sqrt).then_inc(sem("o_root"), 1)
                rms_scalar(act, 1, xn_sb, ("y1_x", 2, 4))
                hT_scalar(act, 1)

            @block.vector
            def _(v):
                v.wait_ge(sem("o_sq"), U)
                v.tensor_scalar(st_a[:, 0:16], st_a[:, 128:144], 1.0 / P, EPS, ALU.mult, ALU.add).then_inc(sem("o_ms"), 1)
                v.wait_ge(sem("o_root"), 1)
                v_step(v.reciprocal(st_a[:, 48:64], st_a[:, 16:32]))
                og = o_heads.rearrange("p (g d) -> p g d", d=P)
                v.tensor_tensor(og, og, st_a[:, 48:64].unsqueeze(2).broadcast_to((P, 16, P)), ALU.mult).then_inc(sem("o_normed"), 1)
                for c in range(H):
                    v.wait_ge(sem("oT_psum"), 2 * (c // 2) + 2)
                    o = (c % 2) * S
                    v.tensor_scalar(oT[:, c, :], ps[4 + c // 2][:, o:o + S], sub08, None, ALU.mult).then_inc(sem("oT_done"), 1)
                for i in range(0, ADA2_AHEAD, 2):
                    sum_ada2(v, i)
                    if i >= 4:
                        residual(v, i // 2 - 2, 0, "y1")
                residual(v, 2, 0, "y1")
                residual(v, 3, 0, "y1")
                rms_vector(v, 1, xn3)
                hT_vector(v, 1)

        def route(k, ne, has_bg):
            EP = ne // NG
            NR = NG + ne
            W_TAB = ROUNDS * ne + 2
            rw = tmp[:, 2048:2048 + KC * NR].rearrange("p (c n) -> p c n", c=KC)
            bias = tmp[:, 2400:2400 + NR]
            pos = pos_t[:, 0:NT * W_TAB].rearrange("p (t n) -> p t n", t=NT)
            mask = mask_t[:, 0:NT * W_TAB].rearrange("p (t n) -> p t n", t=NT)
            gate = gate_t[:, 0:NT * W_TAB].rearrange("p (t n) -> p t n", t=NT)
            at = [2500]

            def t2(*dims):
                n = int(np.prod(dims))
                a = tmp[:, at[0]:at[0] + n]
                at[0] += n
                if len(dims) == 2:
                    return a.rearrange("p (t n) -> p t n", t=dims[0])
                if len(dims) == 3:
                    return a.rearrange("p (t g n) -> p t g n", t=dims[0], g=dims[1])
                return a
            L = t2(NT, NR)
            prio = t2(8)
            gm, em, zs, v1, m1, v2, m2, d12, w1, w2, gw = [t2(NT) for _ in range(11)]
            ohg, gs = t2(NT, NG), t2(NT, NG)
            prod = t2(NT, NG, EP)
            esel, e2, oh1, oh2, ew, em_ = [t2(NT, EP) for _ in range(6)]
            cnt, thr, rf = t2(ne), t2(4), t2(4)

            def per(a, n):
                return a.unsqueeze(2).broadcast_to((P, NT, n))

            with nc.Block() as block:
                @block.gpsimd
                def _(pool):
                    pool.iota(prio, pattern=[[-1, 8]], base=8, channel_multiplier=0,
                              allow_small_or_imprecise_dtypes=True).then_inc(sem("prio"), 1)

                @block.tensor
                def _(pe):
                    if k == 0:
                        for q in range(3):
                            pe.wait_ge(sem(f"ada2_used{q}"), 2)
                        ada_columns(pe, (0, 1), 2, "modc_psum")
                    pe.wait_ge(sem("masked"), k + 1)
                    pe.matmul(ps[1][:, 0:ne], before[:, :], mask[:, 0, 0:ne], start=True, stop=True)
                    pe.matmul(ps[1][:, ne:2 * ne], ones[:, :], mask[:, 0, 0:ne], start=True, stop=False)
                    pe.matmul(ps[1][:, ne:2 * ne], before[:, :], mask[:, 1, 0:ne], start=False, stop=True)
                    pe.matmul(ps[1][:, 2 * ne:3 * ne], ones[:, :], mask[:, 0, 0:ne], start=True, stop=False)
                    pe.matmul(ps[1][:, 2 * ne:3 * ne], ones[:, :], mask[:, 1, 0:ne], start=False, stop=True).then_inc(
                        sem("places"), 1)

                @block.scalar
                def _(act):
                    act.wait_ge(sem("g_shifted"), k + 1)
                    act.activation(gs, gs, ACT.Exp).then_inc(sem("g_exp"), 1)
                    act.wait_ge(sem("d12"), k + 1)
                    act.activation(d12, d12, ACT.Exp).then_inc(sem("d12_exp"), 1)

                @block.vector
                def _(v):
                    v_step(v.memset(pos, 0.0))
                    v_step(v.memset(mask, 0.0))
                    v_step(v.memset(gate, 0.0))
                    v.wait_ge(sem("prio"), k + 1)
                    v.wait_ge(sem("logits"), k + 1)
                    for t in range(NT):
                        if has_bg:
                            v_step(v.tensor_tensor(L[:, t, :], ps[t][:, 0:NR], bias, ALU.add))
                        else:
                            v.tensor_copy(L[:, t, 0:NG], ps[t][:, 0:NG])
                            v_step(v.tensor_tensor(L[:, t, NG:], ps[t][:, NG:NR], bias[:, NG:], ALU.add))
                    G = L[:, :, 0:NG]
                    E4 = L[:, :, NG:].rearrange("p t (g e) -> p t g e", g=NG)

                    def first_max(src, n, top, best, oh):
                        v_step(v.tensor_reduce(top, src, X, ALU.max))
                        v_step(v.tensor_tensor(oh, src, per(top, n), ALU.is_equal))
                        v_step(v.tensor_tensor(oh, oh, prio[:, 0:n].unsqueeze(1).broadcast_to((P, NT, n)), ALU.mult))
                        v_step(v.tensor_reduce(best, oh, X, ALU.max))
                        v_step(v.tensor_tensor(oh, oh, per(best, n), ALU.is_equal))
                    first_max(G, NG, gm, em, ohg)
                    v.tensor_tensor(gs, G, per(gm, NG), ALU.subtract).then_inc(sem("g_shifted"), 1)
                    v_step(v.tensor_tensor(prod, E4, ohg.unsqueeze(3).broadcast_to((P, NT, NG, EP)), ALU.mult))
                    v_step(v.tensor_reduce(esel, prod.rearrange("p t g e -> p t e g"), X, ALU.add))
                    first_max(esel, EP, v1, m1, oh1)
                    v_step(v.scalar_tensor_tensor(e2, oh1, -BIG, esel, ALU.mult, ALU.add))
                    first_max(e2, EP, v2, m2, oh2)
                    v.tensor_tensor(d12, v2, v1, ALU.subtract).then_inc(sem("d12"), 1)
                    v.wait_ge(sem("g_exp"), k + 1)
                    v_step(v.tensor_reduce(zs, gs, X, ALU.add))
                    v_step(v.reciprocal(gw, zs))
                    v.wait_ge(sem("d12_exp"), k + 1)
                    v_step(v.tensor_scalar(w1, d12, 1.0, None, ALU.add))
                    v_step(v.reciprocal(w1, w1))
                    v_step(v.tensor_tensor(w1, w1, gw, ALU.mult))
                    v_step(v.tensor_tensor(w2, w1, d12, ALU.mult))
                    v_step(v.tensor_tensor(em_, oh1, oh2, ALU.add))
                    v_step(v.tensor_tensor(oh1, oh1, per(w1, EP), ALU.mult))
                    v_step(v.tensor_tensor(oh2, oh2, per(w2, EP), ALU.mult))
                    v_step(v.tensor_tensor(ew, oh1, oh2, ALU.add))
                    for dst, src in ((mask, em_), (gate, ew)):
                        ins = v.tensor_tensor(dst[:, :, 0:ne].rearrange("p t (g e) -> p t g e", g=NG),
                                              ohg.unsqueeze(3).broadcast_to((P, NT, NG, EP)),
                                              src.unsqueeze(2).broadcast_to((P, NT, NG, EP)), ALU.mult)
                        if dst is mask:
                            ins.then_inc(sem("masked"), 1)
                        else:
                            v_step(ins)
                    v.wait_ge(sem("masked"), k + 1)
                    for q in range(1, ROUNDS):
                        v.tensor_copy(mask[:, :, q * ne:(q + 1) * ne], mask[:, :, 0:ne])
                        v.tensor_copy(gate[:, :, q * ne:(q + 1) * ne], gate[:, :, 0:ne])
                    if k == 0:
                        v.wait_ge(sem("modc_psum"), FIRST_COLS + 2)
                        fill_modc(v, 3, 0, KC, ps[2], 0, KC, colA("mix_norm_g_2", 0, KC), colB("ada_b_2", 0, KC), colB("ada_b_2", KC, KC))
                    v.wait_ge(sem("places"), k + 1)
                    pp = ps[1][:, 0:NT * ne].rearrange("p (t n) -> p t n", t=NT)
                    for q in range(ROUNDS):
                        v.tensor_scalar(pos[:, :, q * ne:(q + 1) * ne], pp, -float(q * SLOTS), None, ALU.add)
                    v_step(v.tensor_reduce(cnt[:, 0:1], ps[1][:, 2 * ne:3 * ne], X, ALU.max))
                    for q in range(1, ROUNDS):
                        v_step(v.tensor_scalar(thr[:, q:q + 1], cnt[:, 0:1], float(q * SLOTS), None, ALU.is_gt))
                    v_step(v.tensor_tensor(rf[:, 0:1], thr[:, 1:2], thr[:, 2:3], ALU.add))
                    v_step(v.tensor_tensor(rf[:, 0:1], rf[:, 0:1], thr[:, 3:4], ALU.add))
                    v_step(v.tensor_scalar(rounds_i[:, :], rf[:, 0:1], 1.0, None, ALU.add))

        def experts(k, ne, sides=None, afterwards=None, ahead=True):
            NP = ne // 2
            W_TAB = ROUNDS * ne + 2
            pos = pos_t[:, 0:NT * W_TAB].rearrange("p (t n) -> p t n", t=NT)
            mask = mask_t[:, 0:NT * W_TAB].rearrange("p (t n) -> p t n", t=NT)
            gate = gate_t[:, 0:NT * W_TAB].rearrange("p (t n) -> p t n", t=NT)
            xg = hT_sb[:, 0:1024].rearrange("p (c n) -> p c n", c=KC)
            outb = hT_sb[:, 1024:2048]
            hid = tmp[:, 0:FE]
            hidT = tmp[:, FE:2 * FE].rearrange("p (f n) -> p f n", f=FC)
            oh = tmp[:, 1024:1280].rearrange("p (t n) -> p t n", t=NT)
            ohw = tmp[:, 1280:1536].rearrange("p (t n) -> p t n", t=NT)
            pT = tmp[:, 1536:1792]
            zero = tmp[:, 1792:1792 + 512]
            y_ps, gate_ps, up_ps, out_ps = ps[0:4], ps[4], ps[5], ps[6:8]
            n = f"{k}"

            SPARE = {0: {0: 1}, 1: {0: 0, 1: 1}}[k]

            def odd(e, j, par):
                return par == 1 and j == 0 and e in SPARE

            def dst(e, j, par):
                if odd(e, j, par):
                    return side[:, SPARE[e] * CELL:(SPARE[e] + 1) * CELL].rearrange("p (c n) -> p c n", c=KC)
                return expert_cell(3 * e + j)

            def loaded(e, j, par):
                return sem(f"moe{n}_odd{e}" if odd(e, j, par) else f"moe{n}_loaded{3 * e + j}")

            def wait_loaded(pe, e, j, i, par):
                own = j == 0 and e in SPARE
                pe.wait_ge(loaded(e, j, par), 16 * i + 16 if own else 32 * i + 16 * par + 16)

            def load_weights(sp, e, j, pair, par):
                w = MOE[k][j][bass.ds(2 * pair + e, 1), :, :].rearrange("o (c p) n -> p (o c) n", p=P)
                sp.dma_start(dst(e, j, par), w).then_inc(loaded(e, j, par), 16)

            def load_spared(sp, pair, it, par):
                if not isinstance(it, int):
                    sp.wait_ge(sem("gate_used" + n), it - 1)
                for e in SPARE:
                    load_weights(sp, e, 0, pair, par)

            def load_rest(sp, pair, it, par):
                for j in range(3):
                    for e in range(2):
                        if j or e not in SPARE:
                            sp.wait_ge(sem(("gate_used", "up_used", "down_used")[j] + n), it)
                            load_weights(sp, e, j, pair, par)

            with nc.Block() as block:
                @block.sync
                def _(sp):
                    if not ahead:
                        load_expert(sp, k, (0, 3, 1, 4, 2, 5))
                    if sides is not None:
                        sides(sp, 0)
                    load_spared(sp, 1, 1, 1)
                    with sp.Fori(1, NP // 2) as i:
                        for par in (1, 0):
                            it = 2 * i - par
                            load_spared(sp, it + 1, it + 1, 1 - par)
                            load_rest(sp, it, it, par)
                            if sides is not None:
                                sides(sp, it)
                    load_rest(sp, NP - 1, NP - 1, 1)
                    if sides is not None:
                        sides(sp, NP - 1)
                    rounds = sp.value_load(rounds_i[0:1, 0:1], min_val=1, max_val=ROUNDS)
                    with sp.If(rounds > 1):
                        with sp.Fori(1, rounds) as q:
                            with sp.Fori(0, NP // 2) as i:
                                for par in range(2):
                                    load_spared(sp, 2 * i + par, q * NP + 2 * i + par, par)
                                    load_rest(sp, 2 * i + par, q * NP + 2 * i + par, par)
                    sp.nop()
                    if afterwards is not None:
                        afterwards(sp)

                @block.tensor
                def _(pe):
                    rounds = pe.value_load(rounds_i[0:1, 0:1], min_val=1, max_val=ROUNDS)

                    def gather(half):
                        for c in range(4 * half, 4 * half + 4):
                            for t in range(NT):
                                last = pe.matmul((gate_ps, up_ps)[half][:, (c % 4) * P:(c % 4 + 1) * P],
                                                 xn3[:, t, c * P:(c + 1) * P], oh[:, t, :],
                                                 start=(t == 0), stop=(t == NT - 1))
                        last.then_inc(sem("gat_psum" + n), 1)

                    def project(j, bank, par):
                        for c in range(KC):
                            for e in range(2):
                                last = pe.matmul(bank[e * SLOTS:(e + 1) * SLOTS, :], xg[:, c, e * SLOTS:(e + 1) * SLOTS],
                                                 dst(e, j, par)[:, c, :], start=(c == 0), stop=(c == KC - 1))
                        return last

                    def down():
                        for h in range(2):
                            for f in range(FC):
                                for e in range(2):
                                    last = pe.matmul(out_ps[h][e * SLOTS:(e + 1) * SLOTS, :],
                                                     hidT[:, f, e * SLOTS:(e + 1) * SLOTS],
                                                     dst(e, 2, 0)[:, f, h * 512:(h + 1) * 512],
                                                     start=(f == 0), stop=(f == FC - 1))
                        last.then_inc(sem("down_used" + n), 1)

                    def scatter(stop):
                        for t in range(NT):
                            for h in range(2):
                                last = pe.matmul(y_ps[2 * t + h][:, :], pT[:, t * P:(t + 1) * P], outb[:, h * 512:(h + 1) * 512],
                                                 start=False, stop=stop, skip_group_check=True)
                            if stop:
                                last.then_inc(sem("y_done" + n), 1)

                    pe.wait_ge(sem("moe_zero" + n), 1)
                    for b in range(4):
                        pe.matmul(y_ps[b][:, :], zero[:, 0:P], zero, start=True, stop=False, skip_group_check=True)
                    pe.wait_ge(sem("oh_done" + n), 1)
                    gather(0)
                    gather(1)
                    with pe.Fori(0, rounds * (NP // 2)) as i:
                        for par in range(2):
                            it = 2 * i + par
                            pe.wait_ge(sem("gat_done" + n), 2 * it + 2)
                            for e in range(2):
                                wait_loaded(pe, e, 0, i, par)
                            project(0, gate_ps, par).then_inc(sem("gate_used" + n), 1)
                            pe.wait_ge(sem("out0_done" + n), it + 1)
                            pe.wait_ge(sem("out1_done" + n), it + 1)
                            pe.wait_ge(sem("pT_done" + n), it + 1)
                            scatter(False)
                            pe.wait_ge(sem("oh_done" + n), it + 1)
                            for t in range(NT):
                                last = pe.transpose(out_ps[1][:, t * P:(t + 1) * P], ohw[:, t, :], ident[:, :])
                            last.then_inc(sem("pT_psum" + n), 1)
                            for e in range(2):
                                wait_loaded(pe, e, 1, i, par)
                            project(1, up_ps, par).then_inc(sem("up_used" + n), 1)
                            pe.wait_ge(sem("hid_done" + n), it + 1)
                            for f in range(FC):
                                last = pe.transpose(out_ps[0][:, f * P:(f + 1) * P], hid[:, f * P:(f + 1) * P], ident[:, :])
                            last.then_inc(sem("hidT_psum" + n), 1)
                            pe.wait_ge(sem("oh_done" + n), it + 2)
                            gather(0)
                            gather(1)
                            pe.wait_ge(sem("pT_done" + n), it + 2)
                            pe.wait_ge(sem("hidT_done" + n), it + 1)
                            for e in range(2):
                                wait_loaded(pe, e, 2, i, par)
                            down()
                    pe.wait_ge(sem("out0_done" + n), rounds * NP + 1)
                    pe.wait_ge(sem("out1_done" + n), rounds * NP + 1)
                    scatter(True)

                @block.scalar
                def _(act):
                    rounds = act.value_load(rounds_i[0:1, 0:1], min_val=1, max_val=ROUNDS)

                    def take(half, count):
                        act.wait_ge(sem("gat_psum" + n), count)
                        for c in range(4 * half, 4 * half + 4):
                            last = act.activation(xg[:, c, :], (gate_ps, up_ps)[half][:, (c % 4) * P:(c % 4 + 1) * P],
                                                  ACT.Identity, scale=modc[:, 2 * KC + c:2 * KC + c + 1],
                                                  bias=modc[:, 3 * KC + c:3 * KC + c + 1])
                        last.then_inc(sem("gat_done" + n), 1)
                    take(0, 1)
                    take(1, 2)
                    with act.Fori(0, rounds * NP) as it:
                        act.wait_ge(sem("gate_used" + n), it + 1)
                        act.activation(hid, gate_ps[:, :], ACT.Sigmoid).then_inc(sem("sig_done" + n), 1)
                        take(0, 2 * it + 3)
                        take(1, 2 * it + 4)
                        act.wait_ge(sem("down_used" + n), it + 1)
                        act.activation(outb[:, 512:1024], out_ps[1][:, :], ACT.Copy).then_inc(sem("out1_done" + n), 1)
                    if k == 0:
                        load_sqrt(act, 1)

                @block.vector
                def _(v):
                    rounds = v.value_load(rounds_i[0:1, 0:1], min_val=1, max_val=ROUNDS)

                    def slots_of(col):
                        for e in range(2):
                            for t in range(NT):
                                if isinstance(col, int):
                                    p1, m1, g1 = [a[:, t, col + e:col + e + 1] for a in (pos, mask, gate)]
                                else:
                                    p1, m1, g1 = [a[:, t, bass.ds(col + e, 1)] for a in (pos, mask, gate)]
                                v.tensor_scalar(oh[:, t, e * SLOTS:(e + 1) * SLOTS], slot_ids[:, :], p1, m1,
                                                ALU.is_equal, ALU.mult)
                                last = v.tensor_scalar(ohw[:, t, e * SLOTS:(e + 1) * SLOTS], slot_ids[:, :], p1, g1,
                                                       ALU.is_equal, ALU.mult)
                        last.then_inc(sem("oh_done" + n), 1)

                    def body(it, side):
                        v.wait_ge(sem("sig_done" + n), it + 1)
                        v.tensor_tensor(hid, gate_ps[:, :], hid, ALU.mult).then_inc(sem("silu" + n), 1)
                        v.wait_ge(sem("pT_psum" + n), it + 1)
                        v.tensor_copy(pT, out_ps[1][:, 0:256]).then_inc(sem("pT_done" + n), 1)
                        slots_of(2 * it + 2)
                        v.wait_ge(sem("silu" + n), it + 1)
                        v.wait_ge(sem("up_used" + n), it + 1)
                        v.tensor_tensor(hid, up_ps[:, :], hid, ALU.mult).then_inc(sem("hid_done" + n), 1)
                        v.wait_ge(sem("hidT_psum" + n), it + 1)
                        v.tensor_copy(hidT, out_ps[0][:, :].rearrange("p (f n) -> p f n", f=FC)).then_inc(
                            sem("hidT_done" + n), 1)
                        if side is not None:
                            side(v, it)
                        v.wait_ge(sem("down_used" + n), it + 1)
                        v.tensor_copy(outb[:, 0:512], out_ps[0][:, :]).then_inc(sem("out0_done" + n), 1)

                    v.memset(zero, 0.0).then_inc(sem("moe_zero" + n), 1)
                    slots_of(0)
                    v.memset(pT, 0.0).then_inc(sem("pT_done" + n), 1)
                    v.memset(outb[:, 0:512], 0.0).then_inc(sem("out0_done" + n), 1)
                    v.memset(outb[:, 512:1024], 0.0).then_inc(sem("out1_done" + n), 1)
                    if sides is None:
                        with v.Fori(0, rounds * NP) as it:
                            body(it, None)
                    else:
                        with v.Fori(0, NP) as it:
                            body(it, sides)
                        with v.If(rounds > 1):
                            with v.Fori(NP, rounds * NP) as it:
                                body(it, None)
                        v.nop()
                    def y_of(g):
                        return tmp[:, 2304 + g * 512:2304 + (g + 1) * 512] if g < 3 else tmp[:, 0:512]

                    for g in range(5):
                        if g < 4:
                            t, h = g // 2, g % 2
                            v.wait_ge(sem("y_done" + n), t + 1)
                            v.tensor_tensor(y_of(g), y_ps[g][:, :], g_b[:, 1, h * 512:(h + 1) * 512], ALU.mult).then_inc(
                                sem("gy" + n), 1)
                        if g:
                            t, h = (g - 1) // 2, (g - 1) % 2
                            v.wait_ge(sem("gy" + n), g)
                            xs = x3[:, t, h * 512:(h + 1) * 512]
                            v.tensor_tensor(xs, xs, y_of(g - 1), ALU.add).then_inc(sem("x_new" + n), 1)

        def ada2_side(eng, it):
            n2 = ADA2_PER_PAIR
            for j in range(n2):
                ws = ada2_slot(j)
                before_ = len([i for i in range(ADA2_AHEAD) if i % 5 == j])
                first_col = ADA2_AHEAD * AW + j * AW + (it * n2 * AW if isinstance(it, int) else 0)
                if eng is nc.sync:
                    cols = (slice(first_col, first_col + AW) if isinstance(it, int) else
                            bass.ds(it * (n2 * AW) + first_col, AW))
                    eng.wait_ge(sem(f"ada2_used{j}"), it + before_)
                    eng.dma_start(ws, inp["ada_w_2"][0][:, cols].rearrange("(c p) n -> p c n", p=P)).then_inc(
                        sem(f"ada2_loaded{j}"), 16)
                else:
                    a = acc[:, bass.ds(it * (n2 * AW) + first_col, AW)]
                    eng.wait_ge(sem(f"ada2_loaded{j}"), 16 * it + 16 * (before_ + 1))
                    for c in range(KC):
                        s = cond[:, KC + c:KC + c + 1]
                        if c == 0:
                            ins = eng.tensor_scalar(a, ws[:, c, :], s, None, ALU.mult)
                        else:
                            ins = eng.scalar_tensor_tensor(a, ws[:, c, :], s, a, ALU.mult, ALU.add)
                        if c < KC - 1:
                            ins.then_inc(sem("ada2_chain"), 1)
                            eng.wait_ge(sem("ada2_chain"), it * (n2 * (KC - 1)) + j * (KC - 1) + c + 1)
                        else:
                            ins.then_inc(sem(f"ada2_used{j}"), 1)

        route(0, 16, True)
        experts(0, 16, sides=ada2_side,
                afterwards=lambda sp: sp.dma_start(
                    g_b[:, 0, :], inp["norm_final"].rearrange("(a n) -> a n", a=1).broadcast_to((P, D))).then_inc(
                        sem("nf_loaded"), 16))

        give_back()
        w_in = inp["w_in_2"][0]
        MIX_CELLS = 4
        SH0 = 1064
        GA0 = SH0 + 1824
        pieces = [(0, 512), (512, 1024), (SH0, SH0 + 512), (SH0 + 512, SH0 + 1024), (SH0 + 1024, SH0 + 1536),
                  (SH0 + 1536, GA0)]
        LORA, GATE0 = 6, 7

        def p2_load(sp, i, dst, src):
            sp.dma_start(dst, src).then_inc(sem(f"p2_loaded{i % MIX_CELLS}"), 16)

        SHIFT_NOW = 5
        SHIFT_BANKS = [m % 4 for m in range(SHIFT_NOW)] + [7, 4, 7, 5, 6, 4, 7, 7, 7, 7]
        LATE_SHIFT = 11

        def shifted_product(pe, m, halves=(0, 1)):
            i = 2 + m // 4 if m < 12 else 5
            o = (m % 4) * P if m < 12 else (m - 12) * P
            n = 32 if m == 14 else P
            if o == 0 and 0 in halves:
                p2_ready(pe, i)
            before_ = [x for x in range(m) if SHIFT_BANKS[x] == SHIFT_BANKS[m]]
            if before_:
                pe.wait_ge(sem("mixed_done"), before_[-1] + 1)
            for c in range(4 * halves[0], 4 * halves[-1] + 4):
                last = pe.matmul(ps[SHIFT_BANKS[m]][0:n, 0:S], p2(i)[:, c, o:o + n], hT[:, c, :], start=(c == 0), stop=(c == KC - 1))
            if 1 in halves:
                last.then_inc(sem("pj_shift"), 1)

        def shifted_own(act, m):
            n = 32 if m == 14 else P
            act.wait_ge(sem("pj_shift"), m + 1)
            act.activation(mixed[0:n, m, :], ps[SHIFT_BANKS[m]][0:n, 0:S], ACT.Copy, scale=omm[0:n, m:m + 1]).then_inc(
                sem("mixed_own"), 1)

        def shifted_before(v, m):
            n = 32 if m == 14 else P
            v.wait_ge(sem("mixed_own"), m + 1)
            a = mixed[0:n, m, 1:S]
            v.scalar_tensor_tensor(a, ps[SHIFT_BANKS[m]][0:n, 0:S - 1], colsB[0:n, MU0 + m:MU0 + m + 1], a,
                                   ALU.mult, ALU.add).then_inc(sem("mixed_done"), 1)

        p2_loads = {}
        count = [0] * MIX_CELLS
        for i in range(GATE0 + 4):
            count[i % MIX_CELLS] += 4 if i == LORA else 1
            p2_loads[i] = 16 * count[i % MIX_CELLS]

        def p2_ready(pe, i):
            pe.wait_ge(sem(f"p2_loaded{i % MIX_CELLS}"), p2_loads[i])

        def p2(i, kc=8, w=512):
            return cell(i % MIX_CELLS, kc, w)

        q_tok = tmp[:, 0:1024].rearrange("p (t d) -> p t d", t=NT)
        kvl = tmp[:, 1024:1536].rearrange("p (t d) -> p t d", t=NT)
        qiT = tmp[:, 1536:2048].rearrange("p (c s) -> p c s", c=2)
        kiT = tmp[:, 2048:2304]
        wi_w = tmp[:, 3008:3072].rearrange("p (c n) -> p c n", c=KC)
        krep = tmp[:, 3072:4096].rearrange("p (c n) -> p c n", c=KC)
        w_idx = small[:, 24:40]
        omm = small[:, 40:55]
        mixed = ring[:, 4 * CELL:4 * CELL + 15 * S].rearrange("p (c s) -> p c s", c=15)
        lora = p2(LORA, 1, 4096)[:, 0, :]
        kv_up = cell(5)[:, 0:4, :].rearrange("p (c m) n -> p c (m n)", c=2)
        M_STRICT, M_INCL = pos_t[:, 0:P], pos_t[:, P:2 * P]
        M_16, M_OFF = mask_t[:, 0:P], mask_t[:, P:2 * P]
        M_16L = gate_t[:, 0:P]
        chunk_of = gate_t[:, P:P + 4]

        with nc.Block() as block:
            @block.sync
            def _(sp):
                for i in range(4):
                    p2_load(sp, i, p2(i), w_cols(w_in, *pieces[i]))
                for i, m in enumerate((2, 5)):
                    sp.dma_start(side[:, i * D:(i + 1) * D], inp["ada_b_2"][0:1, m * D:(m + 1) * D].broadcast_to((P, D))).then_inc(
                        sem("gb2_loaded"), 16)
                for r in range(4):
                    sp.dma_start(krep[:, :, r * 32:(r + 1) * 32], w_cols(w_in, 1024, 1056)).then_inc(sem("ki_loaded"), 16)
                sp.dma_start(wi_w, w_cols(w_in, 1056, 1064)).then_inc(sem("ki_loaded"), 16)
                sp.dma_start(kv_up, inp["w_kv_up_2"][0].rearrange("(c p) n -> p c n", p=P)).then_inc(sem("kv_up_loaded"), 16)
                sp.wait_ge(sem("pj_q"), 2)
                p2_load(sp, 4, p2(4), w_cols(w_in, *pieces[4]))
                sp.wait_ge(sem("pj_qi"), 1)
                p2_load(sp, 5, p2(5)[:, :, 0:288], w_cols(w_in, *pieces[5]))
                sp.wait_ge(sem("pj_shift"), 4)
                sp.wait_ge(sem("lora_zero"), 1)
                p2_load(sp, LORA, lora[0:64, 0:512], inp["rwkv_w2_2"][0])
                p2_load(sp, LORA, lora[64:128, 0:512], inp["rwkv_a2_2"][0])
                p2_load(sp, LORA, lora[:, 512:1024], inp["rwkv_g2_2"][0][0:128, :])
                p2_load(sp, LORA, lora[0:32, 1024:1536], inp["rwkv_g2_2"][0][128:160, :])

            @block.gpsimd
            def _(pool):
                pool.memset(mixed[:, 14, :], 0.0).then_inc(sem("mixed_zero"), 1)
                pool.wait_ge(sem("mixed_zero"), 1)
                for m in (M_STRICT, M_INCL, M_16, M_OFF, M_16L, chunk_of):
                    p_step(pool.memset(m, 0.0 if m is M_OFF else 1.0))

                def block_mask(m, size, upper, strict):
                    v3_ = m.rearrange("p (b n) -> p b n", n=size)
                    s_ = 1 if upper else -1
                    p_step(pool.affine_select(out=v3_, in_=v3_, compare_op=ALU.is_gt if strict else ALU.is_ge, fill=0.0,
                                              base=0, pattern=[[s_ * size, P // size], [s_, size]], channel_multiplier=-s_))
                    p_step(pool.affine_select(out=v3_, in_=v3_, compare_op=ALU.is_ge, fill=0.0, base=0,
                                              pattern=[[-size, P // size], [0, size]], channel_multiplier=1))
                    p_step(pool.affine_select(out=v3_, in_=v3_, compare_op=ALU.is_gt, fill=0.0, base=size,
                                              pattern=[[size, P // size], [0, size]], channel_multiplier=-1))
                block_mask(M_STRICT, 32, True, True)
                block_mask(M_INCL, 32, True, False)
                block_mask(M_16, 16, True, True)
                block_mask(M_16L, 16, False, True)
                p_step(pool.tensor_tensor(M_OFF, M_STRICT, M_16, ALU.subtract))
                p_step(pool.affine_select(out=chunk_of, in_=chunk_of, compare_op=ALU.is_ge, fill=0.0, base=0,
                                          pattern=[[-32, 4]], channel_multiplier=1))
                p_step(pool.affine_select(out=chunk_of, in_=chunk_of, compare_op=ALU.is_gt, fill=0.0, base=32,
                                          pattern=[[32, 4]], channel_multiplier=-1))
                pool.wait_ge(sem("pj_shift"), 4)
                pool.memset(lora[:, 1024:1536], 0.0).then_inc(sem("lora_zero"), 1)

            @block.tensor
            def _(pe):
                ada_columns(pe, (3, 4), 2, "modc_psum")
                hT_tensor(pe, 2)
                hT_wait(pe, 2)
                for t in range(NT):
                    if t == 0:
                        p2_ready(pe, 0)
                    for c in range(KC):
                        last = pe.matmul(ps[t][:, :], hT[:, c, t * P:(t + 1) * P], p2(0)[:, c, :], start=(c == 0), stop=(c == KC - 1))
                    last.then_inc(sem("pj_q"), 1)
                p2_ready(pe, 1)
                pe.wait_ge(sem("modc_ready"), 4)
                for t in range(NT):
                    for c in range(KC):
                        last = pe.matmul(ps[2][:, t * S:(t + 1) * S], hT[:, c, t * P:(t + 1) * P], p2(1)[:, c, 0:S],
                                         start=(c == 0), stop=(c == KC - 1))
                last.then_inc(sem("pj_kv"), 1)
                for j in range(2):
                    for c in range(KC):
                        last = pe.matmul(ps[3][:, j * S:(j + 1) * S], p2(1)[:, c, S + j * P:S + (j + 1) * P], hT[:, c, :],
                                         start=(c == 0), stop=(c == KC - 1))
                last.then_inc(sem("pj_qi"), 1)
                pe.wait_ge(sem("ki_loaded"), 80)
                for c in range(KC):
                    last = pe.matmul(ps[4][:, 0:S], krep[:, c, :], hT[:, c, :], start=(c == 0), stop=(c == KC - 1))
                for t in range(NT):
                    for c in range(KC):
                        last = pe.matmul(ps[4][:, S + t * 8:S + (t + 1) * 8], hT[:, c, t * P:(t + 1) * P], wi_w[:, c, :],
                                         start=(c == 0), stop=(c == KC - 1))
                last.then_inc(sem("pj_ki"), 1)
                pe.wait_ge(sem("pj_q_out"), 2)
                ada_rows(pe, 2, 0, "g_psum")
                pe.wait_ge(sem("g_out"), 3)
                ada_rows(pe, 5, 0, "g_psum")
                pe.wait_ge(sem("g_out"), 4)
                pe.wait_ge(sem("pj_kv_out"), 1)
                pe.wait_ge(sem("pj_qi_out"), 1)
                for m in range(SHIFT_NOW):
                    shifted_product(pe, m)

            @block.scalar
            def _(act):
                rms_scalar(act, 2, xn_sb, ("x_new0", 2, 4))
                rms_scalar(act, 3, xn_sb, ("x_ready", 1, 1))
                hT_scalar(act, 2)
                for t in range(NT):
                    act.wait_ge(sem("pj_q"), t + 1)
                    act.activation(q_tok[:, t, :], ps[t][:, :], ACT.Copy).then_inc(sem("pj_q_out"), 1)
                act.wait_ge(sem("pj_kv"), 1)
                act.activation(tmp[:, 1024:1536], ps[2][:, :], ACT.Copy).then_inc(sem("pj_kv_out"), 1)
                act.wait_ge(sem("pj_qi"), 1)
                act.activation(tmp[:, 1536:2048], ps[3][:, :], ACT.Copy).then_inc(sem("pj_qi_out"), 1)
                act.wait_ge(sem("pj_ki"), 1)
                act.activation(kiT, ps[4][:, 0:S], ACT.Copy).then_inc(sem("pj_ki_out"), 1)
                act.activation(w_idx, ps[4][:, S:S + 16], ACT.Copy, scale=1.0 / 16.0).then_inc(sem("pj_ki_out"), 1)
                act.wait_ge(sem("omm"), 1)
                act.wait_ge(sem("mixed_zero"), 1)
                for m in range(SHIFT_NOW):
                    shifted_own(act, m)

            @block.vector
            def _(v):
                v.wait_ge(sem("nf_loaded"), 16)
                rms_vector(v, 2, x3, weight=g_b[:, 0, :], name="x_ready")
                rms_vector(v, 3, xn3)
                hT_vector(v, 2)
                v.wait_ge(sem("modc_psum"), FIRST_COLS + 3)
                fill_modc(v, 4, 2 * KC, 3 * KC, ps[2], 0, KC, colA("moe_norm_g_2", 0, KC), colB("ada_b_2", 3 * KC, KC),
                          colB("ada_b_2", 4 * KC, KC))
                v.tensor_scalar(omm, colsB[:, MU0:MU0 + 15], -1.0, 1.0, ALU.mult, ALU.add).then_inc(sem("omm"), 1)
                v.wait_ge(sem("gb2_loaded"), 32)
                for i in range(2):
                    v.wait_ge(sem("g_psum"), i + 3)
                    for n in range(2):
                        a = g_b[:, i, n * 512:(n + 1) * 512]
                        ins = v.tensor_tensor(a, ps[n][:, :], side[:, i * D + n * 512:i * D + (n + 1) * 512], ALU.add)
                    ins.then_inc(sem("g_out"), 1)
                for m in range(SHIFT_NOW):
                    shifted_before(v, m)

        give_back()
        k_tok = side[:, 0:1024].rearrange("p (t d) -> p t d", t=NT)
        vv_tok = side[:, 1024:2048].rearrange("p (t d) -> p t d", t=NT)
        qT2 = side[:, 2048:3072].rearrange("p (c s) -> p c s", c=4)
        kT2 = side[:, 3072:4096].rearrange("p (c s) -> p c s", c=4)
        latT = side[:, 4096:4608].rearrange("p (c s) -> p c s", c=2)
        work = side[:, 4608:5120].rearrange("p (t s) -> p t s", t=NT)
        drop = side[:, 5120:5632].rearrange("p (t s) -> p t s", t=NT)
        dst2 = side[:, 5632:6144].rearrange("p (t s) -> p t s", t=NT)
        o_tok = side[:, 6144:7168].rearrange("p (t d) -> p t d", t=NT)
        oaT = side[:, 7168:8192].rearrange("p (c s) -> p c s", c=4)
        sq6 = acc[:, 0:1024]
        rl = acc[:, 1024:2048].rearrange("p (b s) -> p b s", b=4)
        lg = acc[:, 0:768].rearrange("p (b s) -> p b s", b=3)
        ee = acc[:, 2560:3072].rearrange("p (b s) -> p b s", b=2)
        eT = acc[:, 3072:3584].rearrange("p (b s) -> p b s", b=2)
        st6 = acc[:, 3584:3840]

        def unit(u):
            return 2 * (u // 4) + u % 2, u // 2 % NT

        TAKEN = -3.3e38
        TOPK = 64

        def load_gates(sp, i):
            p2_load(sp, GATE0 + i, p2(GATE0 + i), w_cols(w_in, GA0 + i * 512, GA0 + (i + 1) * 512))

        gates_sb = p2(GATE0).rearrange("p (k t) (w n) -> p w k t n", t=NT, w=4)

        with nc.Block() as block:
            @block.sync
            def _(sp):
                sp.wait_ge(sem("pj_shift"), 8)
                load_gates(sp, 0)
                sp.wait_ge(sem("pj_shift"), 12)
                load_gates(sp, 1)
                sp.wait_ge(sem("pj_shift"), 15)
                load_gates(sp, 2)

            @block.gpsimd
            def _(pool):
                pool.iota(dst2, pattern=[[P, NT], [-1, S]], base=0, channel_multiplier=1,
                          allow_small_or_imprecise_dtypes=True).then_inc(sem("dst2"), 1)
                for t in range(NT):
                    pool.wait_ge(sem("idx_score"), t + 1)
                    pool.affine_select(out=work[:, t, :], in_=work[:, t, :], compare_op=ALU.is_ge, fill=-BIG, base=t * P,
                                       pattern=[[-1, S]], channel_multiplier=1).then_inc(sem("idx_causal"), 1)
                pool.wait_ge(sem("drop_raw"), 1)
                for t in range(NT):
                    pool.affine_select(out=drop[:, t, :], in_=drop[:, t, :], compare_op=ALU.is_ge, fill=-1.0, base=t * P,
                                       pattern=[[-1, S]], channel_multiplier=1).then_inc(sem("drop"), 1)

            @block.tensor
            def _(pe):
                def dots(u):
                    t, h = u // 8, u % 8
                    r = 32 * (h % 4)
                    if u >= 4:
                        pe.wait_ge(sem("idx_relu"), u - 3)
                    pe.matmul(ps[h % 4][:, 0:S], qiT[r:r + 32, h // 4, t * P:(t + 1) * P], kiT[r:r + 32, :],
                              start=True, stop=True).then_inc(sem("idx_dots"), 1)
                for u in range(4):
                    dots(u)
                shifted_product(pe, SHIFT_NOW)
                pe.wait_ge(sem("lat_normed"), 1)
                for c in range(2):
                    for t in range(NT):
                        last = pe.transpose(ps[4][:, c * S + t * P:c * S + (t + 1) * P], kvl[:, t, c * P:(c + 1) * P], ident[:, :])
                last.then_inc(sem("lat_psum"), 1)
                pe.wait_ge(sem("q_normed"), 1)
                for c in range(4):
                    for t in range(NT):
                        last = pe.transpose(ps[5 + c // 2][:, (c % 2) * S + t * P:(c % 2) * S + (t + 1) * P],
                                            q_tok[:, t, c * P:(c + 1) * P], ident[:, :])
                last.then_inc(sem("q_psum"), 1)
                for u in range(4, 8):
                    dots(u)
                pe.wait_ge(sem("kv_up_loaded"), 16)
                pe.wait_ge(sem("mixed_done"), SHIFT_NOW + 1)
                pe.wait_ge(sem("latT_done"), 2)
                for n in range(2):
                    for t in range(NT):
                        if n == 0 and t == 1:
                            pe.wait_ge(sem("latT_done"), 2)
                        if n == 1:
                            pe.wait_ge(sem("kv_out"), t + 1)
                            if t == 0:
                                pe.wait_ge(sem("qT_done"), 4)
                        b = ps[7] if (t == 0) else ps[4]
                        for c in range(2):
                            last = pe.matmul(b[:, :], latT[:, c, t * P:(t + 1) * P], kv_up[:, c, n * 512:(n + 1) * 512],
                                             start=(c == 0), stop=(c == 1))
                        last.then_inc(sem("kv_psum"), 1)
                for u in range(8, 16):
                    dots(u)
                pe.wait_ge(sem("k_normed"), 1)
                for c in range(4):
                    for t in range(NT):
                        last = pe.transpose(ps[5 + c // 2][:, (c % 2) * S + t * P:(c % 2) * S + (t + 1) * P],
                                            k_tok[:, t, c * P:(c + 1) * P], ident[:, :])
                last.then_inc(sem("k_psum"), 1)

                def scores(u):
                    h, t = unit(u)
                    jo = (h % 2) * 64
                    if u == 0:
                        pe.wait_ge(sem("kT_done"), 4)
                        pe.wait_ge(sem("idx_relu"), 16)
                    if u >= 4:
                        pe.wait_ge(sem("sa_biased"), u - 3)
                    pe.matmul(ps[u % 4][:, 0:S], qT2[jo:jo + 64, h // 2, t * P:(t + 1) * P], kT2[jo:jo + 64, h // 2, :],
                              start=True, stop=True).then_inc(sem("sa_scores"), 1)

                def turn(u):
                    pe.wait_ge(sem("sa_exp"), u + 1)
                    if u >= 2:
                        pe.wait_ge(sem("sa_eT"), u - 1)
                    if u == 0:
                        pe.wait_ge(sem("kv_out"), 4)
                    for k in range(2):
                        last = pe.transpose(ps[4 + u % 2][:, k * P:(k + 1) * P], ee[:, u % 2, k * P:(k + 1) * P], ident[:, :])
                    last.then_inc(sem("sa_eT_psum"), 1)

                def av(u):
                    h = unit(u)[0]
                    pe.wait_ge(sem("sa_eT"), u + 1)
                    if u:
                        pe.wait_ge(sem("sa_o"), u)
                    for k in range(2):
                        last = pe.matmul(ps[6][:, 0:64], eT[:, u % 2, k * P:(k + 1) * P],
                                         vv_tok[:, k, h * 64:(h + 1) * 64], start=(k == 0), stop=(k == 1))
                    last.then_inc(sem("sa_av"), 1)
                for u in range(4):
                    scores(u)
                pe.wait_ge(sem("kv_out"), 4)
                for m in range(SHIFT_NOW + 1, LATE_SHIFT):
                    shifted_product(pe, m)
                pe.wait_ge(sem("mixed_done"), LATE_SHIFT)
                for u in range(17):
                    if u % 2 and u + 4 < 16:
                        scores(u + 3)
                        scores(u + 4)
                    if u < 16:
                        turn(u)
                    if u >= 1:
                        av(u - 1)
                    if u % 4 in (1, 2) and u < 16:
                        shifted_product(pe, LATE_SHIFT + u // 4, (u % 4 - 1,))
                pe.wait_ge(sem("sa_o"), 16)
                pe.wait_ge(sem("sa_eT"), 16)
                for c in range(4):
                    for t in range(NT):
                        last = pe.transpose(ps[4 + c // 2][:, (c % 2) * S + t * P:(c % 2) * S + (t + 1) * P],
                                            o_tok[:, t, c * P:(c + 1) * P], ident[:, :])
                last.then_inc(sem("oa_psum"), 1)

            @block.scalar
            def _(act):
                for t in range(NT):
                    act.activation(sq6[:, t * S:(t + 1) * S], kvl[:, t, :], ACT.Square,
                                   accum_out=st6[:, t:t + 1]).then_inc(sem("lat_sq"), 1)
                act.wait_ge(sem("lat_ms"), 1)
                act.activation(st6[:, 4:6], st6[:, 2:4], ACT.Sqrt).then_inc(sem("lat_root"), 1)
                act.activation(acc[:, 4096:5120], tmp[:, 0:1024], ACT.Square).then_inc(sem("q_sq"), 1)
                act.wait_ge(sem("q_ms"), 1)
                act.activation(st6[:, 32:48], st6[:, 16:32], ACT.Sqrt).then_inc(sem("q_root"), 1)

                def relu(u):
                    act.wait_ge(sem("idx_dots"), u + 1)
                    if u >= 4:
                        act.wait_ge(sem("idx_added"), u - 3)
                    act.activation(rl[:, u % 4, :], ps[u % 4][:, 0:S], ACT.Relu).then_inc(sem("idx_relu"), 1)
                shifted_own(act, SHIFT_NOW)
                for u in range(8):
                    relu(u)
                for i in range(4):
                    n, t = i // 2, i % 2
                    act.wait_ge(sem("kv_psum"), i + 1)
                    act.activation((k_tok, vv_tok)[n][:, t, :], (ps[7] if t == 0 else ps[4])[:, :], ACT.Copy).then_inc(
                        sem("kv_out"), 1)
                act.wait_ge(sem("kv_out"), 2)
                act.activation(sq6, side[:, 0:1024], ACT.Square).then_inc(sem("k_sq"), 1)
                act.wait_ge(sem("k_ms"), 1)
                act.activation(st6[:, 64:80], st6[:, 48:64], ACT.Sqrt).then_inc(sem("k_root"), 1)
                for u in range(8, 16):
                    relu(u)
                for m in range(SHIFT_NOW + 1, LATE_SHIFT):
                    shifted_own(act, m)
                for u in range(17):
                    if u < 16:
                        act.wait_ge(sem("sa_max"), u + 1)
                        if u >= 2:
                            act.wait_ge(sem("sa_eT_psum"), u - 1)
                        act.activation(ee[:, u % 2, :], lg[:, u % 3, :], ACT.Exp, bias=st6[:, 96 + u:97 + u],
                                       accum_out=st6[:, 112 + u:113 + u]).then_inc(sem("sa_exp"), 1)
                    if u >= 1:
                        act.wait_ge(sem("sa_eT_psum"), u)
                        if u >= 3:
                            act.wait_ge(sem("sa_av"), u - 2)
                        act.activation(eT[:, (u - 1) % 2, :], ps[4 + (u - 1) % 2][:, 0:S], ACT.Copy).then_inc(sem("sa_eT"), 1)
                    if u % 4 == 3:
                        shifted_own(act, LATE_SHIFT + u // 4)

            @block.vector
            def _(v):
                v_step(v.tensor_scalar(qk_cols[:, 1:2], colsB[:, nB:nB + 1], 0.125, None, ALU.mult))
                v.wait_ge(sem("lat_sq"), 2)
                v.tensor_scalar(st6[:, 2:4], st6[:, 0:2], 1.0 / S, EPS, ALU.mult, ALU.add).then_inc(sem("lat_ms"), 1)
                v.wait_ge(sem("lat_root"), 1)
                v_step(v.reciprocal(st6[:, 6:8], st6[:, 4:6]))
                v.tensor_tensor(kvl, kvl, st6[:, 6:8].unsqueeze(2).broadcast_to((P, NT, S)), ALU.mult).then_inc(sem("lat_normed"), 1)

                def head_norm(sq, st, sq_sem, ms_sem, root_sem, a, done):
                    v.wait_ge(sem(sq_sem), 1)
                    v_step(v.tensor_reduce(st6[:, st:st + 16], sq.rearrange("p (g d) -> p g d", d=64), X, ALU.add))
                    v.tensor_scalar(st6[:, st:st + 16], st6[:, st:st + 16], 1.0 / 64, EPS, ALU.mult, ALU.add).then_inc(sem(ms_sem), 1)
                    v.wait_ge(sem(root_sem), 1)
                    v_step(v.reciprocal(st6[:, st:st + 16], st6[:, st + 16:st + 32]))
                    g = a.rearrange("p (g d) -> p g d", d=64)
                    v.tensor_tensor(g, g, st6[:, st:st + 16].unsqueeze(2).broadcast_to((P, 16, 64)), ALU.mult).then_inc(sem(done), 1)
                head_norm(acc[:, 4096:5120], 16, "q_sq", "q_ms", "q_root", tmp[:, 0:1024], "q_normed")
                shifted_before(v, SHIFT_NOW)
                v.wait_ge(sem("lat_psum"), 1)
                for c in range(2):
                    v.tensor_scalar(latT[:, c, :], ps[4][:, c * S:(c + 1) * S], colB("kv_norm_g_2", c), None, ALU.mult).then_inc(
                        sem("latT_done"), 1)
                v.wait_ge(sem("q_psum"), 1)
                for c in range(4):
                    v.tensor_scalar(qT2[:, c, :], ps[5 + c // 2][:, (c % 2) * S:(c % 2 + 1) * S], qk_cols[:, 1:2], None,
                                    ALU.mult).then_inc(sem("qT_done"), 1)

                def add_head(u):
                    t, h = u // 8, u % 8
                    v.wait_ge(sem("idx_relu"), u + 1)
                    w = w_idx[:, t * 8 + h:t * 8 + h + 1]
                    if h == 0:
                        ins = v.tensor_scalar(work[:, t, :], rl[:, u % 4, :], w, None, ALU.mult)
                    else:
                        ins = v.scalar_tensor_tensor(work[:, t, :], rl[:, u % 4, :], w, work[:, t, :], ALU.mult, ALU.add)
                    ins.then_inc(sem("idx_added"), 1)
                    v.wait_ge(sem("idx_added"), u + 1)
                    if h == 7:
                        v.tensor_copy(st6[:, 200 + t:201 + t], work[:, t, 0:1]).then_inc(sem("idx_score"), 1)
                for u in range(8):
                    add_head(u)
                head_norm(sq6, 48, "k_sq", "k_ms", "k_root", side[:, 0:1024], "k_normed")
                for u in range(8, 16):
                    add_head(u)
                v.wait_ge(sem("k_psum"), 1)
                for c in range(4):
                    v.tensor_scalar(kT2[:, c, :], ps[5 + c // 2][:, (c % 2) * S:(c % 2 + 1) * S], colsB[:, nB + 1:nB + 2], None,
                                    ALU.mult).then_inc(sem("kT_done"), 1)
                for r in range(TOPK // 8):
                    for t in range(NT):
                        if r == 0:
                            v.wait_ge(sem("idx_causal"), t + 1)
                        top = st6[:, 160 + 8 * t:168 + 8 * t]
                        v_step(v.max(top, work[:, t, :]))
                        v_step(v.match_replace(work[:, t, :], top, work[:, t, :], TAKEN))
                    if r in (3, 4, 6, 7):
                        shifted_before(v, {3: 6, 4: 7, 6: 8, 7: 9}[r])
                shifted_before(v, 10)
                v.tensor_scalar(drop, work, TAKEN, 1.0, ALU.is_equal, ALU.subtract).then_inc(sem("drop_raw"), 1)
                v.wait_ge(sem("dst2"), 1)
                v.wait_ge(sem("drop"), 2)
                v_step(v.scalar_tensor_tensor(dst2, drop, -1.0e32, dst2, ALU.mult, ALU.add))

                def first(u):
                    h, t = unit(u)
                    b = lg[:, u % 3, :]
                    v.wait_ge(sem("sa_scores"), u + 1)
                    if u >= 3:
                        v.wait_ge(sem("sa_exp"), u - 2)
                    v.scalar_tensor_tensor(b, dst2[:, t, :], -2.0 ** -(h + 1), ps[u % 4][:, 0:S], ALU.mult, ALU.add).then_inc(
                        sem("sa_biased"), 1)
                    v.wait_ge(sem("sa_biased"), u + 1)
                    v_step(v.tensor_reduce(st6[:, 208 + u % 2:209 + u % 2], b, X, ALU.max))
                    v.tensor_scalar(st6[:, 96 + u:97 + u], st6[:, 208 + u % 2:209 + u % 2], -1.0, None, ALU.mult).then_inc(
                        sem("sa_max"), 1)

                def last_(u):
                    h, t = unit(u)
                    v.wait_ge(sem("sa_av"), u + 1)
                    v_step(v.reciprocal(st6[:, 128 + u:129 + u], st6[:, 112 + u:113 + u]))
                    v.tensor_scalar(o_tok[:, t, h * 64:(h + 1) * 64], ps[6][:, 0:64], st6[:, 128 + u:129 + u], None,
                                    ALU.mult).then_inc(sem("sa_o"), 1)
                first(0)
                first(1)
                for u in range(17):
                    if u + 2 < 16:
                        first(u + 2)
                    if u >= 1:
                        last_(u - 1)
                    if u % 4 == 3:
                        shifted_before(v, LATE_SHIFT + u // 4)
                v.wait_ge(sem("oa_psum"), 1)
                for c in range(4):
                    v.tensor_copy(oaT[:, c, :], ps[4 + c // 2][:, (c % 2) * S:(c % 2 + 1) * S])

        C = 32
        NC = S // C
        r_, k_, v_ = [mixed[:, 4 * i:4 * i + 4, :] for i in range(3)]
        c5 = 5 * CELL

        def ch4(a):
            return a.rearrange("p (c s) -> p c s", c=4)
        aa, LL, kk, gg = [ring[:, c5 + i * 1024:c5 + (i + 1) * 1024] for i in range(4)]
        eP, ePrev, eN, bonus, t1, t2_ = [acc[:, i * 1024:(i + 1) * 1024] for i in range(6)]
        tl = tmp[:, :].rearrange("p (w c s) -> p w c s", w=4, c=4)
        rT_, aT_, kT_, bT_ = [tmp[:, i * 1024:(i + 1) * 1024] for i in range(4)]
        toks = side[:, 0:4096].rearrange("p (w t d) -> p w t d", w=4, t=NT)
        v_tk, k_tk, b_tk, a_tk = [toks[:, i, :, :] for i in range(4)]
        tw = side[:, 4096:4352]
        sgl = side[:, 4352:4864].rearrange("p (c s) -> p c s", c=2)
        omka = small[:, 56:60]
        wC = colsB[:, NB_ALL:NB_ALL + 32].rearrange("p (c n) -> p c n", c=4)
        assert NB_ALL + 32 <= P
        EXPM = math.exp(-0.5)

        with nc.Block() as block:
            @block.gpsimd
            def _(pool):
                p_step(pool.memset(t1, 1.0))
                pool.memset(t1.rearrange("p (n c) -> p n c", c=C)[:, :, 0:1], 0.0).then_inc(sem("scan_mask"), 1)

            @block.tensor
            def _(pe):
                p2_ready(pe, LORA)
                pe.wait_ge(sem("tanh"), 1)
                for c in range(4):
                    last = pe.matmul(ps[c // 2][:, (c % 2) * S:(c % 2 + 1) * S], lora[0:64, c * P:(c + 1) * P], tw[0:64, :],
                                     start=True, stop=True)
                last.then_inc(sem("w_psum"), 1)
                for c in range(4):
                    last = pe.matmul(ps[2 + c // 2][:, (c % 2) * S:(c % 2 + 1) * S], lora[64:128, c * P:(c + 1) * P],
                                     mixed[64:128, 12, :], start=True, stop=True)
                last.then_inc(sem("a_psum"), 1)
                pe.wait_ge(sem("sgl"), 1)
                for c in range(4):
                    for k in range(2):
                        last = pe.matmul(ps[4 + c // 2][:, (c % 2) * S:(c % 2 + 1) * S],
                                         lora[:, 512 * (k + 1) + c * P:512 * (k + 1) + (c + 1) * P], sgl[:, k, :],
                                         start=(k == 0), stop=(k == 1))
                last.then_inc(sem("gate_psum"), 1)
                pe.wait_ge(sem("kk_sq"), 1)
                for n in range(2):
                    last = pe.matmul(ps[6 + n][:, :], headones[:, :], t2_[:, n * 512:(n + 1) * 512], start=True, stop=True)
                last.then_inc(sem("kk_psum"), 1)
                pe.wait_ge(sem("wa_out"), 8)

                def turn(w, src, banks, name):
                    for c in range(4):
                        for t in range(NT):
                            last = pe.transpose(ps[banks + t][:, c * P:(c + 1) * P], ch4(src)[:, c, t * P:(t + 1) * P], ident[:, :])
                    last.then_inc(sem("tok_psum"), 1)
                turn(0, ring[:, 4 * CELL + 2048:4 * CELL + 3072], 0, "v")
                p2_ready(pe, GATE0)
                for m in range(4):
                    for t in range(NT):
                        for c in range(KC):
                            last = pe.matmul(ps[2 + m // 2][:, (m % 2) * S + t * P:(m % 2) * S + (t + 1) * P],
                                             p2(GATE0)[:, c, m * P:(m + 1) * P], hT[:, c, t * P:(t + 1) * P],
                                             start=(c == 0), stop=(c == KC - 1))
                    if m % 2:
                        last.then_inc(sem("side_gate"), 1)
                pe.wait_ge(sem("rk_done"), 1)
                pe.wait_ge(sem("kk_root"), 1)
                for n in range(2):
                    last = pe.matmul(ps[6 + n][:, :], headones[:, :], t2_[:, n * 512:(n + 1) * 512], start=True, stop=True)
                last.then_inc(sem("bonus_psum"), 1)
                pe.wait_ge(sem("tilde"), 1)
                pe.wait_ge(sem("side_gate_out"), 2)
                turn(1, kT_, 2, "k")
                pe.wait_ge(sem("tilde"), 2)
                pe.wait_ge(sem("gate_out"), 1)
                turn(2, bT_, 4, "b")
                pe.wait_ge(sem("tilde"), 3)
                pe.wait_ge(sem("tok_out"), 1)
                turn(3, aT_, 0, "a")

            @block.scalar
            def _(act):
                act.activation(tw[0:64, :], mixed[0:64, 12, :], ACT.Tanh).then_inc(sem("tanh"), 1)
                act.activation(sgl, mixed[:, 13:15, :], ACT.Sigmoid).then_inc(sem("sgl"), 1)
                act.wait_ge(sem("w_psum"), 1)
                for c in range(4):
                    act.activation(ch4(ePrev)[:, c, :], ps[c // 2][:, (c % 2) * S:(c % 2 + 1) * S], ACT.Sigmoid,
                                   bias=colB("rwkv_w0_2", c)).then_inc(sem("wa_out"), 1)
                act.wait_ge(sem("a_psum"), 1)
                for c in range(4):
                    act.activation(ch4(aa)[:, c, :], ps[2 + c // 2][:, (c % 2) * S:(c % 2 + 1) * S], ACT.Sigmoid,
                                   bias=colB("rwkv_a0_2", c)).then_inc(sem("wa_out"), 1)
                act.wait_ge(sem("gate_psum"), 1)
                for n in range(2):
                    last = act.activation(gg[:, n * 512:(n + 1) * 512], ps[4 + n][:, :], ACT.Copy)
                last.then_inc(sem("gate_out"), 1)
                act.wait_ge(sem("kk_psum"), 1)
                for n in range(2):
                    last = act.activation(bonus[:, n * 512:(n + 1) * 512], ps[6 + n][:, :], ACT.Sqrt)
                last.then_inc(sem("kk_root"), 1)
                act.wait_ge(sem("tok_psum"), 1)

                def tok(w, banks):
                    act.wait_ge(sem("tok_psum"), w + 1)
                    for t in range(NT):
                        last = act.activation(toks[:, w, t, :], ps[banks + t][:, :], ACT.Copy)
                    last.then_inc(sem("tok_out"), 1)
                tok(0, 0)
                act.wait_ge(sem("logdecay"), 1)
                act.activation(eP, LL, ACT.Exp).then_inc(sem("eP"), 1)
                act.activation(eN, LL, ACT.Exp, scale=-1.0).then_inc(sem("eN"), 1)
                act.wait_ge(sem("logprev"), 1)
                act.activation(ePrev, ePrev, ACT.Exp).then_inc(sem("ePrev"), 1)
                for n in range(2):
                    act.wait_ge(sem("side_gate"), n + 1)
                    act.activation(gates_sb[:, 0, 2 * n:2 * n + 2, :, :], ps[2 + n][:, :].rearrange("p (k t n) -> p k t n", k=2, t=NT),
                                   ACT.Sigmoid).then_inc(sem("side_gate_out"), 1)
                tok(1, 2)
                tok(2, 4)
                tok(3, 0)

            @block.vector
            def _(v):
                v_step(v.tensor_scalar(omka, colB("rwkv_k_a_2", 0, 4), -1.0, 1.0, ALU.mult, ALU.add))
                for c in range(4):
                    ins = v.tensor_scalar(ch4(kk)[:, c, :], k_[:, c, :], colB("rwkv_k_k_2", c), None, ALU.mult)
                v_step(ins)
                v.tensor_tensor(t2_, kk, kk, ALU.mult).then_inc(sem("kk_sq"), 1)
                v.wait_ge(sem("wa_out"), 4)
                v_step(v.tensor_scalar(ePrev, ePrev, -EXPM, None, ALU.mult))
                v.wait_ge(sem("scan_mask"), 1)
                v.tensor_tensor_scan(LL, t1, ePrev, 0.0, ALU.mult, ALU.add).then_inc(sem("logdecay"), 1)
                v.wait_ge(sem("logdecay"), 1)
                v.tensor_tensor(ePrev, LL, ePrev, ALU.subtract).then_inc(sem("logprev"), 1)
                v.wait_ge(sem("wa_out"), 8)
                for c in range(4):
                    ins = v.tensor_scalar(ch4(t1)[:, c, :], ch4(aa)[:, c, :], colB("rwkv_k_a_2", c), omka[:, c:c + 1],
                                          ALU.mult, ALU.add)
                v_step(ins)
                v_step(v.tensor_tensor(k_, k_, ch4(t1), ALU.mult))
                v.wait_ge(sem("kk_root"), 1)
                v_step(v.tensor_scalar(bonus, bonus, 1e-12, None, ALU.max))
                v_step(v.reciprocal(bonus, bonus))
                v_step(v.tensor_tensor(kk, kk, bonus, ALU.mult))
                for c in range(4):
                    ins = v.scalar_tensor_tensor(ch4(t2_)[:, c, :], k_[:, c, :], colB("rwkv_r_k_2", c), r_[:, c, :],
                                                 ALU.mult, ALU.mult)
                ins.then_inc(sem("rk_done"), 1)
                v.wait_ge(sem("eN"), 1)
                v.tensor_tensor(ch4(kT_), k_, ch4(eN), ALU.mult).then_inc(sem("tilde"), 1)
                v_step(v.tensor_tensor(t1, kk, aa, ALU.mult))
                v.tensor_tensor(bT_, t1, eN, ALU.mult).then_inc(sem("tilde"), 1)
                v.wait_ge(sem("ePrev"), 1)
                v.scalar_tensor_tensor(aT_, kk, -1.0, ePrev, ALU.mult, ALU.mult).then_inc(sem("tilde"), 1)
                v.wait_ge(sem("eP"), 1)
                v_step(v.tensor_tensor(ch4(rT_), r_, ch4(eP), ALU.mult))
                v_step(v.tensor_copy(wC, ch4(eP).rearrange("p c (n i) -> p c n i", i=C)[:, :, :, C - 1]))
                v.wait_ge(sem("bonus_psum"), 1)
                for n in range(2):
                    v_step(v.tensor_tensor(bonus[:, n * 512:(n + 1) * 512].rearrange("p (c s) -> p c s", c=2),
                                           ps[6 + n][:, :].rearrange("p (c s) -> p c s", c=2), v_[:, 2 * n:2 * n + 2, :], ALU.mult))

        rbT = ring[:, 4 * CELL:4 * CELL + 2048].rearrange("p (u n) -> p u n", u=16)
        HT = ring[:, 4 * CELL + 2048:4 * CELL + 3072].rearrange("p (u n) -> p u n", u=8)
        Gs = acc[:, 0:1024].rearrange("p (t h d) -> p t h d", t=NT, h=8)
        Yv = acc[:, 1024:2048].rearrange("p (t h d) -> p t h d", t=NT, h=8)
        y_tok = acc[:, 2048:3072].rearrange("p (t h d) -> p t h d", t=NT, h=8)
        MT = side[:, 4096:6144].rearrange("p (q c d) -> p q c d", q=4, c=NC)
        NN = ring[:, c5:c5 + 2048].rearrange("p (q c d) -> p q c d", q=4, c=NC)
        SS = xn_sb[:, :].rearrange("p (q c d) -> p q c d", q=4, c=NC)
        W2 = [acc[:, 4096 + i * 1024:4096 + (i + 1) * 1024] for i in range(2)]
        exp_v = [side[:, 6144 + i * 512:6144 + (i + 1) * 512] for i in range(2)]
        exp_g = [ring[:, c5 + 2048 + i * 256:c5 + 2048 + (i + 1) * 256] for i in range(2)]
        AKT = [ring[:, c5 + 2560 + i * 128:c5 + 2560 + (i + 1) * 128] for i in range(2)]
        RKT = [ring[:, c5 + 2816 + i * 128:c5 + 2816 + (i + 1) * 128] for i in range(2)]

        branch_w = [cell(i, 4, 1024) for i in range(2)]
        QA, QTA, QB, QTB, PTA, PTB, OTM, UH = range(8)

        with nc.Block() as block:
            def mat(b, i, n=1):
                return W2[b][:, i * P:(i + n) * P]

            def inst(u):
                h, t = 2 * (u // 4) + u % 2, u // 2 % NT
                jo = (h % 2) * 64
                return h, t, slice(jo, jo + 64), h // 2, u % 2

            @block.sync
            def _(sp):
                load_gates(sp, 3)
                for i, name in enumerate(("w_branch_attn_2", "w_branch_rwkv_2")):
                    sp.wait_ge(sem("side_gate"), 2 + 8 * (i + 1))
                    sp.dma_start(branch_w[i], inp[name][0].rearrange("(c p) n -> p c n", p=P)).then_inc(
                        sem(f"branch_loaded{i}"), 16)

            GATE_AFTER = (0, 10, 11)

            def gate_bank(i):
                return ps[(3, 3, 7)[i % 3]][:, P:2 * P]

            @block.gpsimd
            def _(pool):
                cm = chunk_of.unsqueeze(2).broadcast_to((P, 4, 64))
                for u in range(16):
                    h, t, js, q, b = inst(u)
                    if u >= 2:
                        pool.wait_ge(sem("i_maps"), u - 1)
                    for i, src in enumerate((b_tk, v_tk)):
                        p_step(pool.tensor_tensor(exp_v[b][:, i * S:(i + 1) * S].rearrange("p (c d) -> p c d", c=4),
                                                  src[:, t, h * 64:(h + 1) * 64].unsqueeze(1).broadcast_to((P, 4, 64)), cm, ALU.mult))
                    pool.memset(small[:, 60:61], 0.0).then_inc(sem("i_spread"), 1)
                    pool.wait_ge(sem("i_spread"), u + 1)

            @block.tensor
            def _(pe):
                def start_(u):
                    if u >= 2:
                        pe.wait_ge(sem("i_end"), u)
                    for i in range(3):
                        for w in (u, u + 1):
                            h, t, js, q, b = inst(w)
                            T = slice(t * P, (t + 1) * P)
                            left = (bT_, kT_, aT_)[i]
                            last = pe.matmul(ps[4 * b + i][:, 0:(S, S, P)[i]], ch4(left)[js, q, T],
                                             tl[js, 0:2, q, T] if i < 2 else ch4(bT_)[js, q, T], start=True, stop=True)
                            if i == 2:
                                last.then_inc(sem("i_prod"), 1)

                def maps(u):
                    pe.wait_ge(sem("i_gh"), u + 2)
                    pe.wait_ge(sem("i_spread"), u + 2)
                    for i in range(3):
                        for w in (u, u + 1):
                            h, t, js, q, b = inst(w)
                            hs = slice(h * 64, (h + 1) * 64)
                            left = (mat(b, UH)[:, 64:P], b_tk[:, t, hs], k_tk[:, t, hs])[i]
                            right = (exp_v[b][:, 0:S], exp_g[b], exp_v[b][:, S:2 * S])[i]
                            last = pe.matmul(ps[4 * b + 2][js, min(i, 1) * S:(min(i, 1) + 1) * S], left, right,
                                             start=(i < 2), stop=(i != 1))
                            if i == 2:
                                last.then_inc(sem("i_maps"), 1)

                def steps(u):
                    h, t, js, q, b = inst(u)
                    B = 4 * b
                    hs = slice(h * 64, (h + 1) * 64)
                    def level(n, Q, QT, last_level):
                        def f():
                            pe.wait_ge(sem(f"i_q{b}"), 4 * (u // 2) + n)
                            if n == 1:
                                pe.wait_ge(sem(f"i_pt{b}"), 5 * (u // 2) + 1)
                            last = pe.matmul(ps[B][:, 0:P], mat(b, QT), mat(b, Q), start=True, stop=True)
                            if not last_level:
                                last = pe.matmul(ps[B][:, P:S], mat(b, Q), mat(b, QT), start=True, stop=True)
                            last.then_inc(sem(f"i_sq{b}"), 1)
                        return f

                    def grow(n, Q, PT):
                        def f():
                            pe.wait_ge(sem(f"i_q{b}"), 4 * (u // 2) + n)
                            pe.wait_ge(sem(f"i_pt{b}"), 5 * (u // 2) + n - 1)
                            pe.matmul(ps[B + 1][:, 0:P], mat(b, Q), mat(b, PT), start=True, stop=True).then_inc(sem(f"i_gr{b}"), 1)
                        return f

                    def off1():
                        pe.wait_ge(sem(f"i_pt{b}"), 5 * (u // 2) + 4)
                        pe.transpose(ps[B + 2][:, 0:P], mat(b, PTB), ident[:, :]).then_inc(sem(f"i_pd{b}"), 1)

                    def off2():
                        pe.wait_ge(sem(f"i_off{b}"), 2 * (u // 2) + 1)
                        pe.matmul(ps[B + 2][:, P:S], mat(b, OTM), mat(b, QA), start=True, stop=True).then_inc(sem(f"i_xt{b}"), 1)
                        pe.wait_ge(sem("side_gate_out"), 2 + 3 * (u // 2) + (1, 0)[b])
                        pe.matmul(ps[B + 3][:, 0:64], AKT[b], v_tk[:, t, hs], start=True, stop=True)
                        pe.matmul(ps[B + 3][:, 64:128], RKT[b], v_tk[:, t, hs], start=True, stop=True).then_inc(sem(f"i_u{b}"), 1)

                    def off3():
                        pe.wait_ge(sem(f"i_off{b}"), 2 * (u // 2) + 2)
                        pe.matmul(ps[B + 1][:, 0:P], mat(b, QB), mat(b, PTB), start=True, stop=True).then_inc(sem(f"i_gr{b}"), 1)

                    def solve():
                        pe.wait_ge(sem(f"i_pt{b}"), 5 * (u // 2) + 5)
                        pe.wait_ge(sem(f"i_ud{b}"), u // 2 + 1)
                        pe.matmul(ps[B][:, 0:64], mat(b, PTA), mat(b, UH)[:, 0:64], start=True, stop=True)
                        pe.matmul(ps[B][:, 64:P], mat(b, PTA), a_tk[:, t, hs], start=True, stop=True)
                        pe.matmul(ps[B + 1][js, 0:P], a_tk[:, t, hs], mat(b, PTA), start=True, stop=True).then_inc(sem("i_sol"), 1)

                    return [lambda: None if u % 2 else start_(u), level(1, QA, QTA, False), level(2, QB, QTB, False),
                            grow(2, QB, PTA), level(3, QA, QTA, True), grow(3, QA, PTB), grow(4, QB, PTA), off1, off2, off3,
                            solve, lambda: maps(u - 1) if u % 2 else None]
                def gate_product(i):
                    m, t = 4 + i // NT, i % NT
                    if i % 8 == 0:
                        p2_ready(pe, GATE0 + m // 4)
                    if i % 3 == 0 and i:
                        pe.wait_ge(sem("side_gate_out"), 2 + i - 1)
                    if i % 3 == 2:
                        pe.wait_ge(sem("i_ud1"), i // 3 + 1)
                    for c in range(KC):
                        last = pe.matmul(gate_bank(i), p2(GATE0 + m // 4)[:, c, (m % 4) * P:(m % 4 + 1) * P],
                                         hT[:, c, t * P:(t + 1) * P], start=(c == 0), stop=(c == KC - 1))
                    last.then_inc(sem("side_gate"), 1)

                for pair in range(8):
                    for k, (fa, fb) in enumerate(zip(steps(2 * pair), steps(2 * pair + 1))):
                        fa()
                        fb()
                        if k in GATE_AFTER:
                            gate_product(3 * pair + GATE_AFTER.index(k))

            @block.scalar
            def _(act):
                def steps(u):
                    h, t, js, q, b = inst(u)
                    B = 4 * b

                    def sq(n, dst):
                        def f():
                            act.wait_ge(sem(f"i_sq{b}"), 3 * (u // 2) + n)
                            k = 2 if n < 3 else 1
                            act.activation(mat(b, dst, k), ps[B][:, 0:k * P], ACT.Copy).then_inc(sem(f"i_q{b}"), 1)
                        return f

                    def uh():
                        act.wait_ge(sem(f"i_u{b}"), u // 2 + 1)
                        act.activation(mat(b, UH)[:, 0:64], ps[B + 3][:, 0:64], ACT.Copy)
                        act.activation(Yv[:, t, h, :], ps[B + 3][:, 64:P], ACT.Copy).then_inc(sem(f"i_ud{b}"), 1)

                    def sol():
                        act.wait_ge(sem("i_sol"), u + 1)
                        act.activation(HT[js, 2 * q + t, :], ps[B + 1][js, 0:P], ACT.Copy)

                    def nmap():
                        act.wait_ge(sem("i_maps"), u + 1)
                        act.wait_ge(sem("i_mdone"), u + 1)
                        act.activation(NN[js, q, 4 * t:4 * t + 4, :], ps[B + 2][js, S:2 * S].rearrange("p (c d) -> p c d", c=4),
                                       ACT.Copy).then_inc(sem("i_end"), 1)
                    return [sq(1, QB), sq(2, QA), sq(3, QB), uh, sol, nmap]

                for c in range(4):
                    act.activation(ch4(bonus)[:, c, :], ch4(bonus)[:, c, :], ACT.Identity, bias=colB("rwkv_ln_b_2", c))

                def gate_sigmoid(i):
                    m, t = 4 + i // NT, i % NT
                    act.wait_ge(sem("side_gate"), 2 + i + 1)
                    act.activation(gates_sb[:, m // 4, m % 4, t, :], gate_bank(i), ACT.Sigmoid).then_inc(sem("side_gate_out"), 1)

                for pair in range(8):
                    for k, (fa, fb) in enumerate(zip(steps(2 * pair), steps(2 * pair + 1))):
                        if k in (0, 5):
                            gate_sigmoid(3 * pair + k // 5)
                        fa()
                        fb()
                    gate_sigmoid(3 * pair + 2)

            @block.vector
            def _(v):
                v_step(v.memset(SS[:, :, 0, :], 0.0))

                def steps(u):
                    h, t, js, q, b = inst(u)
                    B = 4 * b

                    def first():
                        v.wait_ge(sem("i_prod"), u + 1)
                        v.tensor_tensor(mat(b, QTA), ps[B][:, P:S], M_16, ALU.mult)
                        v_step(v.tensor_tensor(mat(b, QA), ps[B + 2][:, 0:P], M_16L, ALU.mult))
                        v.tensor_tensor(mat(b, PTA), mat(b, QTA), ident[:, :], ALU.add).then_inc(sem(f"i_q{b}"), 1)
                        v.wait_ge(sem(f"i_q{b}"), 4 * (u // 2) + 1)
                        v.tensor_tensor(rbT[:, 2 * h + t, :], ps[B][:, 0:P], M_INCL, ALU.mult)
                        v.tensor_tensor(mat(b, OTM), ps[B][:, P:S], M_OFF, ALU.mult)
                        v.tensor_tensor(RKT[b], ps[B + 1][:, 0:P], M_INCL, ALU.mult)
                        v.tensor_tensor(AKT[b], ps[B + 1][:, P:S], M_STRICT, ALU.mult).then_inc(sem(f"i_pt{b}"), 1)

                    def grown(n, src, dst):
                        def f():
                            v.wait_ge(sem(f"i_gr{b}"), 4 * (u // 2) + n)
                            v.tensor_tensor(mat(b, dst), ps[B + 1][:, 0:P], mat(b, src), ALU.add).then_inc(sem(f"i_pt{b}"), 1)
                            v.wait_ge(sem(f"i_pt{b}"), 5 * (u // 2) + n + 1)
                        return f

                    def pd():
                        v.wait_ge(sem(f"i_pd{b}"), u // 2 + 1)
                        v.tensor_copy(mat(b, QA), ps[B + 2][:, 0:P]).then_inc(sem(f"i_off{b}"), 1)

                    def xt():
                        v.wait_ge(sem(f"i_xt{b}"), u // 2 + 1)
                        v.tensor_copy(mat(b, QB), ps[B + 2][:, P:S]).then_inc(sem(f"i_off{b}"), 1)

                    def sol():
                        v.wait_ge(sem("i_sol"), u + 1)
                        v_step(v.tensor_copy(Gs[:, t, h, :], ps[B][:, 0:64]))
                        v.tensor_copy(mat(b, UH)[:, 64:P], ps[B][:, 64:P])
                        v.tensor_tensor(exp_g[b].rearrange("p (c d) -> p c d", c=4),
                                        Gs[:, t, h, :].unsqueeze(1).broadcast_to((P, 4, 64)),
                                        chunk_of.unsqueeze(2).broadcast_to((P, 4, 64)), ALU.mult).then_inc(sem("i_gh"), 1)

                    def maps():
                        v.wait_ge(sem("i_maps"), u + 1)
                        v.tensor_tensor(MT[js, q, 4 * t:4 * t + 4, :], ps[B + 2][js, 0:S].rearrange("p (c d) -> p c d", c=4),
                                        ident[js, js].unsqueeze(1).broadcast_to((64, 4, 64)), ALU.add).then_inc(sem("i_mdone"), 1)
                    return [first, grown(1, PTA, PTB), grown(2, PTB, PTA), grown(3, PTA, PTB), pd, xt, grown(4, PTB, PTA), sol, maps]
                for pair in range(8):
                    for fa, fb in zip(steps(2 * pair), steps(2 * pair + 1)):
                        fa()
                        fb()

        sa_sb = [acc[:, 4096 + t * 512:4096 + (t + 1) * 512].rearrange("p (h d) -> p h d", h=8) for t in range(NT)]
        sq7 = acc[:, 5120:6144]
        st7 = small[:, 24:40]
        y_flat = acc[:, 2048:3072].rearrange("p (t d) -> p t d", t=NT)
        orT = ch4(side[:, 0:1024])
        out_w = [cell(2), cell(4)]

        with nc.Block() as block:
            @block.sync
            def _(sp):
                sp.dma_start(out_w[0], w_cols(inp["w_out_2"][0], 0, 512)).then_inc(sem("out_loaded0"), 16)

            @block.tensor
            def _(pe):
                def attn_branch(m):
                    if m == 0:
                        pe.wait_ge(sem("branch_loaded0"), 16)
                    if m >= 2:
                        pe.wait_ge(sem("gated"), m - 1)
                    for c in range(4):
                        last = pe.matmul(ps[5 + m % 2][:, 0:S], branch_w[0][:, c, m * P:(m + 1) * P], oaT[:, c, :],
                                         start=(c == 0), stop=(c == 3))
                    last.then_inc(sem("attn_branch"), 1)

                for c in range(NC - 1):
                    if c:
                        attn_branch(c - 1)
                        pe.wait_ge(sem("state"), 2 * c)
                    for q in range(4):
                        for par in range(2):
                            js = slice(par * 64, par * 64 + 64)
                            last = pe.matmul(ps[par][js, q * 64:(q + 1) * 64], MT[js, q, c, :], SS[js, q, c, :], start=True, stop=True)
                            if q == 3:
                                last.then_inc(sem("state_psum"), 1)
                attn_branch(NC - 2)
                attn_branch(NC - 1)
                pe.wait_ge(sem("state"), 2 * (NC - 1))
                for t in range(NT):
                    if t:
                        pe.wait_ge(sem("sa_done"), 2)
                        pe.wait_ge(sem("y_out"), 1)
                    for par in range(2):
                        js = slice(par * 64, par * 64 + 64)
                        for q in range(4):
                            for c in range(4):
                                last = pe.matmul(ps[par][c * C:(c + 1) * C, q * 64:(q + 1) * 64], HT[js, 2 * q + t, c * C:(c + 1) * C],
                                                 SS[js, q, 4 * t + c, :], start=True, stop=True)
                    last.then_inc(sem("sa_psum"), 1)
                    for par in range(2):
                        js = slice(par * 64, par * 64 + 64)
                        for q in range(4):
                            for c in range(4):
                                o = t * P + c * C
                                last = pe.matmul(ps[2 + par][c * C:(c + 1) * C, q * 64:(q + 1) * 64], ch4(rT_)[js, q, o:o + C],
                                                 SS[js, q, 4 * t + c, :], start=True, stop=True)
                    pe.wait_ge(sem("sa_done"), 2 * t + 2)
                    for h in range(8):
                        last = pe.matmul(ps[4][:, h * 64:(h + 1) * 64], rbT[:, 2 * h + t, :], sa_sb[t][:, h, :], start=True, stop=True)
                    last.then_inc(sem("y_psum"), 1)
                pe.wait_ge(sem("gated"), 8)
                for t in range(NT):
                    pe.wait_ge(sem("y_normed"), t + 1)
                    for c in range(4):
                        last = pe.transpose(ps[6 + c // 2][:, (c % 2) * S + t * P:(c % 2) * S + (t + 1) * P],
                                            y_flat[:, t, c * P:(c + 1) * P], ident[:, :])
                last.then_inc(sem("yT_psum"), 1)

            @block.scalar
            def _(act):
                load_sqrt(act, 3)
                for t in range(NT):
                    act.wait_ge(sem("y_centred"), t + 1)
                    act.activation(sq7[:, t * 512:(t + 1) * 512], y_flat[:, t, :], ACT.Square).then_inc(sem("y_sq"), 1)
                    act.wait_ge(sem("y_var"), t + 1)
                    act.activation(st7[:, 8 * t:8 * t + 8], st7[:, 8 * t:8 * t + 8], ACT.Sqrt).then_inc(sem("y_root"), 1)

            @block.vector
            def _(v):
                def gate_attn(m):
                    v.wait_ge(sem("attn_branch"), m + 1)
                    g = gates_sb[:, m // 4, m % 4, :, :]
                    v.tensor_tensor(g, ps[5 + m % 2][:, 0:S].rearrange("p (t n) -> p t n", t=NT), g, ALU.mult).then_inc(
                        sem("gated"), 1)

                for c in range(NC - 1):
                    for par in range(2):
                        js = slice(par * 64, par * 64 + 64)
                        v.wait_ge(sem("state_psum"), 2 * c + par + 1)
                        s_ = SS[js, :, c + 1, :]
                        v_step(v.tensor_tensor(s_, ps[par][js, 0:S].rearrange("p (q d) -> p q d", q=4), NN[js, :, c, :], ALU.add))
                        v.tensor_tensor(s_, s_, wC[js, :, c].unsqueeze(2).broadcast_to((64, 4, 64)), ALU.mult).then_inc(sem("state"), 1)
                    if c:
                        gate_attn(c - 1)
                gate_attn(NC - 2)
                gate_attn(NC - 1)

                def removals(t):
                    v.wait_ge(sem("sa_psum"), t + 1)
                    gq = Gs[:, t, :, :].rearrange("p (q r) d -> p r q d", r=2)
                    sq_ = sa_sb[t].rearrange("p (q r) d -> p r q d", r=2)
                    for par in range(2):
                        v.tensor_tensor(sq_[:, par, :, :], ps[par][:, 0:S].rearrange("p (q d) -> p q d", q=4), gq[:, par, :, :],
                                        ALU.add).then_inc(sem("sa_done"), 1)

                def outputs(t):
                    v.wait_ge(sem("y_psum"), t + 1)
                    v_step(v.tensor_tensor(y_tok[:, t, :, :], ps[4][:, :].rearrange("p (h d) -> p h d", h=8), Yv[:, t, :, :], ALU.add))
                    yq = y_tok[:, t, :, :].rearrange("p (q r) d -> p r q d", r=2)
                    for par in range(2):
                        ins = v.tensor_tensor(yq[:, par, :, :], ps[2 + par][:, 0:S].rearrange("p (q d) -> p q d", q=4),
                                              yq[:, par, :, :], ALU.add)
                    ins.then_inc(sem("y_out"), 1)

                def centre(t):
                    v.wait_ge(sem("y_out"), t + 1)
                    m = st7[:, 8 * t:8 * t + 8]
                    v_step(v.tensor_reduce(m, y_tok[:, t, :, :], X, ALU.add))
                    v_step(v.tensor_scalar(m, m, -1.0 / 64, None, ALU.mult))
                    v.tensor_tensor(y_tok[:, t, :, :], y_tok[:, t, :, :], m.unsqueeze(2).broadcast_to((P, 8, 64)),
                                    ALU.add).then_inc(sem("y_centred"), 1)

                def divide(t):
                    m = st7[:, 8 * t:8 * t + 8]
                    v.wait_ge(sem("y_sq"), t + 1)
                    v_step(v.tensor_reduce(m, sq7[:, t * 512:(t + 1) * 512].rearrange("p (g d) -> p g d", d=64), X, ALU.add))
                    v.tensor_scalar(m, m, 1.0 / 64, 64e-5, ALU.mult, ALU.add).then_inc(sem("y_var"), 1)
                    v.wait_ge(sem("y_root"), t + 1)
                    v_step(v.reciprocal(m, m))
                    v.tensor_tensor(y_tok[:, t, :, :], y_tok[:, t, :, :], m.unsqueeze(2).broadcast_to((P, 8, 64)),
                                    ALU.mult).then_inc(sem("y_normed"), 1)
                removals(0)
                outputs(0)
                centre(0)
                removals(1)
                divide(0)
                outputs(1)
                centre(1)
                divide(1)
                v.wait_ge(sem("yT_psum"), 1)
                for c in range(4):
                    ins = v.scalar_tensor_tensor(orT[:, c, :], ps[6 + c // 2][:, (c % 2) * S:(c % 2 + 1) * S],
                                                 colB("rwkv_ln_w_2", c), ch4(bonus)[:, c, :], ALU.mult, ALU.add)
                v_step(ins)
                v_step(v.tensor_tensor(side[:, 0:1024], side[:, 0:1024], gg, ALU.mult))

        give_back()
        mrg = acc[:, 2048:4096].rearrange("p (c s) -> p c s", c=8)
        mrg_half = acc[:, 0:2048].rearrange("p (c s) -> p c s", c=8)

        with nc.Block() as block:
            @block.sync
            def _(sp):
                sp.dma_start(out_w[1], w_cols(inp["w_out_2"][0], 512, 1024)).then_inc(sem("out_loaded1"), 16)
                load_router(sp, 1, inp["router_group_w_2"][0], inp["router_expert_w_2"][0], None, inp["router_expert_bias_2"])
                load_expert(sp, 1, (5,))
                sp.wait_ge(sem("branch_out"), 8)
                load_expert(sp, 1, (0, 3, 1))
                sp.wait_ge(sem("y3"), 4)
                load_expert(sp, 1, (4, 2))

            @block.tensor
            def _(pe):
                pe.wait_ge(sem("branch_loaded1"), 16)
                for m in range(8):
                    if m >= 4:
                        pe.wait_ge(sem("branch_out"), m - 3)
                    for c in range(4):
                        last = pe.matmul(ps[4 + m % 4][:, 0:S], branch_w[1][:, c, m * P:(m + 1) * P],
                                         orT[:, c, :], start=(c == 0), stop=(c == 3))
                    last.then_inc(sem("branch"), 1)
                pe.wait_ge(sem("branch_out"), 8)
                for g in range(4):
                    t, n = g // 2, g % 2
                    if t == 0:
                        pe.wait_ge(sem(f"out_loaded{n}"), 16)
                    for c in range(KC):
                        last = pe.matmul(ps[g][:, :], mrg[:, c, t * P:(t + 1) * P], out_w[n][:, c, :],
                                         start=(c == 0), stop=(c == KC - 1))
                    last.then_inc(sem("y3"), 1)
                hT_tensor(pe, 3)
                router_tensor(pe, 1, 32)

            @block.scalar
            def _(act):
                load_sqrt(act, 2)
                rms_scalar(act, 4, xn_sb, ("y3_x", 2, 4))
                hT_scalar(act, 3)

            @block.vector
            def _(v):
                for m in range(8):
                    v.wait_ge(sem("branch"), m + 1)
                    y, h_, g_ = [a.rearrange("p (t n) -> p t n", t=NT) for a in
                                 (ps[4 + m % 4][:, 0:S], mrg_half[:, m, :], mrg[:, m, :])]
                    v_step(v.tensor_tensor(h_, y, gates_sb[:, 2 + m // 4, m % 4, :, :], ALU.mult))
                    v.tensor_tensor(g_, h_, gates_sb[:, m // 4, m % 4, :, :], ALU.add).then_inc(sem("branch_out"), 1)
                for g in range(4):
                    residual(v, g, 0, "y3")
                rms_vector(v, 4, xn3)
                hT_vector(v, 3)

        route(1, 32, False)

        def store(sp):
            for t in range(NT):
                sp.wait_ge(sem("x_new1"), 2 * t + 2)
                sp.dma_start(out[0, t * P:(t + 1) * P, :], x3[:, t, :]).then_inc(sem("stored"), 16)
            sp.wait_ge(sem("stored"), 16 * NT)

        experts(1, 32, afterwards=store)


OUT_SHAPE = (1, S, D)


def kernel(**inputs):
    import concourse.bacc as bacc
    from concourse.bass_utils import run_bass_kernel_spmd

    nc = bacc.Bacc("TRN2", target_bir_lowering=False, num_devices=1)
    arrays, inp = {}, {}
    for name, value in inputs.items():
        a = np.ascontiguousarray(value)
        if a.size == 0:
            continue
        arrays["in_" + name] = a
        inp[name] = nc.dram_tensor("in_" + name, a.shape, mybir.dt.from_np(a.dtype), kind="ExternalInput").ap()
    out = nc.dram_tensor("out_x", OUT_SHAPE, F32, kind="ExternalOutput").ap()
    build(nc, inp, out)
    r = run_bass_kernel_spmd(nc, [arrays], core_ids=[0])
    return r.results[0]["out_x"]
```
